# Optimizing a Trainium2 kernel written in Bass

```python
import math
import jax, jax.numpy as jnp
from jax import lax
import numpy as np

D_MODEL = 1024
BATCH = 1
SEQ = 512
DEPTH = 1

MEM_TOKENS = 256
EPS = 1e-6
MLA_HEADS = 8
MLA_NOPE = 64
MLA_ROPE = 32
MLA_V = 64
MLA_Q_RANK = 256
MLA_KV_RANK = 128
ROPE_BASE = 10000.0
Q_BLOCK = 128
HY_WIDTH = D_MODEL - MLA_HEADS * MLA_V
HY_ORDER = 2
HY_DIRS = 2
HY_BANDS = 16
HY_EMB = 1 + 2 * HY_BANDS
HY_FFN = 64
HY_TARGET = 1e-2
HY_FAST_PCT = 0.3
HY_SLOW_PCT = 1.5
OFF_Q = 0
OFF_KV = OFF_Q + MLA_Q_RANK
OFF_KR = OFF_KV + MLA_KV_RANK
OFF_HY = OFF_KR + MLA_ROPE
IN_COLS = OFF_HY + 3 * HY_WIDTH
MEM_HEADS = 4
MEM_HEAD_DIM = D_MODEL // MEM_HEADS
N_GROUPS = 4
EXPERTS_PER_GROUP = 8
TOP_K_IN_GROUP = 2
D_EXPERT = 256


def _rms(x, g):
    xf = x.astype(jnp.float32)
    y = xf * lax.rsqrt(jnp.mean(xf * xf, axis=-1, keepdims=True) + EPS)
    return (y * g.astype(jnp.float32)).astype(x.dtype)

def _rope(x, cos, sin):
    x1, x2 = jnp.split(x.astype(jnp.float32), 2, axis=-1)
    return jnp.concatenate([x1 * cos - x2 * sin, x1 * sin + x2 * cos], axis=-1).astype(x.dtype)

def _mla(h_q, h_kv, h_kr, q_norm_g, kv_norm_g, w_uq, w_ukv):
    B, S, _ = h_q.shape
    q = (_rms(h_q, q_norm_g) @ w_uq).reshape(B, S, MLA_HEADS, MLA_NOPE + MLA_ROPE)
    q_nope, q_rot = q[..., :MLA_NOPE], q[..., MLA_NOPE:]
    kv = (_rms(h_kv, kv_norm_g) @ w_ukv).reshape(B, S, MLA_HEADS, MLA_NOPE + MLA_V)
    k_nope, v = kv[..., :MLA_NOPE], kv[..., MLA_NOPE:]
    pos = jnp.arange(S, dtype=jnp.float32)
    half = MLA_ROPE // 2
    inv = ROPE_BASE ** (-jnp.arange(half, dtype=jnp.float32) / half)
    ang = pos[:, None] * inv[None, :]
    cos, sin = jnp.cos(ang), jnp.sin(ang)
    q_rot = _rope(q_rot, cos[:, None, :], sin[:, None, :])
    k_rot = _rope(h_kr, cos, sin)
    scale = (MLA_NOPE + MLA_ROPE) ** -0.5
    nb = S // Q_BLOCK

    def to_blocks(t):
        return jnp.moveaxis(t.reshape(B, nb, Q_BLOCK, *t.shape[2:]), 1, 0)

    def attend(blk):
        qn, qr = blk
        s = (jnp.einsum('bqhd,bkhd->bhqk', qn, k_nope)
             + jnp.einsum('bqhr,bkr->bhqk', qr, k_rot)).astype(jnp.float32) * scale
        p = jax.nn.softmax(s, axis=-1).astype(v.dtype)
        return jnp.einsum('bhqk,bkhd->bqhd', p, v)

    o = lax.map(attend, (to_blocks(q_nope), to_blocks(q_rot)))
    return jnp.moveaxis(o, 0, 1).reshape(B, S, MLA_HEADS * MLA_V)

def _hyena_filters(L, w1, b1, freq, w2, b2, w3, b3, decay):
    f32 = jnp.float32
    t = jnp.arange(L, dtype=f32)
    t01 = t / L
    bands = jnp.linspace(1e-4, HY_BANDS - 1, HY_BANDS, dtype=f32)
    ang = 2.0 * math.pi * t[:, None] * bands[None, :] / L
    z = jnp.concatenate([t01[:, None], jnp.cos(ang), -jnp.sin(ang)], axis=-1)
    fr = freq.astype(f32)
    h = jnp.sin(fr[0] * (z @ w1.astype(f32) + b1.astype(f32)))
    h = jnp.sin(fr[1] * (h @ w2.astype(f32) + b2.astype(f32)))
    h = h @ w3.astype(f32) + b3.astype(f32)
    h = h * jnp.exp(-t01[:, None] * jnp.abs(decay.astype(f32))[None, :])
    h = h.reshape(L, HY_ORDER, HY_DIRS, HY_WIDTH)
    fwd, bwd = h[:, :, 0], h[:, :, 1]
    k = jnp.concatenate([fwd, jnp.zeros((1, HY_ORDER, HY_WIDTH), f32), bwd[:0:-1]], axis=0)
    return jnp.fft.rfft(k, axis=0)

def _hyena(u, conv_w, conv_b, kf, skip):
    B, S, _ = u.shape
    up = jnp.pad(u, ((0, 0), (1, 1), (0, 0)))
    u = up[:, :-2] * conv_w[0] + up[:, 1:-1] * conv_w[1] + up[:, 2:] * conv_w[2] + conv_b
    x1, x2, v = jnp.split(u, 3, axis=-1)
    gates = (x1, x2)
    z = v.astype(jnp.float32)
    for n in range(HY_ORDER):
        zf = jnp.fft.rfft(z, n=2 * S, axis=1)
        conv = jnp.fft.irfft(zf * kf[None, :, n], n=2 * S, axis=1)[:, :S]
        z = gates[n].astype(jnp.float32) * (conv + skip[n].astype(jnp.float32) * z)
    return z.astype(u.dtype)

def _mem_xattn(hx, hm, w_mq, w_mkv, w_mo):
    B, S, _ = hx.shape
    M = hm.shape[1]
    q = (hx @ w_mq).reshape(B, S, MEM_HEADS, MEM_HEAD_DIM)
    k, v = jnp.split(hm @ w_mkv, 2, axis=-1)
    k = k.reshape(B, M, MEM_HEADS, MEM_HEAD_DIM)
    v = v.reshape(B, M, MEM_HEADS, MEM_HEAD_DIM)
    s = jnp.einsum('bshd,bmhd->bhsm', q, k).astype(jnp.float32) * MEM_HEAD_DIM ** -0.5
    p = jax.nn.softmax(s, axis=-1).astype(v.dtype)
    o = jnp.einsum('bhsm,bmhd->bshd', p, v).reshape(B, S, MEM_HEADS * MEM_HEAD_DIM)
    return o @ w_mo

def _hier_moe(h, w_rg, b_rg, w_re, b_re, w_gate, w_up, w_down):
    B, S, D = h.shape
    t = h.reshape(B * S, D)
    g_logits = (t @ w_rg).astype(jnp.float32) + b_rg.astype(jnp.float32)
    g_prob = jax.nn.softmax(g_logits, axis=-1)
    _, g_idx = lax.top_k(g_logits, 1)
    p_group = jnp.take_along_axis(g_prob, g_idx, axis=1)
    e_logits = ((t @ w_re).astype(jnp.float32) + b_re.astype(jnp.float32)).reshape(-1, N_GROUPS, EXPERTS_PER_GROUP)
    e_in = jnp.take_along_axis(e_logits, g_idx[:, :, None], axis=1)[:, 0]
    top_v, top_i = lax.top_k(e_in, TOP_K_IN_GROUP)
    p_exp = jax.nn.softmax(top_v, axis=-1)
    w_e = jnp.sum(jax.nn.one_hot(top_i, EXPERTS_PER_GROUP, dtype=jnp.float32) * p_exp[..., None], axis=1)
    combine = ((p_group * w_e)[:, None, :]
               * jax.nn.one_hot(g_idx[:, 0], N_GROUPS, dtype=jnp.float32)[:, :, None]).astype(t.dtype)
    y = jnp.zeros_like(t)
    for g in range(N_GROUPS):
        a = jnp.einsum('td,edf->tef', t, w_gate[g])
        b = jnp.einsum('td,edf->tef', t, w_up[g])
        m = jax.nn.silu(a) * b * combine[:, g, :, None]
        y = y + jnp.einsum('tef,efd->td', m, w_down[g])
    return y.reshape(B, S, D)

def first_inputs(seed: int = 0) -> dict:
    key = jax.random.key(seed)
    ks = iter(jax.random.split(key, 40))
    f32 = jnp.float32
    L_ = DEPTH

    def nrm(shape, fan_in, scale=1.0):
        return jax.random.normal(next(ks), shape, f32) * (scale * fan_in ** -0.5)

    def gain(shape):
        return 1.0 + 0.02 * jax.random.normal(next(ks), shape, f32)

    def small(shape, s=0.02):
        return s * jax.random.normal(next(ks), shape, f32)

    G, E, F = N_GROUPS, EXPERTS_PER_GROUP, D_EXPERT
    d_min = math.log(1.0 / HY_TARGET) / HY_SLOW_PCT
    d_max = math.log(1.0 / HY_TARGET) / HY_FAST_PCT
    return {
        "x": jax.random.normal(next(ks), (BATCH, SEQ, D_MODEL), f32),
        "mem": jax.random.normal(next(ks), (BATCH, MEM_TOKENS, D_MODEL), f32),
        "mix_norm_g": gain((L_, D_MODEL)),
        "w_in": nrm((L_, D_MODEL, IN_COLS), D_MODEL),
        "q_norm_g": gain((L_, MLA_Q_RANK)),
        "kv_norm_g": gain((L_, MLA_KV_RANK)),
        "w_uq": nrm((L_, MLA_Q_RANK, MLA_HEADS * (MLA_NOPE + MLA_ROPE)), MLA_Q_RANK),
        "w_ukv": nrm((L_, MLA_KV_RANK, MLA_HEADS * (MLA_NOPE + MLA_V)), MLA_KV_RANK),
        "hy_conv_w": nrm((L_, 3, 3 * HY_WIDTH), 3),
        "hy_conv_b": small((L_, 3 * HY_WIDTH)),
        "hy_w1": nrm((L_, HY_EMB, HY_FFN), HY_EMB),
        "hy_b1": small((L_, HY_FFN), 0.1),
        "hy_freq": gain((L_, 2, HY_FFN)),
        "hy_w2": nrm((L_, HY_FFN, HY_FFN), HY_FFN),
        "hy_b2": small((L_, HY_FFN), 0.1),
        "hy_w3": nrm((L_, HY_FFN, HY_ORDER * HY_DIRS * HY_WIDTH), HY_FFN, 0.1),
        "hy_b3": small((L_, HY_ORDER * HY_DIRS * HY_WIDTH), 0.01),
        "hy_decay": jax.random.uniform(next(ks), (L_, HY_ORDER * HY_DIRS * HY_WIDTH), f32, d_min, d_max),
        "hy_skip": jax.random.normal(next(ks), (L_, HY_ORDER, HY_WIDTH), f32),
        "attn_out_g": gain((L_, MLA_HEADS * MLA_V)),
        "hy_out_g": gain((L_, HY_WIDTH)),
        "w_out": nrm((L_, D_MODEL, D_MODEL), D_MODEL),
        "cross_norm_g": gain((L_, D_MODEL)),
        "mem_norm_g": gain((L_, D_MODEL)),
        "w_mq": nrm((L_, D_MODEL, MEM_HEADS * MEM_HEAD_DIM), D_MODEL),
        "w_mkv": nrm((L_, D_MODEL, 2 * MEM_HEADS * MEM_HEAD_DIM), D_MODEL),
        "w_mo": nrm((L_, MEM_HEADS * MEM_HEAD_DIM, D_MODEL), MEM_HEADS * MEM_HEAD_DIM),
        "ffn_norm_g": gain((L_, D_MODEL)),
        "w_route_group": nrm((L_, D_MODEL, G), D_MODEL),
        "b_route_group": small((L_, G), 0.01),
        "w_route_expert": nrm((L_, D_MODEL, G * E), D_MODEL),
        "b_route_expert": small((L_, G * E), 0.01),
        "w_gate": nrm((L_, G, E, D_MODEL, F), D_MODEL),
        "w_up": nrm((L_, G, E, D_MODEL, F), D_MODEL),
        "w_down": nrm((L_, G, E, F, D_MODEL), F),
        "final_norm_g": gain((D_MODEL,)),
    }

def first_block(x, mem, mix_norm_g, w_in, q_norm_g, kv_norm_g, w_uq, w_ukv, hy_conv_w, hy_conv_b,
              hy_w1, hy_b1, hy_freq, hy_w2, hy_b2, hy_w3, hy_b3, hy_decay, hy_skip, attn_out_g, hy_out_g,
              w_out, cross_norm_g, mem_norm_g, w_mq, w_mkv, w_mo, ffn_norm_g, w_route_group, b_route_group,
              w_route_expert, b_route_expert, w_gate, w_up, w_down, final_norm_g):
    S = x.shape[1]
    for l in range(DEPTH):
        h = _rms(x, mix_norm_g[l])
        p = h @ w_in[l]
        a_out = _mla(p[..., OFF_Q:OFF_KV], p[..., OFF_KV:OFF_KR], p[..., OFF_KR:OFF_HY],
                     q_norm_g[l], kv_norm_g[l], w_uq[l], w_ukv[l])
        kf = _hyena_filters(S, hy_w1[l], hy_b1[l], hy_freq[l], hy_w2[l], hy_b2[l], hy_w3[l], hy_b3[l], hy_decay[l])
        h_out = _hyena(p[..., OFF_HY:], hy_conv_w[l], hy_conv_b[l], kf, hy_skip[l])
        mixed = jnp.concatenate([_rms(a_out, attn_out_g[l]), _rms(h_out, hy_out_g[l])], axis=-1)
        x = x + mixed @ w_out[l]
        x = x + _mem_xattn(_rms(x, cross_norm_g[l]), _rms(mem, mem_norm_g[l]), w_mq[l], w_mkv[l], w_mo[l])
        x = x + _hier_moe(_rms(x, ffn_norm_g[l]), w_route_group[l], b_route_group[l], w_route_expert[l],
                          b_route_expert[l], w_gate[l], w_up[l], w_down[l])
    return _rms(x, final_norm_g)


DEPTH_2 = 2

GRID_W = 64
CTX_LEN = 256
N_MIXERS = 2
NORM_EPS = 1e-6
N_HEADS = 16
N_KV_HEADS = 4
HEAD_DIM = D_MODEL // N_HEADS
KV_GROUP = N_HEADS // N_KV_HEADS
ROPE_THETA = 10000.0
ROPE_PAIRS = HEAD_DIM // 4
RWKV_HEAD = 64
RWKV_HEADS = D_MODEL // RWKV_HEAD
DECAY_LORA = 64
ICLR_LORA = 64
GATE_LORA = 128
GN_EPS = 64e-5
D_FF = -(-8 * D_MODEL // (3 * 256)) * 256


def _rmsnorm(x, g):
    xf = x.astype(jnp.float32)
    y = xf * lax.rsqrt(jnp.mean(xf * xf, axis=-1, keepdims=True) + NORM_EPS)
    return (y * g.astype(jnp.float32)).astype(x.dtype)

def _axial_rope_tables(rows, dtype):
    L = rows * GRID_W
    row = jnp.repeat(jnp.arange(rows, dtype=jnp.float32), GRID_W, total_repeat_length=L)
    col = jnp.tile(jnp.arange(GRID_W, dtype=jnp.float32), rows)
    inv_freq = ROPE_THETA ** (-jnp.arange(ROPE_PAIRS, dtype=jnp.float32) / ROPE_PAIRS)
    ang = jnp.stack([row[:, None] * inv_freq, col[:, None] * inv_freq], axis=1)
    return jnp.cos(ang).astype(dtype), jnp.sin(ang).astype(dtype)

def _apply_axial_rope(x, cos, sin):
    xs = x.reshape(x.shape[:-1] + (2, 2, ROPE_PAIRS))
    x1, x2 = xs[..., 0, :], xs[..., 1, :]
    cb, sb = cos[None, :, None], sin[None, :, None]
    out = jnp.stack([x1 * cb - x2 * sb, x1 * sb + x2 * cb], axis=-2)
    return out.reshape(x.shape)

def _gqa_softmax(q, k, v):
    s = jnp.einsum('bqkgd,bskd->bkgqs', q, k).astype(jnp.float32) * (HEAD_DIM ** -0.5)
    p = jax.nn.softmax(s, axis=-1).astype(v.dtype)
    return jnp.einsum('bkgqs,bskd->bqkgd', p, v)

def _attention_mixer(h, hc, wqkv, q_gain, k_gain, wo, cos, sin, need_ctx):
    B, L, _ = h.shape
    C = hc.shape[1]
    nq = N_HEADS * HEAD_DIM
    nk = N_KV_HEADS * HEAD_DIM
    qkv = h @ wqkv
    q = qkv[..., :nq].reshape(B, L, N_HEADS, HEAD_DIM)
    k = qkv[..., nq:nq + nk].reshape(B, L, N_KV_HEADS, HEAD_DIM)
    v = qkv[..., nq + nk:].reshape(B, L, N_KV_HEADS, HEAD_DIM)
    q = _apply_axial_rope(_rmsnorm(q, q_gain), cos, sin)
    k = _apply_axial_rope(_rmsnorm(k, k_gain), cos, sin)
    qkv_c = hc @ (wqkv if need_ctx else wqkv[:, nq:])
    kv_c = qkv_c[..., -2 * nk:]
    k_c = _rmsnorm(kv_c[..., :nk].reshape(B, C, N_KV_HEADS, HEAD_DIM), k_gain)
    v_c = kv_c[..., nk:].reshape(B, C, N_KV_HEADS, HEAD_DIM)
    k_all = jnp.concatenate([k_c, k], axis=1)
    v_all = jnp.concatenate([v_c, v], axis=1)
    nb = L // Q_BLOCK
    q_blocks = q.reshape(B, nb, Q_BLOCK, N_KV_HEADS, KV_GROUP, HEAD_DIM).transpose(1, 0, 2, 3, 4, 5)
    o = lax.map(lambda qb: _gqa_softmax(qb, k_all, v_all), q_blocks)
    o = o.transpose(1, 0, 2, 3, 4, 5).reshape(B, L, nq)
    y = o @ wo
    yc = None
    if need_ctx:
        q_c = _rmsnorm(qkv_c[..., :nq].reshape(B, C, N_KV_HEADS, KV_GROUP, HEAD_DIM), q_gain)
        yc = _gqa_softmax(q_c, k_c, v_c).reshape(B, C, nq) @ wo
    return y, yc

def _centred_shift_delta(u):
    pad = jnp.pad(u, ((0, 0), (1, 1), (0, 0)))
    return 0.5 * (pad[:, :-2] + pad[:, 2:]) - u

def _rwkv_branches(u, mix, w_rkv, w0, w1, w2, a0, a1, a2, g1, g2, k_k, k_a, readout):
    B, T, _ = u.shape
    xx = _centred_shift_delta(u)

    def lerp(j):
        return u + xx * mix[j]

    sel = (0, 2, 3) if readout else (2, 3)
    proj = jnp.einsum('jbtd,jde->jbte', jnp.stack([lerp(s) for s in sel]), w_rkv[-len(sel):])
    k = proj[-2].astype(jnp.float32)

    def heads(z):
        return z.reshape(B, T, RWKV_HEADS, RWKV_HEAD).astype(jnp.float32)

    kk = heads(k * k_k)
    kk = kk * lax.rsqrt(jnp.maximum(jnp.sum(kk * kk, axis=-1, keepdims=True), 1e-24))
    xw, xa = lerp(1), lerp(4)
    dirs = []
    for d in range(2):
        w_log = -jax.nn.softplus(-(w0[d] + jnp.tanh(xw @ w1[d]) @ w2[d]).astype(jnp.float32)) - 0.5
        decay = jnp.exp(-jnp.exp(w_log))
        a = jax.nn.sigmoid((a0[d] + (xa @ a1[d]) @ a2[d]).astype(jnp.float32))
        k_d = k * (1.0 + (a - 1.0) * k_a)
        dirs.append((heads(decay), heads(k_d), heads(a)))
    r = heads(proj[0]) if readout else None
    g = (jax.nn.sigmoid(lerp(5) @ g1) @ g2) if readout else None
    return r, heads(proj[-1]), kk, dirs, g

def _wkv_scan(S0, decay, k, v, kk, a, r, reverse):
    xs = (decay, k, v, kk, a) + (() if r is None else (r,))

    def step(S, inp):
        w_t, k_t, v_t, kk_t, a_t = inp[:5]
        sa = jnp.einsum('bhvk,bhk->bhv', S, -kk_t)
        S = (S * w_t[:, :, None, :] + sa[..., None] * (kk_t * a_t)[:, :, None, :]
             + v_t[..., None] * k_t[:, :, None, :])
        y = jnp.einsum('bhvk,bhk->bhv', S, inp[5]) if len(inp) == 6 else None
        return S, y

    S, ys = lax.scan(step, S0, tuple(jnp.moveaxis(z, 1, 0) for z in xs), reverse=reverse)
    return S, (None if ys is None else jnp.moveaxis(ys, 0, 1))

def _rwkv_readout(wkv, r, v, k_dirs, g, r_k, ln_g, ln_b, wo, dtype):
    B, T, H, N = wkv.shape
    mu = jnp.mean(wkv, axis=-1, keepdims=True)
    var = jnp.mean(jnp.square(wkv - mu), axis=-1, keepdims=True)
    gn = ((wkv - mu) * lax.rsqrt(var + GN_EPS)).reshape(B, T, H * N) * ln_g + ln_b
    bonus = sum(jnp.sum(r * k_d * r_k, axis=-1, keepdims=True) for k_d in k_dirs) * v
    out = (gn + bonus.reshape(B, T, H * N)) * g
    return out.astype(dtype) @ wo

def _rwkv7_mixer(h, hc, mix, w_rkv, w0, w1, w2, a0, a1, a2, g1, g2, k_k, k_a, r_k,
                 ln_g, ln_b, wo, need_ctx):
    params = (mix, w_rkv, w0, w1, w2, a0, a1, a2, g1, g2, k_k, k_a)
    r, v, kk, dirs, g = _rwkv_branches(h, *params, readout=True)
    rc, vc, kkc, dirs_c, gc = _rwkv_branches(hc, *params, readout=need_ctx)
    B = h.shape[0]
    S0 = jnp.zeros((B, RWKV_HEADS, RWKV_HEAD, RWKV_HEAD), jnp.float32)
    wkv = 0.0
    wkv_c = 0.0
    for d, rev in enumerate((False, True)):
        decay_c, k_c, a_c = dirs_c[d]
        S_ctx, yc = _wkv_scan(S0, decay_c, k_c, vc, kkc, a_c, rc, rev)
        decay, k_d, a_d = dirs[d]
        _, y = _wkv_scan(S_ctx, decay, k_d, v, kk, a_d, r, rev)
        wkv = wkv + y
        if need_ctx:
            wkv_c = wkv_c + yc
    y = _rwkv_readout(wkv, r, v, [dd[1] for dd in dirs], g, r_k, ln_g, ln_b, wo, h.dtype)
    yc = None
    if need_ctx:
        yc = _rwkv_readout(wkv_c, rc, vc, [dd[1] for dd in dirs_c], gc, r_k, ln_g, ln_b, wo, hc.dtype)
    return y, yc

def _swiglu(h, wg, wu, wd):
    return (jax.nn.silu(h @ wg) * (h @ wu)) @ wd

def second_inputs(seed: int = 0) -> dict:
    key = jax.random.key(seed)
    ks = iter(jax.random.split(key, 40))
    f32 = jnp.float32
    n_attn = len(range(0, DEPTH_2, N_MIXERS))
    n_rwkv = len(range(1, DEPTH_2, N_MIXERS))
    D = D_MODEL

    def nrm(shape, std):
        return jax.random.normal(next(ks), shape, f32) * std

    def unif(shape, lo, hi):
        return jax.random.uniform(next(ks), shape, f32, lo, hi)

    nqkv = (N_HEADS + 2 * N_KV_HEADS) * HEAD_DIM
    return {
        "x": nrm((BATCH, SEQ, D), 1.0),
        "c": nrm((BATCH, D), 1.0),
        "ctx": nrm((BATCH, CTX_LEN, D), 1.0),
        "c_ctx": nrm((D,), 1.0),
        "mod_w": nrm((DEPTH_2, D, 6 * D), 0.3 * D ** -0.5),
        "mod_b": nrm((DEPTH_2, 6 * D), 0.02),
        "norm1_g": 1.0 + nrm((DEPTH_2, D), 0.02),
        "norm2_g": 1.0 + nrm((DEPTH_2, D), 0.02),
        "ffn_wg": nrm((DEPTH_2, D, D_FF), D ** -0.5),
        "ffn_wu": nrm((DEPTH_2, D, D_FF), D ** -0.5),
        "ffn_wd": nrm((DEPTH_2, D_FF, D), D_FF ** -0.5),
        "attn_wqkv": nrm((n_attn, D, nqkv), D ** -0.5),
        "attn_q_gain": 1.0 + nrm((n_attn, HEAD_DIM), 0.02),
        "attn_k_gain": 1.0 + nrm((n_attn, HEAD_DIM), 0.02),
        "attn_wo": nrm((n_attn, N_HEADS * HEAD_DIM, D), (N_HEADS * HEAD_DIM) ** -0.5),
        "rwkv_mix": unif((n_rwkv, 6, D), 0.0, 1.0),
        "rwkv_wrkv": nrm((n_rwkv, 3, D, D), D ** -0.5),
        "rwkv_w0": unif((n_rwkv, 2, D), -6.0, -1.0),
        "rwkv_w1": nrm((n_rwkv, 2, D, DECAY_LORA), D ** -0.5),
        "rwkv_w2": nrm((n_rwkv, 2, DECAY_LORA, D), 0.5 * DECAY_LORA ** -0.5),
        "rwkv_a0": nrm((n_rwkv, 2, D), 0.1),
        "rwkv_a1": nrm((n_rwkv, 2, D, ICLR_LORA), D ** -0.5),
        "rwkv_a2": nrm((n_rwkv, 2, ICLR_LORA, D), 0.5 * ICLR_LORA ** -0.5),
        "rwkv_g1": nrm((n_rwkv, D, GATE_LORA), D ** -0.5),
        "rwkv_g2": nrm((n_rwkv, GATE_LORA, D), GATE_LORA ** -0.5),
        "rwkv_k_k": 0.85 + nrm((n_rwkv, D), 0.05),
        "rwkv_k_a": 1.0 + nrm((n_rwkv, D), 0.05),
        "rwkv_r_k": nrm((n_rwkv, RWKV_HEADS, RWKV_HEAD), 0.1),
        "rwkv_ln_g": 1.0 + nrm((n_rwkv, D), 0.02),
        "rwkv_ln_b": nrm((n_rwkv, D), 0.02),
        "rwkv_wo": nrm((n_rwkv, D, D), D ** -0.5),
        "final_g": 1.0 + nrm((D,), 0.02),
    }

def second_block(x, c, ctx, c_ctx, mod_w, mod_b, norm1_g, norm2_g, ffn_wg, ffn_wu, ffn_wd,
              attn_wqkv, attn_q_gain, attn_k_gain, attn_wo,
              rwkv_mix, rwkv_wrkv, rwkv_w0, rwkv_w1, rwkv_w2, rwkv_a0, rwkv_a1, rwkv_a2,
              rwkv_g1, rwkv_g2, rwkv_k_k, rwkv_k_a, rwkv_r_k, rwkv_ln_g, rwkv_ln_b, rwkv_wo,
              final_g):
    B, L, D = x.shape
    rows = L // GRID_W
    cos, sin = _axial_rope_tables(rows, x.dtype)
    sc = jax.nn.silu(c)
    scc = jax.nn.silu(c_ctx)
    xc = ctx
    for i in range(DEPTH_2):
        last = i == DEPTH_2 - 1
        j = i // N_MIXERS
        m = (sc @ mod_w[i] + mod_b[i]).reshape(B, 6, 1, D)
        mc = (scc @ mod_w[i] + mod_b[i]).reshape(6, D)
        h = _rmsnorm(x, norm1_g[i]) * (1.0 + m[:, 1]) + m[:, 0]
        hc = _rmsnorm(xc, norm1_g[i]) * (1.0 + mc[1]) + mc[0]
        if i % N_MIXERS == 0:
            y, yc = _attention_mixer(h, hc, attn_wqkv[j], attn_q_gain[j], attn_k_gain[j],
                                     attn_wo[j], cos, sin, not last)
        else:
            y, yc = _rwkv7_mixer(h, hc, rwkv_mix[j], rwkv_wrkv[j], rwkv_w0[j], rwkv_w1[j],
                                 rwkv_w2[j], rwkv_a0[j], rwkv_a1[j], rwkv_a2[j], rwkv_g1[j],
                                 rwkv_g2[j], rwkv_k_k[j], rwkv_k_a[j], rwkv_r_k[j],
                                 rwkv_ln_g[j], rwkv_ln_b[j], rwkv_wo[j], not last)
        x = x + m[:, 2] * y
        h2 = _rmsnorm(x, norm2_g[i]) * (1.0 + m[:, 4]) + m[:, 3]
        x = x + m[:, 5] * _swiglu(h2, ffn_wg[i], ffn_wu[i], ffn_wd[i])
        if not last:
            xc = xc + mc[2] * yc
            hc2 = _rmsnorm(xc, norm2_g[i]) * (1.0 + mc[4]) + mc[3]
            xc = xc + mc[5] * _swiglu(hc2, ffn_wg[i], ffn_wu[i], ffn_wd[i])
    return _rmsnorm(x, final_g)


_first_inputs = second_inputs


def second_inputs(seed=0):
    import zlib

    import numpy as np

    out = dict(_first_inputs(seed))
    spreads = {}
    factors = {'c_ctx': 3.552,
     'norm1_g': 8.0,
     'norm2_g': 8.0,
     'attn_q_gain': 8.0,
     'attn_k_gain': 8.0,
     'rwkv_w1': 64.0,
     'rwkv_w2': 64.0,
     'rwkv_a0': 8.0,
     'rwkv_a1': 3.556,
     'rwkv_a2': 3.524,
     'rwkv_k_k': 64.0,
     'rwkv_k_a': 8.0,
     'rwkv_ln_g': 64.0,
     'rwkv_ln_b': 64.0,
     'final_g': 8.239,
     'rwkv_w0': 8.0}
    for name, (base, spread) in spreads.items():
        noise = np.random.default_rng([zlib.crc32(name.encode()), seed]).standard_normal(out[name].shape)
        drawn = base * np.exp(spread * noise) if base else spread * noise
        out[name] = __import__('jax').numpy.asarray(drawn.astype(out[name].dtype))
    for name, factor in factors.items():
        out[name] = (out[name] * factor).astype(out[name].dtype)
    return out


_narrow_inputs = second_inputs


def second_inputs(seed=0):
    out = dict(_narrow_inputs(seed))
    wider = {'rwkv_k_k': 12.0, 'rwkv_ln_g': 12.0, 'rwkv_ln_b': 12.0, 'final_g': 3.2}
    for name, times in wider.items():
        mean = out[name].mean()
        out[name] = (mean + times * (out[name] - mean)).astype(out[name].dtype)
    return out


def setup_inputs(seed=0):
    out = dict(first_inputs(seed))
    for name, value in second_inputs(seed + 1).items():
        if name != "x":
            out[name + "_2"] = value
    return out


def reference(
    x, mem, mix_norm_g, w_in, q_norm_g, kv_norm_g, w_uq, w_ukv, hy_conv_w, hy_conv_b, hy_w1,
    hy_b1, hy_freq, hy_w2, hy_b2, hy_w3, hy_b3, hy_decay, hy_skip, attn_out_g, hy_out_g, w_out,
    cross_norm_g, mem_norm_g, w_mq, w_mkv, w_mo, ffn_norm_g, w_route_group, b_route_group,
    w_route_expert, b_route_expert, w_gate, w_up, w_down, final_norm_g, c_2, ctx_2, c_ctx_2,
    mod_w_2, mod_b_2, norm1_g_2, norm2_g_2, ffn_wg_2, ffn_wu_2, ffn_wd_2, attn_wqkv_2,
    attn_q_gain_2, attn_k_gain_2, attn_wo_2, rwkv_mix_2, rwkv_wrkv_2, rwkv_w0_2, rwkv_w1_2,
    rwkv_w2_2, rwkv_a0_2, rwkv_a1_2, rwkv_a2_2, rwkv_g1_2, rwkv_g2_2, rwkv_k_k_2, rwkv_k_a_2,
    rwkv_r_k_2, rwkv_ln_g_2, rwkv_ln_b_2, rwkv_wo_2, final_g_2,
):
    x = first_block(
        x, mem, mix_norm_g, w_in, q_norm_g, kv_norm_g, w_uq, w_ukv, hy_conv_w, hy_conv_b, hy_w1,
        hy_b1, hy_freq, hy_w2, hy_b2, hy_w3, hy_b3, hy_decay, hy_skip, attn_out_g, hy_out_g,
        w_out, cross_norm_g, mem_norm_g, w_mq, w_mkv, w_mo, ffn_norm_g, w_route_group,
        b_route_group, w_route_expert, b_route_expert, w_gate, w_up, w_down, final_norm_g,
    )
    return second_block(
        x, c_2, ctx_2, c_ctx_2, mod_w_2, mod_b_2, norm1_g_2, norm2_g_2, ffn_wg_2, ffn_wu_2,
        ffn_wd_2, attn_wqkv_2, attn_q_gain_2, attn_k_gain_2, attn_wo_2, rwkv_mix_2, rwkv_wrkv_2,
        rwkv_w0_2, rwkv_w1_2, rwkv_w2_2, rwkv_a0_2, rwkv_a1_2, rwkv_a2_2, rwkv_g1_2, rwkv_g2_2,
        rwkv_k_k_2, rwkv_k_a_2, rwkv_r_k_2, rwkv_ln_g_2, rwkv_ln_b_2, rwkv_wo_2, final_g_2,
    )


_drawn_inputs = setup_inputs


def setup_inputs(seed=0):
    import zlib

    import numpy as np

    out = dict(_drawn_inputs(seed))
    spreads = {}
    factors = {'rwkv_k_k_2': 4.469, 'rwkv_ln_g_2': 4.489, 'rwkv_ln_b_2': 4.151}
    for name, (base, spread) in spreads.items():
        noise = np.random.default_rng([zlib.crc32(name.encode()), seed]).standard_normal(out[name].shape)
        drawn = base * np.exp(spread * noise) if base else spread * noise
        out[name] = __import__('jax').numpy.asarray(drawn.astype(out[name].dtype))
    for name, factor in factors.items():
        out[name] = (out[name] * factor).astype(out[name].dtype)
    return out
```

```python
from contextlib import ExitStack

import numpy as np

import concourse.bass as bass
from concourse import mybir
from concourse.alu_op_type import AluOpType as ALU

F32R = mybir.dt.float32r
F32 = mybir.dt.float32
ACT = mybir.ActivationFunctionType
AX = mybir.AxisListType.X

P = 128
D = 1024
KC = D // P
T = 512
C = 256
TC = T + C
EPS = 1e-6
BANK = 512
SLAB = 2048
SLOTS = 5

NH1, NOPE, ROT, DV = 8, 64, 32, 64
QK = NOPE + ROT
QR, KVR = 256, 128
HW = 512
L2 = 2 * T
GROUPS, EXPERTS = 4, 8
MEM_H, MEM_D = 4, 256
QH, KVH, HD = 16, 4, 64
FF = 2816
CH = 64
DECAY_SCALE = -float(np.exp(-0.5))
GN_EPS = 64e-5


def vector_columns():
    at, out = 0, {}
    for name, n in [("mix_g", 8), ("qn_g", 2), ("kvn_g", 1), ("aout_g", 4), ("hyout_g", 4), ("cross_g", 8),
                    ("mem_g", 8), ("ffn_g", 8), ("fin_g", 8), ("conv_w", 36), ("conv_b", 12), ("hb1", 1),
                    ("hf0", 1), ("hb2", 1), ("hf1", 1), ("skip1", 4), ("hw1", 64), ("hw2", 64),
                    ("b_route", 36), ("cond", 16), ("mod_b", 96), ("n1_g", 16), ("n2_g", 16), ("q_gain", 1),
                    ("k_gain", 1), ("lerp", 48), ("w0", 16), ("a0", 16), ("k_k", 8), ("k_a", 8), ("r_k", 8),
                    ("ln_g", 8), ("ln_b", 8), ("fin2_g", 8)]:
        out[name] = (at, n)
        at += n
    return out, at


VCOL, NVEC = vector_columns()


def table_columns():
    at, out = 0, {}
    for name, n in [("ident", 128), ("ones", 128), ("heads64", 128), ("swap16", 128), ("eps", 1), ("gn_eps", 1),
                    ("kk_eps", 1), ("dft_scale", 2), ("t01", 4), ("expert_rank", 8), ("resident", 0),
                    ("cos96", 512), ("sin96", 512),
                    ("dft_c", 2048), ("dft_s", 2048), ("alt_col", 128), ("alt_row", 512), ("zemb", 512),
                    ("cos_ax", 512), ("sin_ax", 512),
                    ("eye", 64), ("masks", 16 * 64), ("scan_keep", TC)]:
        out[name] = (at, n)
        at += n
    return out, at


TCOL, NTAB = table_columns()
RESIDENT = TCOL["resident"][0]


def tables():
    t = np.zeros((P, NTAB), np.float32)

    def put(name, a):
        c, n = TCOL[name]
        a = np.asarray(a, np.float64)
        t[:a.shape[0], c:c + n] = a.reshape(a.shape[0], n)

    r = np.arange(P)
    put("ident", np.eye(P))
    put("ones", np.ones((P, P)))
    put("heads64", (r[:, None] // 64 == r[None] // 64))
    put("swap16", (r[:, None] == (r[None] ^ 16)))
    put("eps", np.full((P, 1), EPS))
    put("gn_eps", np.full((P, 1), GN_EPS))
    put("kk_eps", np.full((P, 1), 1e-24))
    sc = np.full((P, 2), 2.0 / L2)
    sc[0, 0] = 1.0 / L2
    put("dft_scale", sc)
    put("t01", -(np.arange(T).reshape(4, P).T / T))
    put("expert_rank", np.tile(8.0 - np.arange(8), (P, 1)))
    half = ROT // 2
    f32 = np.float32
    inv = f32(10000.0) ** (-np.arange(half, dtype=f32) / f32(half))
    ang = (np.arange(T, dtype=f32)[:, None] * inv[None]).astype(np.float64)
    co, si = np.ones((QK, T)), np.zeros((QK, T))
    co[NOPE:NOPE + half] = co[NOPE + half:] = np.cos(ang).T
    si[NOPE:NOPE + half], si[NOPE + half:] = -np.sin(ang).T, np.sin(ang).T
    put("cos96", co)
    put("sin96", si)
    k = np.arange(T)
    w = 2 * np.pi * ((k[:, None] * k[None]) % L2) / L2
    put("dft_c", np.cos(w).reshape(4, P, T).transpose(1, 0, 2))
    put("dft_s", -np.sin(w).reshape(4, P, T).transpose(1, 0, 2))
    alt = 1.0 - 2.0 * (np.arange(T) % 2)
    a = np.zeros((P, P))
    a[:, 0] = alt[:P]
    put("alt_col", a)
    a = np.zeros((P, T))
    a[0] = alt
    put("alt_row", a)
    bands = np.linspace(1e-4, 15, 16, dtype=f32)
    tt = np.arange(T, dtype=f32)
    an = (f32(2.0 * np.pi) * tt[:, None] * bands[None] / f32(T)).astype(np.float64)
    put("zemb", np.concatenate([(tt / T)[:, None], np.cos(an), -np.sin(an)], 1).T)
    inv = f32(10000.0) ** (-np.arange(16, dtype=f32) / f32(16))
    row, col = (np.arange(T) // 64).astype(f32), (np.arange(T) % 64).astype(f32)
    co, si = np.zeros((P, T)), np.zeros((P, T))
    for p in range(P):
        an = ((row, col)[p % 64 // 32] * inv[p % 16]).astype(np.float64)
        co[p], si[p] = np.cos(an), np.sin(an) * (1 if p % 32 // 16 else -1)
    put("cos_ax", co)
    put("sin_ax", si)
    ri, ci = (r % 64)[:, None], np.arange(64)[None]
    put("eye", ri == ci)
    ms = [ri < ci, ri > ci, ri <= ci, ri >= ci]
    for m in (1, 2, 4, 8, 16, 32):
        low = (ri // (2 * m) == ci // (2 * m)) & (ri % (2 * m) >= m) & (ci % (2 * m) < m)
        up = (ri // (2 * m) == ci // (2 * m)) & (ci % (2 * m) >= m) & (ri % (2 * m) < m)
        ms += [low, up]
    put("masks", np.stack(ms, 1))
    put("scan_keep", np.tile((np.arange(TC) % CH != 0), (P, 1)))
    return t


SWAP_ROT = list(range(NOPE)) + list(range(NOPE + 16, NOPE + 32)) + list(range(NOPE, NOPE + 16))


def slab_layout():
    block1 = [("in_q", 1), ("in_kv", 1), ("in_krs", 1), ("in_hy", 6), ("uq", 1), ("uqs", 1), ("ukv", 1),
              ("decay", 1), ("hw3", 1), ("skip0", 1), ("out", 4), ("mk", 4), ("mv", 4), ("mq", 4), ("mo", 4),
              ("route", 1), ("moe", 3 * GROUPS * EXPERTS)]
    block2 = [("mod0", 24), ("qkv_q", 4), ("qkv_k", 2), ("qkv_v", 1), ("wo0", 4), ("ffn0", 33), ("mod1", 24),
              ("rw_k", 4), ("rw_v", 4), ("lora1", 1), ("g1", 1), ("rw_r", 4), ("lora2", 1), ("g2", 1), ("wo1", 4),
              ("ffn1", 33)]
    at, out = 0, {}
    for name, n in block1 + block2:
        out[name] = (at, n)
        at += n
    return out, at


SLABS, NSLAB = slab_layout()


def swiglu_slab(i, n, kind):
    if kind == 2:
        return 3 * i + 4 if i < n - 1 else 3 * n - 1
    return kind if i == 0 else 3 * i - 1 + kind


def pack_slabs(a):
    wall = np.zeros((NSLAB, P, SLAB), np.float32)

    def put(name, i, w, col=0):
        k, m = w.shape
        kc = -(-k // P)
        if k % P:
            wall[SLABS[name][0] + i, :k, col:col + m] = w
        else:
            wall[SLABS[name][0] + i, :, col:col + kc * m] = w.reshape(kc, P, m).transpose(1, 0, 2).reshape(P, kc * m)

    def put_all(name, w, cols=256):
        for i in range(w.shape[1] // cols):
            put(name, i, w[:, i * cols:(i + 1) * cols])

    def put_swiglu(name, i, wg, wu, wd):
        n = SLABS[name][1] // 3
        put(name, swiglu_slab(i, n, 0), wg)
        put(name, swiglu_slab(i, n, 1), wu)
        put(name, swiglu_slab(i, n, 2), wd)

    w = a["w_in"][0]
    put("in_q", 0, w[:, :QR])
    put("in_kv", 0, w[:, QR:QR + KVR])
    kr = w[:, QR + KVR - NOPE:QR + KVR + ROT]
    put("in_kv", 0, kr, KC * KVR)
    put("in_krs", 0, kr[:, SWAP_ROT])
    put_all("in_hy", w[:, QR + KVR + ROT:])
    uq = a["w_uq"][0].reshape(QR, NH1, QK)
    put("uq", 0, uq.reshape(QR, -1))
    put("uqs", 0, uq[:, :, SWAP_ROT].reshape(QR, -1))
    ukv = a["w_ukv"][0].reshape(KVR, NH1, 2, 64).transpose(0, 2, 1, 3)
    put("ukv", 0, ukv.reshape(KVR, -1))
    put("decay", 0, np.broadcast_to(a["hy_decay"][0], (P, 2048)))
    put("hw3", 0, np.concatenate([a["hy_w3"][0], a["hy_b3"]], 0))
    put("skip0", 0, np.broadcast_to(a["hy_skip"][0, 0], (P, HW)))
    put_all("out", a["w_out"][0])
    put_all("mk", a["w_mkv"][0][:, :D])
    put_all("mv", a["w_mkv"][0][:, D:])
    put_all("mq", a["w_mq"][0])
    put_all("mo", a["w_mo"][0])
    put("route", 0, np.concatenate([a["w_route_group"][0], a["w_route_expert"][0]], 1))
    for e in range(GROUPS * EXPERTS):
        g, x = divmod(e, EXPERTS)
        put_swiglu("moe", e, a["w_gate"][0, g, x], a["w_up"][0, g, x], a["w_down"][0, g, x])
    for i in range(2):
        put_all(f"mod{i}", a["mod_w_2"][i])
        for j in range(FF // 256):
            s = slice(256 * j, 256 * j + 256)
            put_swiglu(f"ffn{i}", j, a["ffn_wg_2"][i][:, s], a["ffn_wu_2"][i][:, s], a["ffn_wd_2"][i][s])
    w = a["attn_wqkv_2"][0]
    put_all("qkv_q", w[:, :D])
    k2 = np.repeat(w[:, D:D + 256].reshape(D, KVH, 1, HD), 2, 2).reshape(D, 512)
    put_all("qkv_k", k2)
    put_all("qkv_v", w[:, D + 256:])
    put_all("wo0", a["attn_wo_2"][0])
    put_all("rw_r", a["rwkv_wrkv_2"][0, 0])
    put_all("rw_k", a["rwkv_wrkv_2"][0, 1])
    put_all("rw_v", a["rwkv_wrkv_2"][0, 2])
    put("lora1", 0, a["rwkv_w1_2"][0].transpose(1, 0, 2).reshape(D, P))
    put("lora1", 0, a["rwkv_a1_2"][0].transpose(1, 0, 2).reshape(D, P), D)
    put("g1", 0, a["rwkv_g1_2"][0])
    put("lora2", 0, a["rwkv_w2_2"][0].reshape(P, D))
    put("lora2", 0, a["rwkv_a2_2"][0].reshape(P, D), D)
    put("g2", 0, a["rwkv_g2_2"][0])
    put_all("wo1", a["rwkv_wo_2"][0])
    return wall


def pack_vectors(a):
    v = np.zeros((P, NVEC), np.float32)

    def put(name, x, at=0):
        x = np.asarray(x)
        c = VCOL[name][0] + at
        if x.ndim == 1:
            x = x.reshape(-1, P).T if x.size >= P else x[:, None]
        v[:x.shape[0], c:c + x.shape[1]] = x

    for name, src in [("mix_g", "mix_norm_g"), ("qn_g", "q_norm_g"), ("kvn_g", "kv_norm_g"), ("aout_g", "attn_out_g"),
                      ("hyout_g", "hy_out_g"), ("cross_g", "cross_norm_g"), ("mem_g", "mem_norm_g"),
                      ("ffn_g", "ffn_norm_g"), ("conv_b", "hy_conv_b"), ("hb1", "hy_b1"), ("hb2", "hy_b2"),
                      ("k_k", "rwkv_k_k_2"), ("k_a", "rwkv_k_a_2"),
                      ("ln_g", "rwkv_ln_g_2"), ("ln_b", "rwkv_ln_b_2")]:
        put(name, a[src][0])
    put("r_k", a["rwkv_r_k_2"][0].reshape(-1))
    put("fin_g", a["final_norm_g"])
    put("fin2_g", a["final_g_2"])
    for j in range(3):
        put("conv_w", a["hy_conv_w"][0, j], 12 * j)
    put("hf0", a["hy_freq"][0, 0])
    put("hf1", a["hy_freq"][0, 1])
    put("skip1", a["hy_skip"][0, 1])
    put("hw1", a["hy_w1"][0])
    put("hw2", a["hy_w2"][0])
    put("b_route", np.broadcast_to(np.concatenate([a["b_route_group"][0], a["b_route_expert"][0]]), (P, 36)))
    put("cond", np.stack([a["c_2"][0].reshape(KC, P), a["c_ctx_2"].reshape(KC, P)], 2).transpose(1, 0, 2).reshape(P, 16))
    for i in range(2):
        put("mod_b", a["mod_b_2"][i], 48 * i)
        put("n1_g", a["norm1_g_2"][i], 8 * i)
        put("n2_g", a["norm2_g_2"][i], 8 * i)
        put("w0", a["rwkv_w0_2"][0, i], 8 * i)
        put("a0", a["rwkv_a0_2"][0, i], 8 * i)
    put("q_gain", np.concatenate([a["attn_q_gain_2"][0]] * 2))
    put("k_gain", np.concatenate([a["attn_k_gain_2"][0]] * 2))
    for j in range(6):
        put("lerp", a["rwkv_mix_2"][0, j], 8 * j)
    return v


def feature_major(x):
    return np.ascontiguousarray(x.T.reshape(KC, P, -1).transpose(1, 0, 2))


class Lane:

    def __init__(self, m, eng, name):
        self.m, self.eng, self.name = m, eng, name
        self.step, self.steps = m.sem(f"{name}_step"), 0
        self.counts = {}
        self.bank_at, self.filled, self.freed = 0, [0] * 8, [0] * 8
        self.slab_at = 0

    def next_step(self):
        self.steps += 1
        return self.steps

    def nth(self, what, n=1):
        self.counts[what] = self.counts.get(what, 0) + n
        return self.counts[what]

    def next_bank(self, n=1):
        if n == 2 and self.bank_at % 8 == 7:
            self.bank_at += 1
        b = self.bank_at % 8
        self.bank_at += n
        self.bank_full, self.bank_free = self.m.bank_full[b], self.m.bank_free[b]
        self.bank_free2 = self.m.bank_free[(b + 1) % 8]
        self.bank_frees = [(self.m.bank_free[b + i], self.freed[b + i]) for i in range(n) if self.freed[b + i]]
        self.filled[b] += 1
        for i in range(n):
            self.freed[b + i] += 1
        self.fill = self.filled[b]
        return self.m.psum[:, b * BANK:(b + n) * BANK]

    def next_slab(self, name, i=0):
        n = self.slab_at
        assert n == SLABS[name][0] + i, (name, i, n)
        self.slab_at += 1
        self.landed, self.landings = self.m.slab_landed[n % SLOTS], 16 * (n // SLOTS + 1)
        self.high, self.low = self.m.high[:, n % SLOTS, :], self.m.low[:, n % SLOTS, :]
        return self.m.ring[:, n % SLOTS, :]


class Mem:

    def __init__(self, nc, ctx):
        self.nc, self.ctx, self.sems = nc, ctx, {}

    def sem(self, name):
        if name not in self.sems:
            self.sems[name] = self.ctx.enter_context(self.nc.semaphore(name))
        return self.sems[name]

    def sb(self, name, shape):
        return self.ctx.enter_context(self.nc.sbuf_tensor(name, shape, F32))

    def rounded(self, name, off, *shape):
        assert off + int(np.prod(shape)) <= ARENA, (name, off)
        return self.nc.alloc_sbuf_tensor_at(name, [P, *shape], F32R, offset=self.arena_place + 4 * off)

    def at(self, off, *shape, parts=P):
        n = int(np.prod(shape))
        assert off + n <= ARENA, (off, shape)
        v = self.arena[0:parts, off:off + n]
        if len(shape) == 2:
            v = v.rearrange("p (a b) -> p a b", a=shape[0])
        if len(shape) == 3:
            v = v.rearrange("p (a b c) -> p a b c", a=shape[0], b=shape[1])
        return v

    def slab_of(self, L, name):
        n = SLABS[name][0]
        L.eng.wait_ge(self.slab_landed[n % SLOTS], 16 * (n // SLOTS + 1))
        return self.ring[:, n % SLOTS, :]

    def vec(self, name, i=0, n=1, parts=P):
        c = VCOL[name][0] + i
        return self.vecs[0:parts, c:c + n]

    def tab(self, name, i=0, n=None, parts=P):
        c, w = TCOL[name]
        return self.tabs[0:parts, c + i:c + i + (w if n is None else n)]


ARENA = 34000
HIGH = ARENA - SLOTS * SLAB - 208
NX, NC_ = (0, T), (T, C)


def matmuls(L, out, pairs):
    for i, (a, b) in enumerate(pairs):
        last = L.eng.matmul(out, a, b, start=(i == 0), stop=(i == len(pairs) - 1))
    return last


def split_matmuls(L, out, terms):
    for i, (a_hi, a_lo, b_hi, b_lo) in enumerate(terms):
        L.eng.matmul(out, a_hi, b_hi, start=(i == 0), stop=False)
        L.eng.matmul(out, a_hi, b_lo, start=False, stop=False)
        last = L.eng.matmul(out, a_lo, b_hi, start=False, stop=(i == len(terms) - 1))
    return last


def round_slab(L, m, n):
    L.eng.wait_ge(m.slab_landed[n % SLOTS], 16 * (n // SLOTS + 1))
    L.eng.activation(m.high[:, n % SLOTS, :], m.ring[:, n % SLOTS, :], ACT.Copy).then_inc(m.sem("slab_rounded"), 1)


def split_slabs(L, m, name):
    for n in range(SLABS[name][0], SLABS[name][0] + SLABS[name][1]):
        L.eng.wait_ge(m.sem("slab_rounded"), L.nth("slab_rounded"))
        L.eng.tensor_tensor(m.low[:, n % SLOTS, :], m.ring[:, n % SLOTS, :], m.high[:, n % SLOTS, :].bitcast(F32),
                            ALU.subtract).then_inc(m.sem("slab_split"), 1)


def split_vector(L, m, x, high, low, what):
    L.eng.tensor_copy(high, x).then_inc(L.step, 1)
    L.eng.wait_ge(L.step, L.next_step())
    L.eng.tensor_tensor(low, x, high.bitcast(F32), ALU.subtract).then_inc(m.sem(what), 1)
    L.nth(what)


def norm_tensor(L, m, sq, n, lo=0):
    ps = L.next_bank()
    for bank_free, count in L.bank_frees:
        L.eng.wait_ge(bank_free, count)
    w = sq(0).shape[1]
    for c in range(n):
        L.eng.wait_ge(m.sem("squares"), L.nth("squares"))
        last = L.eng.matmul(ps[:, :w], m.tab("ones"), sq(c), start=(c == 0), stop=(c == n - 1))
    last.then_inc(L.bank_full, 1)


def norm_scalar(L, m, src, sq, n, eps="eps"):
    for c in range(n):
        L.eng.activation(sq(c), src(c), ACT.Square).then_inc(m.sem("squares"), 1)
        L.eng.wait_ge(m.sem("squares"), L.nth("squares"))
    w = sq(0).shape[1]
    ps = L.next_bank()
    L.eng.wait_ge(L.bank_full, L.fill)
    L.eng.activation(m.root[:, :w], ps[:, :w], ACT.Sqrt, bias=m.tab(eps), scale=1.0 / (n * P)).then_inc(L.step, 1)
    L.eng.wait_ge(L.step, L.next_step())
    L.eng.sem_inc(L.bank_free, 1)
    L.eng.sem_inc(m.sem("root"), 1)
    L.nth("root")


def norm_vector(L, m, src, dst, n, gain, bias=None):
    L.next_bank()
    w = src(0).shape[1]
    L.eng.wait_ge(m.sem("root"), L.nth("root"))
    L.eng.reciprocal(m.root[:, :w], m.root[:, :w]).then_inc(L.step, 1)
    L.eng.wait_ge(L.step, L.next_step())
    for c in range(n):
        L.eng.scalar_tensor_tensor(dst(c), src(c), gain(c), m.root[:, :w], ALU.mult, ALU.mult).then_inc(L.step, 1)
        L.eng.wait_ge(L.step, L.next_step())
        if bias:
            L.eng.tensor_scalar(dst(c), dst(c), bias(c), None, ALU.add).then_inc(L.step, 1)
            L.eng.wait_ge(L.step, L.next_step())


def project_tensor(L, m, name, rhs, groups, kc=KC, cols=256, n=None):
    for i in range(SLABS[name][1] if n is None else n):
        w = L.next_slab(name, i)
        L.eng.wait_ge(L.landed, L.landings)
        for t in range(cols // P):
            for lo, wd in groups:
                ps = L.next_bank()
                for bank_free, count in L.bank_frees:
                    L.eng.wait_ge(bank_free, count)
                matmuls(L, ps[:, :wd], [(w[:, k * cols + t * P:k * cols + (t + 1) * P],
                                                rhs(k)[:, lo:lo + wd]) for k in range(kc)]).then_inc(L.bank_full, 1)
        L.eng.drain().then_inc(m.sem("slab_used"), 1)


def read_banks(L, count, mine, fn):
    for g in range(count):
        if mine(g):
            ps = L.next_bank()
            L.eng.wait_ge(L.bank_full, L.fill)
            fn(g, ps).then_inc(L.step, 1)
            L.eng.wait_ge(L.step, L.next_step())
            L.eng.sem_inc(L.bank_free, 1)
        else:
            L.next_bank()


def even(g):
    return g % 2 == 0


def odd(g):
    return g % 2 == 1


def never(g):
    return False


def always(g):
    return True


LAG = 2
NPROB = 3


def attention_order(heads, qts):
    return [(h, q) for h in range(heads) for q in range(qts)]


def attention_tensor(L, m, A, score, value):
    tiles = attention_order(A.heads, A.qts)
    n, nb = len(tiles), (A.keys + BANK - 1) // BANK
    for i in range(n + LAG + 1):
        if i < n:
            ps = L.next_bank(nb)
            for bank_free, count in L.bank_frees:
                L.eng.wait_ge(bank_free, count)
            score(ps, *tiles[i]).then_inc(L.bank_full, 1)
        if LAG <= i < n + LAG:
            j = i - LAG
            L.eng.wait_ge(m.sem("probs"), L.nth("probs"))
            ps = L.next_bank(nb)
            for bank_free, count in L.bank_frees:
                L.eng.wait_ge(bank_free, count)
            for kt in range(A.keys // P):
                last = L.eng.transpose(ps[:, kt * P:(kt + 1) * P], A.probs[:, j % NPROB, kt * P:(kt + 1) * P],
                                       m.tab("ident"))
            last.then_inc(L.bank_full, 1)
        if i > LAG and (i - LAG) % A.qts == 0:
            h = tiles[i - LAG - 1][0]
            L.eng.wait_ge(m.sem("probs_turned"), L.nth("probs_turned", A.qts))
            for mt in range(A.mts):
                ps = L.next_bank()
                for bank_free, count in L.bank_frees:
                    L.eng.wait_ge(bank_free, count)
                matmuls(L, ps[0:A.vd, 0:A.qts * P], [(value(h, kt, mt), A.turned[:, h % 2, kt, :])
                                                          for kt in range(A.keys // P)]).then_inc(L.bank_full, 1)


def attention_scalar(L, m, A):
    tiles = attention_order(A.heads, A.qts)
    n, nb = len(tiles), (A.keys + BANK - 1) // BANK
    for i in range(n + LAG + 1):
        if i < n:
            ps = L.next_bank(nb)
            L.eng.wait_ge(L.bank_full, L.fill)
            L.eng.wait_ge(m.sem("row_max"), L.nth("row_max"))
            L.eng.activation(A.probs[:, i % NPROB, :], ps[:, :A.keys], ACT.Exp, bias=m.stat[:, i % NPROB:i % NPROB + 1],
                                  scale=A.scale, accum_out=m.stat[:, 4 + i % NPROB:5 + i % NPROB]).then_inc(L.step, 1)
            L.eng.wait_ge(L.step, L.next_step())
            L.eng.sem_inc(L.bank_free, 1)
            if nb == 2:
                L.eng.sem_inc(L.bank_free2, 1)
            L.eng.sem_inc(m.sem("exps"), 1)
            L.nth("exps")
        if LAG <= i < n + LAG:
            h, q = tiles[i - LAG]
            if q == 0 and h >= 2:
                L.eng.wait_ge(m.sem("head_out"), L.nth("head_out"))
            ps = L.next_bank(nb)
            L.eng.wait_ge(L.bank_full, L.fill)
            L.eng.activation(A.turned[:, h % 2, :, q * P:(q + 1) * P],
                                  ps[:, :A.keys].rearrange("p (a b) -> p a b", b=P), ACT.Copy).then_inc(L.step, 1)
            L.eng.wait_ge(L.step, L.next_step())
            L.eng.sem_inc(L.bank_free, 1)
            if nb == 2:
                L.eng.sem_inc(L.bank_free2, 1)
            L.eng.sem_inc(m.sem("probs_turned"), 1)
            L.nth("probs_turned")
        if i > LAG and (i - LAG) % A.qts == 0:
            L.next_bank(1)
            for _ in range(A.mts - 1):
                L.next_bank(1)
    L.eng.wait_ge(m.sem("head_out"), L.nth("head_out", min(2, A.heads)))


def attention_vector(L, m, A, out):
    tiles = attention_order(A.heads, A.qts)
    n, nb = len(tiles), (A.keys + BANK - 1) // BANK
    for i in range(n + LAG + 1):
        if i < n:
            s = i % NPROB
            ps = L.next_bank(nb)
            L.eng.wait_ge(L.bank_full, L.fill)
            L.eng.tensor_reduce(m.stat[:, 8 + s:9 + s], ps[:, :A.keys], AX, ALU.max).then_inc(L.step, 1)
            L.eng.wait_ge(L.step, L.next_step())
            L.eng.tensor_scalar(m.stat[:, s:s + 1], m.stat[:, 8 + s:9 + s], -A.scale, None, ALU.mult).then_inc(m.sem("row_max"), 1)
            L.eng.wait_ge(m.sem("row_max"), L.nth("row_max"))
        if LAG <= i < n + LAG:
            L.next_bank(nb)
        if 1 <= i <= n:
            s = (i - 1) % NPROB
            L.eng.wait_ge(m.sem("exps"), L.nth("exps"))
            L.eng.reciprocal(m.stat[:, 12 + s:13 + s], m.stat[:, 4 + s:5 + s]).then_inc(L.step, 1)
            L.eng.wait_ge(L.step, L.next_step())
            L.eng.tensor_scalar(A.probs[:, s, :], A.probs[:, s, :], m.stat[:, 12 + s:13 + s], None, ALU.mult).then_inc(m.sem("probs"), 1)
            L.eng.wait_ge(m.sem("probs"), L.nth("probs"))
        if i > LAG and (i - LAG) % A.qts == 0:
            h = tiles[i - LAG - 1][0]
            for mt in range(A.mts):
                ps = L.next_bank()
                L.eng.wait_ge(L.bank_full, L.fill)
                L.eng.tensor_copy(out(h, mt), ps[0:A.vd, 0:A.qts * P]).then_inc(L.step, 1)
                L.eng.wait_ge(L.step, L.next_step())
                L.eng.sem_inc(L.bank_free, 1)
            L.eng.sem_inc(m.sem("head_out"), 1)
            L.nth("head_out")


class Attention:
    def __init__(self, m, heads, qts, keys, scale, vd, mts, at):
        self.heads, self.qts, self.keys, self.scale, self.vd, self.mts = heads, qts, keys, scale, vd, mts
        self.probs = m.at(at, NPROB, keys)
        self.turned = m.at(at + NPROB * keys, 2 * (keys // P), qts * P).rearrange("p (a b) c -> p a b c", a=2)


def swiglu_tensor(L, m, name, n, S, groups, combine=None):
    for i in range(n + 1):
        if i < n:
            L.next_slab(name, swiglu_slab(i, n, 0))
            gate_slab = L.high, L.low
            L.eng.wait_ge(m.sem("slab_split"), L.nth("slab_split"))
            L.next_slab(name, swiglu_slab(i, n, 1))
            up_slab = L.high, L.low
            L.eng.wait_ge(m.sem("slab_split"), L.nth("slab_split"))
            if i == 0:
                L.eng.wait_ge(m.sem("h_split"), L.nth("h_split", KC))
            if combine is not None:
                ps = L.next_bank()
                for bank_free, count in L.bank_frees:
                    L.eng.wait_ge(bank_free, count)
                L.eng.matmul(ps[:, :T], m.tab("ident", i, 1, parts=32).to_broadcast([32, P]), combine,
                                    start=True, stop=True).then_inc(L.bank_full, 1)
            for t in range(2):
                for lo, wd in groups:
                    for high, low in (gate_slab, up_slab):
                        ps = L.next_bank()
                        for bank_free, count in L.bank_frees:
                            L.eng.wait_ge(bank_free, count)
                        split_matmuls(L, ps[:, :wd], [
                            (high[:, k * 256 + t * P:k * 256 + (t + 1) * P], low[:, k * 256 + t * P:k * 256 + (t + 1) * P],
                             S.h_high[:, k, lo:lo + wd], S.h_low[:, k, lo:lo + wd]) for k in range(KC)]).then_inc(L.bank_full, 1)
            L.eng.drain().then_inc(m.sem("slab_used"), 1)
            L.eng.drain().then_inc(m.sem("slab_used"), 1)
        if i > 0:
            L.next_slab(name, swiglu_slab(i - 1, n, 2))
            L.eng.wait_ge(m.sem("slab_split"), L.nth("slab_split"))
            L.eng.wait_ge(m.sem("hidden"), L.nth("hidden", 2 * len(groups)))
            for c in range(KC):
                for lo, wd in groups:
                    ps = L.next_bank()
                    for bank_free, count in L.bank_frees:
                        L.eng.wait_ge(bank_free, count)
                    split_matmuls(L, ps[:, :wd], [
                        (L.high[:, k * D + c * P:k * D + (c + 1) * P], L.low[:, k * D + c * P:k * D + (c + 1) * P],
                         S.hidden_high[:, (i - 1) % 2, k, lo:lo + wd], S.hidden_low[:, (i - 1) % 2, k, lo:lo + wd])
                        for k in range(2)]).then_inc(L.bank_full, 1)
            L.eng.drain().then_inc(m.sem("slab_used"), 1)


def swiglu_scalar(L, m, name, n, gate, groups, weight=None):
    first, count = SLABS[name]
    for k in range(3):
        round_slab(L, m, first + k)
    for i in range(n + 1):
        if i < n and 3 * i + 3 < count:
            round_slab(L, m, first + 3 * i + 3)
        if i < n:
            if weight is not None:
                if i >= 2:
                    L.eng.wait_ge(m.sem("weight_used"), L.nth("weight_used"))
                ps = L.next_bank()
                L.eng.wait_ge(L.bank_full, L.fill)
                L.eng.activation(weight[:, i % 2, :], ps[:, :T], ACT.Copy).then_inc(L.step, 1)
                L.eng.wait_ge(L.step, L.next_step())
                L.eng.sem_inc(L.bank_free, 1)
                L.eng.sem_inc(m.sem("weight"), 1)
                L.nth("weight")
            for t in range(2):
                for lo, wd in groups:
                    ps = L.next_bank()
                    L.eng.wait_ge(L.bank_full, L.fill)
                    if i >= 1:
                        L.eng.wait_ge(m.sem("gate_used"), L.nth("gate_used"))
                    L.eng.activation(gate[:, t, lo:lo + wd], ps[:, :wd], ACT.Silu).then_inc(L.step, 1)
                    L.eng.wait_ge(L.step, L.next_step())
                    L.eng.sem_inc(L.bank_free, 1)
                    L.eng.sem_inc(m.sem("gate"), 1)
                    L.nth("gate")
                    L.next_bank()
            for k in range(3 * i + 4, min(3 * i + 6, count)):
                round_slab(L, m, first + k)
        if i > 0:
            for _ in range(KC * len(groups)):
                L.next_bank()
    L.eng.wait_ge(m.sem("gate_used"), L.nth("gate_used", 2 * len(groups)))
    if weight is not None:
        L.eng.wait_ge(m.sem("weight_used"), L.nth("weight_used", 2))


def swiglu_vector(L, m, n, S, groups, add, weight=None):
    gate, hidden = S.gate, S.hidden
    h = slice(0, groups[-1][0] + groups[-1][1])
    for c in range(KC):
        split_vector(L, m, S.h[:, c, h], S.h_high[:, c, h], S.h_low[:, c, h], "h_split")
    for i in range(n + 1):
        if i < n:
            if weight is not None:
                L.next_bank()
                L.eng.wait_ge(m.sem("weight"), L.nth("weight"))
            for t in range(2):
                for lo, wd in groups:
                    L.next_bank()
                    ps = L.next_bank()
                    L.eng.wait_ge(L.bank_full, L.fill)
                    L.eng.wait_ge(m.sem("gate"), L.nth("gate"))
                    o = hidden[:, i % 2, t, lo:lo + wd]
                    L.eng.tensor_tensor(o, gate[:, t, lo:lo + wd], ps[:, :wd], ALU.mult).then_inc(L.step, 1)
                    L.eng.wait_ge(L.step, L.next_step())
                    L.eng.sem_inc(L.bank_free, 1)
                    L.eng.sem_inc(m.sem("gate_used"), 1)
                    L.nth("gate_used")
                    if weight is not None:
                        L.eng.tensor_tensor(o, o, weight[:, i % 2, :], ALU.mult).then_inc(L.step, 1)
                        L.eng.wait_ge(L.step, L.next_step())
                    split_vector(L, m, o, S.hidden_high[:, i % 2, t, lo:lo + wd], S.hidden_low[:, i % 2, t, lo:lo + wd], "hidden")
            if weight is not None:
                L.eng.sem_inc(m.sem("weight_used"), 1)
                L.nth("weight_used")
        if i > 0:
            for c in range(KC):
                for g in range(len(groups)):
                    ps = L.next_bank()
                    L.eng.wait_ge(L.bank_full, L.fill)
                    add(c, g, ps).then_inc(L.step, 1)
                    L.eng.wait_ge(L.step, L.next_step())
                    L.eng.sem_inc(L.bank_free, 1)


def bcast(ap, n):
    return ap.unsqueeze(2).to_broadcast([ap.shape[0], ap.shape[1], n])


H1, MIX = 0, 4096
U0 = 8192


class Block1:

    def __init__(self, m):
        self.h = m.at(H1, KC, T)
        self.mix = m.at(MIX, KC, T)
        self.u = m.at(U0, 12, T + 2)
        self.aq = m.at(14360, 2, T)
        self.akv = m.at(15384, 1, T)
        self.kr = m.at(15896, T, parts=QK)
        self.aqn = m.at(16408, 2, T)
        self.akvn = m.at(17432, 1, T)
        self.q = m.at(17944, NH1, T, parts=QK)
        self.k = m.at(22040, NH1, T, parts=QK)
        self.v = m.at(26136, 4, HW)
        self.att = Attention(m, NH1, 4, T, QK ** -0.5, DV, 1, 28184)
        self.cos = m.at(28184, T, parts=QK)
        self.sin = m.at(28696, T, parts=QK)
        self.rot_a = m.at(1024, T, parts=QK)
        self.o = m.at(1536, 4, T)
        self.hu = m.at(14360, 12, T)
        self.vt = m.at(8192, 4, HW)
        self.x1t = m.at(10240, 4, HW)
        self.x2f = m.at(16408, 4, T)
        self.y = m.at(12288, 8, HW)
        self.dft = m.at(18456, 5248)
        self.dc = self.dft[:, 0:2048].rearrange("p (a b) -> p a b", a=4)
        self.ds = self.dft[:, 2048:4096].rearrange("p (a b) -> p a b", a=4)
        self.alt_col = self.dft[:, 4096:4224]
        self.alt_row = self.dft[:, 4224:4736]
        self.zemb = self.dft[0:33, 4736:5248]
        self.h1 = m.at(6144, T, parts=64)
        self.h2 = m.at(6656, T, parts=65)
        self.ang = m.at(7168, T, parts=64)
        self.turn = m.at(7680, T, parts=64)
        self.tmp = m.at(23704, 2, T)
        self.nyq = m.at(24728, T, parts=1)
        self.filt = m.at(25808, 4, 2048)
        self.kf = m.at(0, 8, HW)
        self.z1f = m.at(10240, 4, T)
        self.z2f = m.at(8192, 4, T)
        self.mem = m.at(4096, KC, C)
        self.hm = m.at(6144, KC, C)
        self.mk = m.at(8192, KC, C)
        self.mv = m.at(10240, 2, D)
        self.mq = m.at(12288, KC, T)
        self.mo = m.at(16384, KC, T)
        self.matt = Attention(m, MEM_H, 4, C, MEM_D ** -0.5, P, 2, 20480)
        self.logit = m.at(4096, 4, 36)
        self.cmb = m.at(4352, 4, 32)
        self.small = lambda i: m.at(4608 + 128 * i, 128)
        self.cmbt = m.at(8192, T, parts=32)
        self.gate = m.at(8704, 2, TC)
        self.hidden = m.at(10240, 4, TC).rearrange("p (a b) c -> p a b c", a=2)
        self.weight = m.at(13312, 2, T)
        self.hidden_low = m.rounded("moe_hidden_low", 10240, 2, 2, TC)
        self.hidden_high = m.rounded("moe_hidden_high", 14336, 2, 2, TC)
        self.h_low = m.rounded("moe_h_low", H1, KC, T)
        self.h_high = m.rounded("moe_h_high", 17408, KC, T)


def chunk(t, lo=0, n=None):
    return lambda c: t[:, c, lo:(t.shape[2] if n is None else lo + n)]


def gains(m, name, at=0):
    return lambda c: m.vec(name, at + c)


def mix_in_tensor(L, m, B):
    h = chunk(B.h)
    norm_tensor(L, m, h, KC)
    L.eng.wait_ge(m.sem("normed"), L.nth("normed"))
    project_tensor(L, m, "in_q", h, [(0, T)])
    w = L.next_slab("in_kv")
    L.eng.wait_ge(L.landed, L.landings)
    ps = L.next_bank()
    for bank_free, count in L.bank_frees:
        L.eng.wait_ge(bank_free, count)
    matmuls(L, ps, [(w[:, k * P:(k + 1) * P], h(k)) for k in range(KC)]).then_inc(L.bank_full, 1)
    ps = L.next_bank()
    for bank_free, count in L.bank_frees:
        L.eng.wait_ge(bank_free, count)
    matmuls(L, ps[0:QK], [(w[:, KC * P + k * QK:KC * P + (k + 1) * QK], h(k)) for k in range(KC)]).then_inc(L.bank_full, 1)
    L.eng.drain().then_inc(m.sem("slab_used"), 1)
    w = L.next_slab("in_krs")
    L.eng.wait_ge(L.landed, L.landings)
    ps = L.next_bank()
    for bank_free, count in L.bank_frees:
        L.eng.wait_ge(bank_free, count)
    matmuls(L, ps[0:QK], [(w[:, k * QK:(k + 1) * QK], h(k)) for k in range(KC)]).then_inc(L.bank_full, 1)
    L.eng.drain().then_inc(m.sem("slab_used"), 1)
    project_tensor(L, m, "in_hy", h, [(0, T)])


def mix_in_scalar(L, m, B):
    norm_scalar(L, m, chunk(m.x), chunk(B.h), KC)
    for c in range(2):
        ps = L.next_bank()
        L.eng.wait_ge(L.bank_full, L.fill)
        L.eng.activation(B.aq[:, c, :], ps, ACT.Copy).then_inc(L.step, 1)
        L.eng.wait_ge(L.step, L.next_step())
        L.eng.sem_inc(L.bank_free, 1)
    ps = L.next_bank()
    L.eng.wait_ge(L.bank_full, L.fill)
    L.eng.activation(B.akv[:, 0, :], ps, ACT.Copy).then_inc(L.step, 1)
    L.eng.wait_ge(L.step, L.next_step())
    L.eng.sem_inc(L.bank_free, 1)
    L.next_bank()
    L.next_bank()
    read_banks(L, 12, odd, lambda g, ps: L.eng.activation(B.u[:, g, 1:T + 1], ps, ACT.Copy))


def mix_in_vector(L, m, B):
    L.eng.memset(B.u[:, :, 0:1], 0.0).then_inc(L.step, 1)
    L.eng.wait_ge(L.step, L.next_step())
    L.eng.memset(B.u[:, :, T + 1:T + 2], 0.0).then_inc(L.step, 1)
    L.eng.wait_ge(L.step, L.next_step())
    norm_vector(L, m, chunk(m.x), chunk(B.h), KC, gains(m, "mix_g"))
    L.eng.sem_inc(m.sem("normed"), 1)
    L.nth("normed")
    L.next_bank()
    L.next_bank()
    L.next_bank()
    a = L.next_bank()
    L.eng.wait_ge(L.bank_full, L.fill)
    L.eng.wait_ge(m.sem("rope96"), L.nth("rope96", 16))
    L.eng.tensor_tensor(B.kr, a[0:QK], B.cos, ALU.mult).then_inc(L.step, 1)
    L.eng.wait_ge(L.step, L.next_step())
    L.eng.sem_inc(L.bank_free, 1)
    b = L.next_bank()
    L.eng.wait_ge(L.bank_full, L.fill)
    L.eng.tensor_tensor(B.q[:, 0, :], b[0:QK], B.sin, ALU.mult).then_inc(L.step, 1)
    L.eng.wait_ge(L.step, L.next_step())
    L.eng.sem_inc(L.bank_free, 1)
    L.eng.tensor_tensor(B.kr, B.kr, B.q[:, 0, :], ALU.add).then_inc(L.step, 1)
    L.eng.wait_ge(L.step, L.next_step())
    read_banks(L, 12, even, lambda g, ps: L.eng.tensor_copy(B.u[:, g, 1:T + 1], ps))


def latent_tensor(L, m, B):
    norm_tensor(L, m, chunk(B.aqn), 2)
    norm_tensor(L, m, chunk(B.akvn), 1)
    L.eng.wait_ge(m.sem("normed"), L.nth("normed", 2))
    w = L.next_slab("uq")
    L.eng.wait_ge(L.landed, L.landings)
    ws = L.next_slab("uqs")
    L.eng.wait_ge(L.landed, L.landings)
    for h in range(NH1):
        for a in (w, ws):
            ps = L.next_bank()
            for bank_free, count in L.bank_frees:
                L.eng.wait_ge(bank_free, count)
            matmuls(L, ps[0:QK], [(a[:, k * NH1 * QK + h * QK:k * NH1 * QK + (h + 1) * QK], B.aqn[:, k, :])
                                         for k in range(2)]).then_inc(L.bank_full, 1)
    L.eng.drain().then_inc(m.sem("slab_used"), 1)
    L.eng.drain().then_inc(m.sem("slab_used"), 1)
    w = L.next_slab("ukv")
    L.eng.wait_ge(L.landed, L.landings)
    for h in range(NH1):
        ps = L.next_bank()
        for bank_free, count in L.bank_frees:
            L.eng.wait_ge(bank_free, count)
        matmuls(L, ps[0:NOPE], [(w[:, h * NOPE:(h + 1) * NOPE], B.akvn[:, 0, :])]).then_inc(L.bank_full, 1)
    for t in range(4):
        ps = L.next_bank()
        for bank_free, count in L.bank_frees:
            L.eng.wait_ge(bank_free, count)
        matmuls(L, ps, [(B.akvn[:, 0, t * P:(t + 1) * P], w[:, 512:1024])]).then_inc(L.bank_full, 1)
    L.eng.drain().then_inc(m.sem("slab_used"), 1)


def latent_scalar(L, m, B):
    norm_scalar(L, m, chunk(B.aq), chunk(B.aqn), 2)
    L.eng.wait_ge(m.sem("root_used"), L.nth("root_used"))
    norm_scalar(L, m, chunk(B.akv), chunk(B.akvn), 1)
    for h in range(NH1):
        L.next_bank()
        L.next_bank()
    for h in range(NH1):
        ps = L.next_bank()
        L.eng.wait_ge(L.bank_full, L.fill)
        L.eng.activation(B.k[0:NOPE, h, :], ps[0:NOPE], ACT.Copy).then_inc(L.step, 1)
        L.eng.wait_ge(L.step, L.next_step())
        L.eng.sem_inc(L.bank_free, 1)
        L.eng.activation(B.k[NOPE:QK, h, :], B.kr[NOPE:QK], ACT.Copy).then_inc(L.step, 1)
        L.eng.wait_ge(L.step, L.next_step())
    for t in range(4):
        ps = L.next_bank()
        L.eng.wait_ge(L.bank_full, L.fill)
        L.eng.activation(B.v[:, t, :], ps, ACT.Copy).then_inc(L.step, 1)
        L.eng.wait_ge(L.step, L.next_step())
        L.eng.sem_inc(L.bank_free, 1)


def latent_vector(L, m, B):
    norm_vector(L, m, chunk(B.aq), chunk(B.aqn), 2, gains(m, "qn_g"))
    L.eng.sem_inc(m.sem("normed"), 1)
    L.nth("normed")
    L.eng.sem_inc(m.sem("root_used"), 1)
    L.nth("root_used")
    norm_vector(L, m, chunk(B.akv), chunk(B.akvn), 1, gains(m, "kvn_g"))
    L.eng.sem_inc(m.sem("normed"), 1)
    L.nth("normed")
    for h in range(NH1):
        ps = L.next_bank()
        L.eng.wait_ge(L.bank_full, L.fill)
        L.eng.tensor_tensor(B.q[:, h, :], ps[0:QK], B.cos, ALU.mult).then_inc(L.step, 1)
        L.eng.wait_ge(L.step, L.next_step())
        L.eng.sem_inc(L.bank_free, 1)
        ps = L.next_bank()
        L.eng.wait_ge(L.bank_full, L.fill)
        L.eng.tensor_tensor(B.rot_a, ps[0:QK], B.sin, ALU.mult).then_inc(L.step, 1)
        L.eng.wait_ge(L.step, L.next_step())
        L.eng.sem_inc(L.bank_free, 1)
        L.eng.tensor_tensor(B.q[:, h, :], B.q[:, h, :], B.rot_a, ALU.add).then_inc(L.step, 1)
        L.eng.wait_ge(L.step, L.next_step())
    for _ in range(NH1 + 4):
        L.next_bank()


def latent_attention_tensor(L, m, B):
    def score(ps, h, q):
        return matmuls(L, ps, [(B.q[:, h, q * P:(q + 1) * P], B.k[:, h, :])])
    attention_tensor(L, m, B.att, score, lambda h, kt, mt: B.v[:, kt, h * DV:(h + 1) * DV])


def latent_attention_vector(L, m, B):
    attention_vector(L, m, B.att, lambda h, mt: B.o[64 * (h % 2):64 * (h % 2) + 64, h // 2, :])


def conv_vector(L, m, B):
    for c in range(12):
        o, u = B.hu[:, c, :], B.u[:, c, :]
        L.eng.tensor_scalar(o, u[:, 0:T], m.vec("conv_w", c), m.vec("conv_b", c), ALU.mult, ALU.add).then_inc(L.step, 1)
        L.eng.wait_ge(L.step, L.next_step())
        L.eng.scalar_tensor_tensor(o, u[:, 1:T + 1], m.vec("conv_w", 12 + c), o, ALU.mult, ALU.add).then_inc(L.step, 1)
        L.eng.wait_ge(L.step, L.next_step())
        L.eng.scalar_tensor_tensor(o, u[:, 2:T + 2], m.vec("conv_w", 24 + c), o, ALU.mult, ALU.add).then_inc(L.step, 1)
        L.eng.wait_ge(L.step, L.next_step())


def turn_tensor(L, m, src, dst_chunks):
    for d in range(dst_chunks):
        ps = L.next_bank()
        for bank_free, count in L.bank_frees:
            L.eng.wait_ge(bank_free, count)
        for i in range(4):
            last = L.eng.transpose(ps[:, i * P:(i + 1) * P], src(d, i), m.tab("ident"))
        last.then_inc(L.bank_full, 1)


def conv_turn_tensor(L, m, B):
    for first in (8, 0):
        turn_tensor(L, m, lambda d, i: B.hu[:, first + i, d * P:(d + 1) * P], 4)


def conv_turn_scalar(L, m, B):
    read_banks(L, 8, always, lambda g, ps: L.eng.activation((B.vt, B.x1t)[g // 4][:, g % 4, :], ps, ACT.Copy))


def filter_tensor(L, m, B):
    L.eng.wait_ge(m.sem("dft_landed"), L.nth("dft_landed", 16))
    ps = L.next_bank()
    for bank_free, count in L.bank_frees:
        L.eng.wait_ge(bank_free, count)
    matmuls(L, ps[0:64], [(m.vec("hw1", 0, 64, parts=33), B.zemb)]).then_inc(L.bank_full, 1)
    L.eng.wait_ge(m.sem("sine"), L.nth("sine"))
    ps = L.next_bank()
    for bank_free, count in L.bank_frees:
        L.eng.wait_ge(bank_free, count)
    matmuls(L, ps[0:64], [(m.vec("hw2", 0, 64, parts=64), B.h1)]).then_inc(L.bank_full, 1)
    L.eng.wait_ge(m.sem("sine"), L.nth("sine"))
    L.next_slab("decay")
    L.eng.wait_ge(L.landed, L.landings)
    w = L.next_slab("hw3")
    L.eng.wait_ge(L.landed, L.landings)
    L.next_slab("skip0")
    L.eng.wait_ge(L.landed, L.landings)
    for q in range(4):
        for t in range(4):
            ps = L.next_bank()
            for bank_free, count in L.bank_frees:
                L.eng.wait_ge(bank_free, count)
            matmuls(L, ps, [(B.h2[:, t * P:(t + 1) * P], w[0:65, q * HW:(q + 1) * HW])]).then_inc(L.bank_full, 1)


def filter_vector(L, m, B):
    L.eng.memset(B.h2[64:65], 1.0).then_inc(L.step, 1)
    L.eng.wait_ge(L.step, L.next_step())
    for b, f in (("hb1", "hf0"), ("hb2", "hf1")):
        ps = L.next_bank()
        L.eng.wait_ge(L.bank_full, L.fill)
        L.eng.tensor_scalar(B.ang, ps[0:64], m.vec(b, parts=64), m.vec(f, parts=64), ALU.add, ALU.mult).then_inc(L.step, 1)
        L.eng.wait_ge(L.step, L.next_step())
        L.eng.sem_inc(L.bank_free, 1)
        L.eng.tensor_scalar(B.turn, B.ang, float(1 / (2 * np.pi)), 12582912.0, ALU.mult, ALU.add).then_inc(L.step, 1)
        L.eng.wait_ge(L.step, L.next_step())
        L.eng.tensor_scalar(B.turn, B.turn, -12582912.0, None, ALU.add).then_inc(L.step, 1)
        L.eng.wait_ge(L.step, L.next_step())
        L.eng.scalar_tensor_tensor(B.ang, B.turn, -6.28125, B.ang, ALU.mult, ALU.add).then_inc(L.step, 1)
        L.eng.wait_ge(L.step, L.next_step())
        L.eng.scalar_tensor_tensor(B.ang, B.turn, -0.0019353071795864769, B.ang, ALU.mult, ALU.add).then_inc(L.step, 1)
        L.eng.wait_ge(L.step, L.next_step())
        L.eng.tensor_scalar(B.ang, B.ang, 3.1415925, -3.1415925, ALU.min, ALU.max).then_inc(m.sem("angle"), 1)
        L.eng.wait_ge(m.sem("angle"), L.nth("angle"))
    for q in range(4):
        for t in range(4):
            ps = L.next_bank()
            L.eng.wait_ge(L.bank_full, L.fill)
            L.eng.wait_ge(m.sem("window"), L.nth("window"))
            L.eng.tensor_tensor(B.filt[:, t, q * HW:(q + 1) * HW], ps, B.tmp[:, t % 2, :], ALU.mult).then_inc(L.step, 1)
            L.eng.wait_ge(L.step, L.next_step())
            L.eng.sem_inc(L.bank_free, 1)
            L.eng.sem_inc(m.sem("window_used"), 1)
            L.nth("window_used")
    for q in (1, 3):
        L.eng.memset(B.filt[0:1, 0, q * HW:(q + 1) * HW], 0.0).then_inc(L.step, 1)
        L.eng.wait_ge(L.step, L.next_step())


def filter_scalar(L, m, B):
    L.next_bank()
    L.eng.wait_ge(m.sem("angle"), L.nth("angle"))
    L.eng.activation(B.h1, B.ang, ACT.Sin).then_inc(m.sem("sine"), 1)
    L.eng.wait_ge(m.sem("sine"), L.nth("sine"))
    L.next_bank()
    L.eng.wait_ge(m.sem("angle"), L.nth("angle"))
    L.eng.activation(B.h2[0:64], B.ang, ACT.Sin).then_inc(m.sem("sine"), 1)
    L.eng.wait_ge(m.sem("sine"), L.nth("sine"))
    dec = m.slab_of(L, "decay")
    L.eng.activation(dec, dec, ACT.Abs).then_inc(L.step, 1)
    L.eng.wait_ge(L.step, L.next_step())
    n = 0
    for q in range(4):
        for t in range(4):
            L.next_bank()
            if n >= 2:
                L.eng.wait_ge(m.sem("window_used"), L.nth("window_used"))
            L.eng.activation(B.tmp[:, t % 2, :], dec[:, q * HW:(q + 1) * HW], ACT.Exp, scale=m.tab("t01", t, 1)).then_inc(m.sem("window"), 1)
            L.eng.wait_ge(m.sem("window"), L.nth("window"))
            n += 1
    L.eng.wait_ge(m.sem("window_used"), L.nth("window_used", 2))


def parts_vector(L, m, B, order):
    f, b = [B.filt[:, :, (2 * order + d) * HW:(2 * order + d + 1) * HW] for d in (0, 1)]
    e = B.y[:, 0:4, :]
    L.eng.tensor_tensor(e, f, b, ALU.add).then_inc(L.step, 1)
    L.eng.wait_ge(L.step, L.next_step())
    L.eng.tensor_tensor(f, f, b, ALU.subtract).then_inc(L.step, 1)
    L.eng.wait_ge(L.step, L.next_step())


def spectrum_tensor(L, m, B, even_part, odd_part, pairs):
    order = [(f, s) for f in range(4) for s in (0, 1)] if pairs else [(f, s) for s in (0, 1) for f in range(4)]
    for f, s in order:
        ps = L.next_bank()
        for bank_free, count in L.bank_frees:
            L.eng.wait_ge(bank_free, count)
        if s == 0:
            ops = [(B.dc[:, t, f * P:(f + 1) * P], even_part(t)) for t in range(4)]
        else:
            ops = [(B.ds[:, t, f * P:(f + 1) * P], odd_part(t)) for t in range(4)]
            if f == 0:
                ops += [(B.alt_col, even_part(t)) for t in range(4)]
        matmuls(L, ps, ops).then_inc(L.bank_full, 1)


def filter_spectrum_tensor(L, m, B, order):
    spectrum_tensor(L, m, B, lambda t: B.y[:, t, :], lambda t: B.filt[:, t, 2 * order * HW:(2 * order + 1) * HW], False)


def filter_spectrum_scalar(L, m, B):
    read_banks(L, 8, always, lambda g, ps: L.eng.activation(
        B.kf[:, g, :], ps, ACT.Copy, scale=m.tab("dft_scale", 0 if g % 4 == 0 else 1, 1)))


def product_tensor(L, m, B):
    spectrum_tensor(L, m, B, lambda t: B.vt[:, t, :], lambda t: B.vt[:, t, :], True)


def product_vector(L, m, B):
    for f in range(4):
        re, im, kr, ki = B.y[:, f, :], B.y[:, 4 + f, :], B.kf[:, f, :], B.kf[:, 4 + f, :]
        t1, t2 = B.tmp[:, 0, :], B.tmp[:, 1, :]
        zr = L.next_bank()
        L.eng.wait_ge(L.bank_full, L.fill)
        zr_free = L.bank_free
        zi = L.next_bank()
        L.eng.wait_ge(L.bank_full, L.fill)
        L.eng.tensor_tensor(re, zr, kr, ALU.mult).then_inc(L.step, 1)
        L.eng.wait_ge(L.step, L.next_step())
        L.eng.tensor_tensor(im, zr, ki, ALU.mult).then_inc(L.step, 1)
        L.eng.wait_ge(L.step, L.next_step())
        L.eng.sem_inc(zr_free, 1)
        L.eng.tensor_tensor(t1, zi, ki, ALU.mult).then_inc(L.step, 1)
        L.eng.wait_ge(L.step, L.next_step())
        L.eng.tensor_tensor(t2, zi, kr, ALU.mult).then_inc(L.step, 1)
        L.eng.wait_ge(L.step, L.next_step())
        L.eng.sem_inc(L.bank_free, 1)
        if f == 0:
            L.eng.tensor_copy(B.nyq, t1[0:1]).then_inc(L.step, 1)
            L.eng.wait_ge(L.step, L.next_step())
            L.eng.memset(t1[0:1], 0.0).then_inc(L.step, 1)
            L.eng.wait_ge(L.step, L.next_step())
        L.eng.tensor_tensor(re, re, t1, ALU.subtract).then_inc(L.step, 1)
        L.eng.wait_ge(L.step, L.next_step())
        L.eng.tensor_tensor(im, im, t2, ALU.add).then_inc(L.step, 1)
        L.eng.wait_ge(L.step, L.next_step())
        if f == 0:
            L.eng.tensor_copy(im[0:1], B.nyq).then_inc(L.step, 1)
            L.eng.wait_ge(L.step, L.next_step())


def inverse0_tensor(L, m, B):
    for t in range(4):
        s = slice(t * P, (t + 1) * P)
        ps = L.next_bank()
        for bank_free, count in L.bank_frees:
            L.eng.wait_ge(bank_free, count)
        matmuls(L, ps, [(B.dc[:, f, s], B.y[:, f, :]) for f in range(4)] +
                       [(B.ds[:, f, s], B.y[:, 4 + f, :]) for f in range(4)] + [(B.alt_row[:, s], B.y[:, 4, :])]).then_inc(L.bank_full, 1)


def inverse0_vector(L, m, B):
    skip = m.slab_of(L, "skip0")[:, 0:HW]
    for t in range(4):
        t1 = B.tmp[:, 0, :]
        L.eng.tensor_tensor(t1, B.vt[:, t, :], skip, ALU.mult).then_inc(L.step, 1)
        L.eng.wait_ge(L.step, L.next_step())
        ps = L.next_bank()
        L.eng.wait_ge(L.bank_full, L.fill)
        L.eng.tensor_tensor(t1, t1, ps, ALU.add).then_inc(L.step, 1)
        L.eng.wait_ge(L.step, L.next_step())
        L.eng.sem_inc(L.bank_free, 1)
        L.eng.tensor_tensor(B.vt[:, t, :], t1, B.x1t[:, t, :], ALU.mult).then_inc(L.step, 1)
        L.eng.wait_ge(L.step, L.next_step())


def inverse1_tensor(L, m, B):
    for c in range(4):
        s = slice(c * P, (c + 1) * P)
        ps = L.next_bank()
        for bank_free, count in L.bank_frees:
            L.eng.wait_ge(bank_free, count)
        matmuls(L, ps, [(B.y[:, f, s], B.dc[:, f, :]) for f in range(4)] +
                       [(B.y[:, 4 + f, s], B.ds[:, f, :]) for f in range(4)] + [(B.y[:, 4, s], B.alt_row)]).then_inc(L.bank_full, 1)


def inverse1_vector(L, m, B):
    for c in range(4):
        t1 = B.tmp[:, 0, :]
        ps = L.next_bank()
        L.eng.wait_ge(L.bank_full, L.fill)
        L.eng.scalar_tensor_tensor(t1, B.z1f[:, c, :], m.vec("skip1", c), ps, ALU.mult, ALU.add).then_inc(L.step, 1)
        L.eng.wait_ge(L.step, L.next_step())
        L.eng.sem_inc(L.bank_free, 1)
        L.eng.tensor_tensor(B.z2f[:, c, :], t1, B.x2f[:, c, :], ALU.mult).then_inc(L.step, 1)
        L.eng.wait_ge(L.step, L.next_step())


def add_to_x(L, m, col=None, lo=0, w=T):
    def fn(c, ps):
        o = m.x[:, c, :]
        if col is None:
            return L.eng.tensor_tensor(o, o, ps[:, :w], ALU.add)
        return L.eng.scalar_tensor_tensor(o, ps[:, :w], col(c), o, ALU.mult, ALU.add)
    return fn


def memory_tensor(L, m, B):
    norm_tensor(L, m, chunk(B.hm), KC)
    L.eng.wait_ge(m.sem("normed"), L.nth("normed"))
    project_tensor(L, m, "mk", chunk(B.hm), [(0, C)])
    for i in range(4):
        w = L.next_slab("mv", i)
        L.eng.wait_ge(L.landed, L.landings)
        for t in range(2):
            ps = L.next_bank()
            for bank_free, count in L.bank_frees:
                L.eng.wait_ge(bank_free, count)
            matmuls(L, ps[:, :256], [(B.hm[:, k, t * P:(t + 1) * P], w[:, k * 256:(k + 1) * 256]) for k in range(KC)]).then_inc(L.bank_full, 1)
        L.eng.drain().then_inc(m.sem("slab_used"), 1)
    norm_tensor(L, m, chunk(B.h), KC)
    L.eng.wait_ge(m.sem("normed"), L.nth("normed"))
    project_tensor(L, m, "mq", chunk(B.h), [(0, T)])


def memory_scalar(L, m, B):
    L.eng.wait_ge(m.sem("mem_landed"), L.nth("mem_landed", 16))
    norm_scalar(L, m, chunk(B.mem), chunk(B.hm), KC)
    read_banks(L, 8, odd, lambda g, ps: L.eng.activation(B.mk[:, g, :], ps[:, :C], ACT.Copy))
    read_banks(L, 8, odd, lambda g, ps: L.eng.activation(
        B.mv[:, g % 2, g // 2 * 256:g // 2 * 256 + 256], ps[:, :256], ACT.Copy))
    L.eng.wait_ge(m.sem("root_used"), L.nth("root_used"))
    norm_scalar(L, m, chunk(m.x), chunk(B.h), KC)
    read_banks(L, 8, odd, lambda g, ps: L.eng.activation(B.mq[:, g, :], ps, ACT.Copy))


def memory_vector(L, m, B):
    norm_vector(L, m, chunk(B.mem), chunk(B.hm), KC, gains(m, "mem_g"))
    L.eng.sem_inc(m.sem("normed"), 1)
    L.nth("normed")
    L.eng.sem_inc(m.sem("root_used"), 1)
    L.nth("root_used")
    read_banks(L, 8, even, lambda g, ps: L.eng.tensor_copy(B.mk[:, g, :], ps[:, :C]))
    read_banks(L, 8, even, lambda g, ps: L.eng.tensor_copy(
        B.mv[:, g % 2, g // 2 * 256:g // 2 * 256 + 256], ps[:, :256]))
    norm_vector(L, m, chunk(m.x), chunk(B.h), KC, gains(m, "cross_g"))
    L.eng.sem_inc(m.sem("normed"), 1)
    L.nth("normed")
    read_banks(L, 8, even, lambda g, ps: L.eng.tensor_copy(B.mq[:, g, :], ps))


def memory_attention_tensor(L, m, B):
    def score(ps, h, q):
        return matmuls(L, ps[:, :C], [(B.mq[:, 2 * h + k, q * P:(q + 1) * P], B.mk[:, 2 * h + k, :]) for k in range(2)])
    attention_tensor(L, m, B.matt, score,
                     lambda h, kt, mt: B.mv[:, kt, h * MEM_D + mt * P:h * MEM_D + (mt + 1) * P])


def route_tensor(L, m, B):
    norm_tensor(L, m, chunk(B.h), KC)
    L.eng.wait_ge(m.sem("normed"), L.nth("normed"))
    w = L.next_slab("route")
    L.eng.wait_ge(L.landed, L.landings)
    ps = L.next_bank()
    for bank_free, count in L.bank_frees:
        L.eng.wait_ge(bank_free, count)
    for t in range(4):
        last = matmuls(L, ps[:, t * 36:(t + 1) * 36], [(B.h[:, k, t * P:(t + 1) * P], w[:, k * 36:(k + 1) * 36])
                                                       for k in range(KC)])
    last.then_inc(L.bank_full, 1)
    L.eng.drain().then_inc(m.sem("slab_used"), 1)
    L.eng.wait_ge(m.sem("combined"), L.nth("combined"))
    ps = L.next_bank()
    for bank_free, count in L.bank_frees:
        L.eng.wait_ge(bank_free, count)
    for t in range(4):
        last = L.eng.transpose(ps[0:32, t * P:(t + 1) * P], B.cmb[:, t, :], m.tab("ident"))
    last.then_inc(L.bank_full, 1)


def route_scalar(L, m, B):
    norm_scalar(L, m, chunk(m.x), chunk(B.h), KC)
    L.next_bank()
    for i in range(2):
        L.eng.wait_ge(m.sem("gap"), L.nth("gap"))
        s = B.small(i)
        L.eng.activation(s[:, 0:16], s[:, 0:16], ACT.Exp).then_inc(m.sem("gap_exp"), 1)
        L.eng.wait_ge(m.sem("gap_exp"), L.nth("gap_exp"))
    ps = L.next_bank()
    L.eng.wait_ge(L.bank_full, L.fill)
    L.eng.activation(B.cmbt, ps[0:32], ACT.Copy).then_inc(L.step, 1)
    L.eng.wait_ge(L.step, L.next_step())
    L.eng.sem_inc(L.bank_free, 1)


def first_best(L, m, v, best, hot, tmp, n):
    a = v.shape[1]
    rank = m.tab("expert_rank", 0, n).unsqueeze(1).to_broadcast([P, a, n])
    L.eng.tensor_reduce(best, v, AX, ALU.max).then_inc(L.step, 1)
    L.eng.wait_ge(L.step, L.next_step())
    L.eng.tensor_tensor(hot, v, bcast(best, n), ALU.is_equal).then_inc(L.step, 1)
    L.eng.wait_ge(L.step, L.next_step())
    L.eng.tensor_tensor(hot, hot, rank, ALU.mult).then_inc(L.step, 1)
    L.eng.wait_ge(L.step, L.next_step())
    L.eng.tensor_reduce(tmp, hot, AX, ALU.max).then_inc(L.step, 1)
    L.eng.wait_ge(L.step, L.next_step())
    L.eng.tensor_tensor(hot, hot, bcast(tmp, n), ALU.is_equal).then_inc(L.step, 1)
    L.eng.wait_ge(L.step, L.next_step())


def route_vector(L, m, B):
    norm_vector(L, m, chunk(m.x), chunk(B.h), KC, gains(m, "ffn_g"))
    L.eng.sem_inc(m.sem("normed"), 1)
    L.nth("normed")
    ps = L.next_bank()
    L.eng.wait_ge(L.bank_full, L.fill)
    e = L.eng
    e.tensor_tensor(B.logit, ps[:, :144].rearrange("p (a b) -> p a b", a=4),
                         m.vec("b_route", 0, 36).unsqueeze(1).to_broadcast([P, 4, 36]), ALU.add).then_inc(L.step, 1)
    L.eng.wait_ge(L.step, L.next_step())
    L.eng.sem_inc(L.bank_free, 1)
    gap, x = B.small(0)[:, 0:16], B.small(1)[:, 0:16]
    s2, s3 = B.small(2), B.small(3)
    g = B.logit[:, :, 0:4]
    ghot = B.small(4)[:, 0:16].rearrange("p (a b) -> p a b", a=4)
    gmax, tmp4, pg, tmp16 = s2[:, 0:4], s2[:, 4:8], s2[:, 8:12], s2[:, 16:32]
    first_best(L, m, g, gmax, ghot, tmp4, 4)
    gap3 = gap.rearrange("p (a b) -> p a b", a=4)
    e.tensor_tensor(gap3, g, bcast(gmax, 4), ALU.subtract).then_inc(m.sem("gap"), 1)
    L.eng.wait_ge(m.sem("gap"), L.nth("gap"))
    L.eng.wait_ge(m.sem("gap_exp"), L.nth("gap_exp"))
    e.tensor_reduce(pg, gap3, AX, ALU.add).then_inc(L.step, 1)
    L.eng.wait_ge(L.step, L.next_step())
    e.reciprocal(pg, pg).then_inc(L.step, 1)
    L.eng.wait_ge(L.step, L.next_step())
    e.tensor_tensor(ghot, ghot, bcast(pg, 4), ALU.mult).then_inc(L.step, 1)
    L.eng.wait_ge(L.step, L.next_step())
    ex, hot1, hot2 = [B.small(i).rearrange("p (a b) -> p a b", a=16) for i in (5, 6, 7)]
    e.tensor_copy(B.small(5).rearrange("p (a b) -> p a b", a=4), B.logit[:, :, 4:36]).then_inc(L.step, 1)
    L.eng.wait_ge(L.step, L.next_step())
    b1, b2 = s3[:, 0:16], s3[:, 16:32]
    first_best(L, m, ex, b1, hot1, tmp16, 8)
    e.scalar_tensor_tensor(ex, hot1, -1e30, ex, ALU.mult, ALU.add).then_inc(L.step, 1)
    L.eng.wait_ge(L.step, L.next_step())
    first_best(L, m, ex, b2, hot2, tmp16, 8)
    e.tensor_tensor(x, b2, b1, ALU.subtract).then_inc(m.sem("gap"), 1)
    L.eng.wait_ge(m.sem("gap"), L.nth("gap"))
    L.eng.wait_ge(m.sem("gap_exp"), L.nth("gap_exp"))
    p1 = s3[:, 32:48]
    e.tensor_scalar(p1, x, 1.0, None, ALU.add).then_inc(L.step, 1)
    L.eng.wait_ge(L.step, L.next_step())
    e.reciprocal(p1, p1).then_inc(L.step, 1)
    L.eng.wait_ge(L.step, L.next_step())
    e.tensor_tensor(p1, p1, ghot.rearrange("p a b -> p (a b)"), ALU.mult).then_inc(L.step, 1)
    L.eng.wait_ge(L.step, L.next_step())
    e.tensor_tensor(x, x, p1, ALU.mult).then_inc(L.step, 1)
    L.eng.wait_ge(L.step, L.next_step())
    e.tensor_tensor(hot1, hot1, bcast(p1, 8), ALU.mult).then_inc(L.step, 1)
    L.eng.wait_ge(L.step, L.next_step())
    e.tensor_tensor(hot2, hot2, bcast(x, 8), ALU.mult).then_inc(L.step, 1)
    L.eng.wait_ge(L.step, L.next_step())
    c = B.cmb.rearrange("p a (b c) -> p (a b) c", b=4)
    e.tensor_tensor(c, hot1, hot2, ALU.add).then_inc(m.sem("combined"), 1)
    L.eng.wait_ge(m.sem("combined"), L.nth("combined"))
    L.next_bank()


BOTH = [NX, NC_]
XCH, ALLCH = T // CH, TC // CH
MASK = {"before": (0, 1), "upto": (2, 3)}


class Block2:

    def __init__(self, m):
        self.h = m.at(0, KC, TC)
        self.q = m.at(6144, KC, TC)
        self.k = m.at(12288, 4, TC)
        self.v = m.at(15360, 6, 256)
        self.att = Attention(m, QH, 4, TC, HD ** -0.5, HD, 1, 16896)
        self.catt = Attention(m, QH, 2, C, HD ** -0.5, HD, 1, 16896)
        self.o = m.at(25344, KC, TC)
        self.rope = m.at(31488, 2, T)
        self.sq = m.at(0, 2, TC)
        self.root2 = m.at(1536, 2, TC)
        self.rot = m.at(3072, T)
        self.gate = m.at(6144, 2, TC)
        self.hidden = m.at(7680, 4, TC).rearrange("p (a b) c -> p a b c", a=2)
        self.hidden_low = m.rounded("ffn_hidden_low", 7680, 2, 2, TC)
        self.hidden_high = m.rounded("ffn_hidden_high", 10752, 2, 2, TC)
        self.h_low = m.rounded("h_low", 0, KC, TC)
        self.h_high = m.rounded("h_high", 13824, KC, TC)
        self.xx = m.at(6144, KC, TC)
        self.lp = m.at(12288, KC, TC)
        self.pk = m.at(18432, KC, TC)
        self.pv = m.at(24576, KC, TC)
        self.pr = m.at(18432, KC, T)
        self.tw = m.at(30720, TC)
        self.ta = m.at(31488, TC)
        self.tg = m.at(32256, T)
        self.out = m.at(26624, KC, T)
        self.load = [m.at(2048 * i, 2048) for i in range(2)]
        at = [4096]

        def new(n=TC, back=0):
            at[0] += n
            return m.at(at[0] - n, n)

        self.kk, self.kd, self.bk = new(), new(), new(T)
        self.al, self.be, self.ka, self.rh = new(), new(), new(), new()
        self.vtok, self.altok, self.betok, self.katok = new(), new(), new(), new()
        low = at[0]
        self.t1, self.t2, self.lw, self.a, self.b, self.ci, self.cm = [new() for _ in range(7)]
        at[0] = low
        self.nt, self.ti, self.tt, self.x, self.akt, self.rbt, self.rkt = [new() for _ in range(7)]
        self.akv, self.ua, self.uv = new(), new(), new()
        self.rp, self.yj = new(T), new(T)
        self.mt, self.g, self.s = new(), new(), new()
        self.masks = new(16 * CH)
        self.eye = new(CH)
        self.keep = new()
        assert self.keep.shape[1] == TC and at[0] <= 26624, at


def mod_tensor(L, m, i):
    if i == 0:
        L.eng.wait_ge(m.sem("cond"), L.nth("cond"))
    ps = L.next_bank()
    for bank_free, count in L.bank_frees:
        L.eng.wait_ge(bank_free, count)
    for s in range(24):
        w = L.next_slab(f"mod{i}", s)
        L.eng.wait_ge(L.landed, L.landings)
        for t in range(2):
            c = 2 * (2 * s + t)
            last = matmuls(L, ps[:, c:c + 2], [(w[:, k * 256 + t * P:k * 256 + (t + 1) * P], m.cond[:, 2 * k:2 * k + 2])
                                               for k in range(KC)])
        if s == 23:
            last.then_inc(L.bank_full, 1)
        L.eng.drain().then_inc(m.sem("slab_used"), 1)


def mod_scalar(L, m, i):
    if i == 0:
        L.eng.activation(m.cond, m.vec("cond", 0, 16), ACT.Silu).then_inc(m.sem("cond"), 1)
        L.eng.wait_ge(m.sem("cond"), L.nth("cond"))
    L.next_bank()


def mod_vector(L, m, i):
    ps = L.next_bank()
    L.eng.wait_ge(L.bank_full, L.fill)
    mod = m.mod.rearrange("p (a b) -> p a b", b=2)
    L.eng.tensor_tensor(mod, ps[:, :96].rearrange("p (a b) -> p a b", b=2), bcast(m.vec("mod_b", 48 * i, 48), 2), ALU.add).then_inc(L.step, 1)
    L.eng.wait_ge(L.step, L.next_step())
    L.eng.sem_inc(L.bank_free, 1)
    for n, g in ((0, "n1_g"), (1, "n2_g")):
        src = mod[:, 8 * (3 * n + 1):8 * (3 * n + 2), :]
        dst = m.modg[:, 16 * n:16 * n + 16].rearrange("p (a b) -> p a b", b=2)
        L.eng.tensor_scalar(dst, src, 1.0, None, ALU.add).then_inc(L.step, 1)
        L.eng.wait_ge(L.step, L.next_step())
        L.eng.tensor_tensor(dst, dst, bcast(m.vec(g, 8 * i, 8), 2), ALU.mult).then_inc(L.step, 1)
        L.eng.wait_ge(L.step, L.next_step())


def mod_col(m, part, w):
    return lambda c: m.mod[:, 2 * (8 * part + c) + w:2 * (8 * part + c) + w + 1]


def modnorm_tensor(L, m, B, ctx=True):
    norm_tensor(L, m, chunk(B.h, 0, T), KC)
    if ctx:
        norm_tensor(L, m, chunk(B.h, T, C), KC)


def modnorm_scalar(L, m, B, ctx=True):
    norm_scalar(L, m, chunk(m.x), chunk(B.h, 0, T), KC)
    if ctx:
        L.eng.wait_ge(m.sem("root_used"), L.nth("root_used"))
        norm_scalar(L, m, chunk(m.xc), chunk(B.h, T, C), KC)


def modnorm_vector(L, m, B, n, ctx=True):
    for w, x in enumerate((m.x, m.xc)[:1 + ctx]):
        norm_vector(L, m, chunk(x), chunk(B.h, *BOTH[w]), KC,
                    lambda c: m.modg[:, 16 * n + 2 * c + w:16 * n + 2 * c + w + 1], mod_col(m, 3 * n, w))
        if w == 0 and ctx:
            L.eng.sem_inc(m.sem("root_used"), 1)
            L.nth("root_used")


def qkv_tensor(L, m, B):
    h = chunk(B.h)
    project_tensor(L, m, "qkv_q", h, BOTH)
    project_tensor(L, m, "qkv_k", h, BOTH)
    w = L.next_slab("qkv_v")
    L.eng.wait_ge(L.landed, L.landings)
    for t in range(6):
        ps = L.next_bank()
        for bank_free, count in L.bank_frees:
            L.eng.wait_ge(bank_free, count)
        matmuls(L, ps[:, :256], [(B.h[:, k, t * P:(t + 1) * P], w[:, k * 256:(k + 1) * 256]) for k in range(KC)]).then_inc(L.bank_full, 1)
    L.eng.drain().then_inc(m.sem("slab_used"), 1)


def qkv_read(L, m, B, mine, copy):
    def fn(g, ps):
        lo, w = BOTH[g % 2]
        c = g // 2
        return copy((B.q[:, c] if c < 8 else B.k[:, c - 8])[:, lo:lo + w], ps[:, :w])
    read_banks(L, 24, mine, fn)
    read_banks(L, 6, mine, lambda g, ps: copy(B.v[:, g, :], ps[:, :256]))


def head_chunks(B):
    return [B.q[:, c, :] for c in range(8)] + [B.k[:, c, :] for c in range(4)]


def head_norm_tensor(L, m, B):
    ch = head_chunks(B)
    for i in range(13):
        if i < 12:
            L.eng.wait_ge(m.sem("squares"), L.nth("squares"))
            ps = L.next_bank(2)
            for bank_free, count in L.bank_frees:
                L.eng.wait_ge(bank_free, count)
            for lo, w in BOTH:
                last = L.eng.matmul(ps[:, lo:lo + w], m.tab("heads64"), B.sq[:, i % 2, lo:lo + w], start=True, stop=True)
            last.then_inc(L.bank_full, 1)
        if i > 0:
            L.eng.wait_ge(m.sem("head_normed"), L.nth("head_normed"))
            ps = L.next_bank()
            for bank_free, count in L.bank_frees:
                L.eng.wait_ge(bank_free, count)
            L.eng.matmul(ps, m.tab("swap16"), ch[i - 1][:, 0:T], start=True, stop=True).then_inc(L.bank_full, 1)


def head_norm_scalar(L, m, B):
    ch = head_chunks(B)
    for i in range(13):
        if i < 12:
            L.eng.activation(B.sq[:, i % 2, :], ch[i], ACT.Square).then_inc(m.sem("squares"), 1)
            L.eng.wait_ge(m.sem("squares"), L.nth("squares"))
            ps = L.next_bank(2)
            L.eng.wait_ge(L.bank_full, L.fill)
            if i >= 2:
                L.eng.wait_ge(m.sem("root_used"), L.nth("root_used"))
            L.eng.activation(B.root2[:, i % 2, :], ps[:, :TC], ACT.Sqrt, bias=m.tab("eps"), scale=1.0 / HD).then_inc(L.step, 1)
            L.eng.wait_ge(L.step, L.next_step())
            L.eng.sem_inc(L.bank_free, 1)
            L.eng.sem_inc(L.bank_free2, 1)
            L.eng.sem_inc(m.sem("root"), 1)
            L.nth("root")
        if i > 0:
            L.next_bank()
    L.eng.wait_ge(m.sem("root_used"), L.nth("root_used", 2))


def head_norm_vector(L, m, B):
    ch = head_chunks(B)
    L.eng.wait_ge(m.sem("rope_ax"), L.nth("rope_ax", 16))
    for i in range(13):
        if i < 12:
            L.next_bank(2)
            L.eng.wait_ge(m.sem("root"), L.nth("root"))
            r = B.root2[:, i % 2, :]
            L.eng.reciprocal(r, r).then_inc(L.step, 1)
            L.eng.wait_ge(L.step, L.next_step())
            L.eng.scalar_tensor_tensor(ch[i], ch[i], m.vec("q_gain" if i < 8 else "k_gain"), r, ALU.mult, ALU.mult).then_inc(m.sem("root_used"), 1)
            L.eng.wait_ge(m.sem("root_used"), L.nth("root_used"))
            L.eng.sem_inc(m.sem("head_normed"), 1)
            L.nth("head_normed")
        if i > 0:
            x = ch[i - 1][:, 0:T]
            ps = L.next_bank()
            L.eng.wait_ge(L.bank_full, L.fill)
            L.eng.tensor_tensor(B.rot, ps, B.rope[:, 1, :], ALU.mult).then_inc(L.step, 1)
            L.eng.wait_ge(L.step, L.next_step())
            L.eng.sem_inc(L.bank_free, 1)
            L.eng.tensor_tensor(x, x, B.rope[:, 0, :], ALU.mult).then_inc(L.step, 1)
            L.eng.wait_ge(L.step, L.next_step())
            L.eng.tensor_tensor(x, x, B.rot, ALU.add).then_inc(L.step, 1)
            L.eng.wait_ge(L.step, L.next_step())


def gqa_tensor(L, m, B, ctx):
    def score(ps, h, q):
        r = slice(64 * (h % 2), 64 * (h % 2) + 64)
        lo = T if ctx else 0
        lhs = B.q[r, h // 2, lo + q * P:lo + (q + 1) * P]
        for klo, w in ([NC_] if ctx else BOTH):
            o = klo - lo if ctx else klo
            last = L.eng.matmul(ps[:, o:o + w], lhs, B.k[r, h // 4, klo:klo + w], start=True, stop=True)
        return last
    first = 4 if ctx else 0
    attention_tensor(L, m, B.catt if ctx else B.att, score,
                     lambda h, kt, mt: B.v[:, first + kt, (h // 4) * HD:(h // 4 + 1) * HD])


def gqa_vector(L, m, B, ctx):
    lo, w = NC_ if ctx else NX
    attention_vector(L, m, B.catt if ctx else B.att,
                     lambda h, mt: B.o[64 * (h % 2):64 * (h % 2) + 64, h // 2, lo:lo + w])


def gated_add(L, m, part):
    def add(c, g, ps):
        w = BOTH[g][1]
        o = (m.x, m.xc)[g][:, c, :]
        return L.eng.scalar_tensor_tensor(o, ps[:, :w], mod_col(m, part, g)(c), o, ALU.mult, ALU.add)
    return add


def shift_vector(L, m, B):
    e = L.eng
    for lo, w in BOTH:
        h, x = B.h[:, :, lo:lo + w], B.xx[:, :, lo:lo + w]
        e.tensor_tensor(x[:, :, 1:w - 1], h[:, :, 0:w - 2], h[:, :, 2:w], ALU.add).then_inc(L.step, 1)
        L.eng.wait_ge(L.step, L.next_step())
        e.tensor_copy(x[:, :, 0:1], h[:, :, 1:2]).then_inc(L.step, 1)
        L.eng.wait_ge(L.step, L.next_step())
        e.tensor_copy(x[:, :, w - 1:w], h[:, :, w - 2:w - 1]).then_inc(L.step, 1)
        L.eng.wait_ge(L.step, L.next_step())
    for c in range(KC):
        e.scalar_tensor_tensor(B.xx[:, c, :], B.xx[:, c, :], 0.5, B.h[:, c, :], ALU.mult, ALU.subtract).then_inc(L.step, 1)
        L.eng.wait_ge(L.step, L.next_step())
    e.tensor_scalar(m.one_less_ka, m.vec("k_a", 0, 8), -1.0, 1.0, ALU.mult, ALU.add).then_inc(L.step, 1)
    L.eng.wait_ge(L.step, L.next_step())


def lerp_vector(L, m, B, j):
    for c in range(KC):
        L.eng.scalar_tensor_tensor(B.lp[:, c, :], B.xx[:, c, :], m.vec("lerp", 8 * j + c), B.h[:, c, :],
                                        ALU.mult, ALU.add).then_inc(m.sem("lerped"), 1)
        L.eng.wait_ge(m.sem("lerped"), L.nth("lerped"))


def lora_tensor(L, m, B, w, at, groups):
    for lo, wd in groups:
        ps = L.next_bank()
        for bank_free, count in L.bank_frees:
            L.eng.wait_ge(bank_free, count)
        matmuls(L, ps[:, :wd], [(w[:, at + k * P:at + (k + 1) * P], B.lp[:, k, lo:lo + wd]) for k in range(KC)]).then_inc(L.bank_full, 1)


TT = TC // P
TX = T // P


def square(a, hh, tt, p):
    c = (TT * hh + tt) * CH
    return a[64 * p:64 * p + 64, c:c + CH]


def tok(a, hh, tt, p):
    return a[64 * p:64 * p + 64, tt * P + 64 * hh:tt * P + 64 * hh + 64]


def feat(a, hh, tt, p):
    return a[64 * hh:64 * hh + 64, tt * P + 64 * p:tt * P + 64 * p + 64]


def squares_tensor(L, hh, pairs, n=TT):
    ps = L.next_bank()
    for bank_free, count in L.bank_frees:
        L.eng.wait_ge(bank_free, count)
    for tt in range(n):
        for p in range(2):
            last = matmuls(L, ps[64 * p:64 * p + 64, tt * CH:(tt + 1) * CH], pairs(hh, tt, p))
    last.then_inc(L.bank_full, 1)


def feats_tensor(L, p, pairs, n=TT):
    ps = L.next_bank()
    for bank_free, count in L.bank_frees:
        L.eng.wait_ge(bank_free, count)
    for tt in range(n):
        for hh in range(2):
            last = matmuls(L, ps[64 * hh:64 * hh + 64, tt * CH:(tt + 1) * CH], pairs(hh, tt, p))
    last.then_inc(L.bank_full, 1)


TURNS = [(0, 4), (4, 6)]


def turn_pair_tensor(L, m, src, tiles):
    lo, hi = tiles
    ps = L.next_bank()
    for bank_free, count in L.bank_frees:
        L.eng.wait_ge(bank_free, count)
    for t in range(lo, hi):
        last = L.eng.transpose(ps[:, (t - lo) * P:(t - lo + 1) * P], src[:, t * P:(t + 1) * P], m.tab("ident"))
    last.then_inc(L.bank_full, 1)


def of_head(a, hh, n=TT):
    return a[:, TT * CH * hh:(TT * hh + n) * CH].rearrange("q (t c) -> q t c", c=CH)


def of_chunk(a, p, n=TT):
    return a[:, 0:n * P].rearrange("q (t p c) -> q t p c", p=2, c=CH)[:, :, p, :]


def tiled(a):
    return a.rearrange("p (a b) -> p a b", b=CH)


def over(mask, n):
    return mask.unsqueeze(1).to_broadcast([P, n, CH])


class Pair:

    def __init__(self, B, j):
        b = B.load[j % 2]
        self.k, self.v, self.r = b[:, 0:TC], b[:, TC:2 * TC], b[:, 2 * TC:2 * TC + T]


def pair_tensor(L, m, B, j):
    L.eng.wait_ge(m.sem("kk_squares"), L.nth("kk_squares"))
    ps = L.next_bank(2)
    for bank_free, count in L.bank_frees:
        L.eng.wait_ge(bank_free, count)
    for lo, w in BOTH:
        last = L.eng.matmul(ps[:, lo:lo + w], m.tab("heads64"), B.t2[:, lo:lo + w], start=True, stop=True)
    last.then_inc(L.bank_full, 1)
    for tiles in TURNS:
        turn_pair_tensor(L, m, Pair(B, j).v, tiles)


def pair_scalar(L, m, B, j):
    L.eng.wait_ge(m.sem("kk_raw"), L.nth("kk_raw"))
    L.eng.activation(B.t2, B.t1, ACT.Square).then_inc(m.sem("kk_squares"), 1)
    L.eng.wait_ge(m.sem("kk_squares"), L.nth("kk_squares"))
    L.next_bank(2)
    L.eng.wait_ge(m.sem("kk_floor"), L.nth("kk_floor"))
    L.eng.activation(B.t2, B.t2, ACT.Sqrt).then_inc(m.sem("kk_root"), 1)
    L.eng.wait_ge(m.sem("kk_root"), L.nth("kk_root"))
    for lo, hi in TURNS:
        ps = L.next_bank()
        L.eng.wait_ge(L.bank_full, L.fill)
        L.eng.activation(B.vtok[:, lo * P:hi * P], ps[:, :(hi - lo) * P], ACT.Copy).then_inc(L.step, 1)
        L.eng.wait_ge(L.step, L.next_step())
        L.eng.sem_inc(L.bank_free, 1)


def pair_vector(L, m, B, j):
    e = L.eng
    p = Pair(B, j)
    L.eng.wait_ge(m.sem(f"pair_landed{j % 2}"), L.nth(f"pair_landed{j % 2}", 16))
    e.tensor_scalar(B.t1, p.k, m.vec("k_k", j), None, ALU.mult).then_inc(m.sem("kk_raw"), 1)
    L.eng.wait_ge(m.sem("kk_raw"), L.nth("kk_raw"))
    ps = L.next_bank(2)
    L.eng.wait_ge(L.bank_full, L.fill)
    e.tensor_scalar(B.t2, ps[:, :TC], 1e-24, None, ALU.max).then_inc(L.step, 1)
    L.eng.wait_ge(L.step, L.next_step())
    L.eng.sem_inc(L.bank_free, 1)
    L.eng.sem_inc(L.bank_free2, 1)
    L.eng.sem_inc(m.sem("kk_floor"), 1)
    L.nth("kk_floor")
    L.eng.wait_ge(m.sem("kk_root"), L.nth("kk_root"))
    e.reciprocal(B.t2, B.t2).then_inc(L.step, 1)
    L.eng.wait_ge(L.step, L.next_step())
    e.tensor_tensor(B.kk, B.t1, B.t2, ALU.mult).then_inc(L.step, 1)
    L.eng.wait_ge(L.step, L.next_step())
    for _ in TURNS:
        L.next_bank()


def decay_tensor(L, m, B, j, d, w):
    r = slice(64 * d, 64 * d + 64)
    for at, src in ((0, B.tw), (D, B.ta)):
        ps = L.next_bank(2)
        for bank_free, count in L.bank_frees:
            L.eng.wait_ge(bank_free, count)
        for lo, wd in BOTH:
            last = L.eng.matmul(ps[:, lo:lo + wd], w[r, at + j * P:at + (j + 1) * P], src[r, lo:lo + wd],
                                start=True, stop=True)
        last.then_inc(L.bank_full, 1)


def decay_scalar(L, m, B, j, d):
    e = L.eng
    for dst, b in ((B.lw, "w0"), (B.a, "a0")):
        ps = L.next_bank(2)
        L.eng.wait_ge(L.bank_full, L.fill)
        e.activation(dst, ps[:, :TC], ACT.Sigmoid, bias=m.vec(b, 8 * d + j)).then_inc(L.step, 1)
        L.eng.wait_ge(L.step, L.next_step())
        L.eng.sem_inc(L.bank_free, 1)
        L.eng.sem_inc(L.bank_free2, 1)
        L.eng.sem_inc(m.sem("gate_sigmoid"), 1)
        L.nth("gate_sigmoid")
    L.eng.wait_ge(m.sem("decay_sum"), L.nth("decay_sum"))
    e.activation(B.t1, B.cm, ACT.Exp).then_inc(L.step, 1)
    L.eng.wait_ge(L.step, L.next_step())
    e.activation(B.t2, B.cm, ACT.Exp, scale=-1.0).then_inc(L.step, 1)
    L.eng.wait_ge(L.step, L.next_step())
    e.activation(B.ci, B.ci, ACT.Exp).then_inc(L.step, 1)
    L.eng.wait_ge(L.step, L.next_step())
    e.activation(m.ecol, m.ecol, ACT.Exp).then_inc(m.sem("decay_exp"), 1)
    L.eng.wait_ge(m.sem("decay_exp"), L.nth("decay_exp"))


def decay_vector(L, m, B, j, d):
    e = L.eng
    p = Pair(B, j)
    L.next_bank(2)
    L.next_bank(2)
    L.eng.wait_ge(m.sem("gate_sigmoid"), L.nth("gate_sigmoid"))
    e.tensor_scalar(B.lw, B.lw, DECAY_SCALE, None, ALU.mult).then_inc(L.step, 1)
    L.eng.wait_ge(L.step, L.next_step())
    e.tensor_tensor_scan(B.ci, B.keep, B.lw, 0.0, ALU.mult, ALU.add).then_inc(L.step, 1)
    L.eng.wait_ge(L.step, L.next_step())
    ci = tiled(B.ci)
    e.tensor_copy(m.tot, ci[:, :, CH - 1:CH].rearrange("p a b -> p (a b)")).then_inc(L.step, 1)
    L.eng.wait_ge(L.step, L.next_step())
    if d == 1:
        e.tensor_tensor(B.ci, B.lw, B.ci, ALU.subtract).then_inc(L.step, 1)
        L.eng.wait_ge(L.step, L.next_step())
        e.tensor_tensor(ci, ci, bcast(m.tot, CH), ALU.add).then_inc(L.step, 1)
        L.eng.wait_ge(L.step, L.next_step())
    e.tensor_scalar(m.mid, m.tot, 0.5, None, ALU.mult).then_inc(L.step, 1)
    L.eng.wait_ge(L.step, L.next_step())
    e.tensor_tensor(tiled(B.cm), ci, bcast(m.mid, CH), ALU.subtract).then_inc(L.step, 1)
    L.eng.wait_ge(L.step, L.next_step())
    e.tensor_tensor(B.ci, B.cm, B.lw, ALU.subtract).then_inc(L.step, 1)
    L.eng.wait_ge(L.step, L.next_step())
    e.memset(m.ecol, 0.0).then_inc(L.step, 1)
    L.eng.wait_ge(L.step, L.next_step())
    mid, n, x = m.mid, ALLCH, XCH
    spans = [((x, n - 1), (x + 1, n)), ((n - 1, n), (0, 1)), ((0, x - 1), (1, x))]
    if d == 1:
        spans = [((x + 1, n), (x, n - 1)), ((x, x + 1), (x - 1, x)), ((1, x), (0, x - 1))]
    for (a, b), (c, f) in spans:
        e.tensor_tensor(m.ecol[:, a:b], mid[:, a:b], mid[:, c:f], ALU.add).then_inc(L.step, 1)
        L.eng.wait_ge(L.step, L.next_step())
    L.eng.sem_inc(m.sem("decay_sum"), 1)
    L.nth("decay_sum")
    L.eng.wait_ge(m.sem("gate_sigmoid"), L.nth("gate_sigmoid"))
    e.tensor_scalar(B.kd, B.a, m.vec("k_a", j), m.one_less_ka[:, j:j + 1], ALU.mult, ALU.add).then_inc(L.step, 1)
    L.eng.wait_ge(L.step, L.next_step())
    e.tensor_tensor(B.kd, B.kd, p.k, ALU.mult).then_inc(L.step, 1)
    L.eng.wait_ge(L.step, L.next_step())
    if d == 0:
        e.tensor_copy(B.bk, B.kd[:, 0:T]).then_inc(L.step, 1)
        L.eng.wait_ge(L.step, L.next_step())
    else:
        e.tensor_tensor(B.bk, B.bk, B.kd[:, 0:T], ALU.add).then_inc(L.step, 1)
        L.eng.wait_ge(L.step, L.next_step())
    e.tensor_tensor(B.b, B.kk, B.a, ALU.mult).then_inc(L.step, 1)
    L.eng.wait_ge(L.step, L.next_step())
    L.eng.wait_ge(m.sem("decay_exp"), L.nth("decay_exp"))
    e.tensor_tensor(B.al, B.kk, B.ci, ALU.mult).then_inc(L.step, 1)
    L.eng.wait_ge(L.step, L.next_step())
    e.tensor_tensor(B.be, B.b, B.t2, ALU.mult).then_inc(L.step, 1)
    L.eng.wait_ge(L.step, L.next_step())
    e.tensor_tensor(B.ka, B.kd, B.t2, ALU.mult).then_inc(L.step, 1)
    L.eng.wait_ge(L.step, L.next_step())
    e.tensor_tensor(B.rh[:, 0:T], p.r, B.t1[:, 0:T], ALU.mult).then_inc(L.step, 1)
    L.eng.wait_ge(L.step, L.next_step())


def chunk_order(d):
    x, c = list(range(XCH)), list(range(XCH, ALLCH))
    return c + x if d == 0 else c[::-1] + x[::-1]


LEVELS = (2, 4, 8, 16, 32)


def tile_tensor(L, m, B, j, d):
    for lhs, rhs in ((B.be, B.al), (B.al, B.be), (B.ka, B.al)):
        for hh in range(2):
            squares_tensor(L, hh, lambda *at: [(feat(lhs, *at), feat(rhs, *at))])
    for lhs in (B.be, B.ka):
        for hh in range(2):
            squares_tensor(L, hh, lambda *at: [(feat(lhs, *at), feat(B.rh, *at))], TX)
    for src in (B.al, B.be, B.ka):
        for tiles in TURNS:
            turn_pair_tensor(L, m, src, tiles)
    for hh in range(2):
        L.eng.wait_ge(m.sem("masked"), L.nth("masked"))
        squares_tensor(L, hh, lambda *at: [(square(B.akt, *at), tok(B.vtok, *at))])
    for lv in LEVELS:
        for hh in range(2):
            L.eng.wait_ge(m.sem("inverse"), L.nth("inverse", 2))
            squares_tensor(L, hh, lambda *at: [(square(B.nt, *at), square(B.ti, *at))])
        for hh in range(2):
            L.eng.wait_ge(m.sem("corner"), L.nth("corner"))
            if lv != LEVELS[-1]:
                squares_tensor(L, hh, lambda *at: [(square(B.tt, *at), square(B.x, *at))])
            squares_tensor(L, hh, lambda *at: [(square(B.x, *at), square(B.tt, *at))])
    L.eng.wait_ge(m.sem("turned"), L.nth("turned", 8))
    for hh in range(2):
        L.eng.wait_ge(m.sem("inverse"), L.nth("inverse"))
        squares_tensor(L, hh, lambda *at: [(square(B.tt, *at), tok(B.altok, *at))])
        squares_tensor(L, hh, lambda *at: [(square(B.tt, *at), square(B.akv, *at))])
    L.eng.wait_ge(m.sem("solved"), L.nth("solved", 4))
    for p in range(2):
        feats_tensor(L, p, lambda *at: [(square(B.ua, *at), tok(B.betok, *at))])
        feats_tensor(L, p, lambda *at: [(tok(B.betok, *at), square(B.uv, *at)), (tok(B.katok, *at), tok(B.vtok, *at))])
    for p in range(2):
        feats_tensor(L, p, lambda *at: [(square(B.ua, *at), square(B.rbt, *at))], TX)
        feats_tensor(L, p, lambda *at: [(square(B.uv, *at), square(B.rbt, *at)), (tok(B.vtok, *at), square(B.rkt, *at))], TX)
    for q in chunk_order(d)[:-1]:
        L.eng.wait_ge(m.sem("state"), L.nth("state"))
        ps = L.next_bank()
        for bank_free, count in L.bank_frees:
            L.eng.wait_ge(bank_free, count)
        for hh in range(2):
            r = slice(64 * hh, 64 * hh + 64)
            last = L.eng.matmul(ps[r, 0:CH], B.mt[r, q * CH:(q + 1) * CH], B.s[r, q * CH:(q + 1) * CH], start=True, stop=True)
        last.then_inc(L.bank_full, 1)
    L.eng.wait_ge(m.sem("state"), L.nth("state"))
    ps = L.next_bank()
    for bank_free, count in L.bank_frees:
        L.eng.wait_ge(bank_free, count)
    for hh in range(2):
        for q in range(XCH):
            at = (hh, q // 2, q % 2)
            last = L.eng.matmul(feat(ps, *at), feat(B.s, *at), feat(B.rp, *at), start=True, stop=True)
    last.then_inc(L.bank_full, 1)


def tile_scalar(L, m, B, j, d):
    e = L.eng

    def copy(dst, src, scale, what):
        e.activation(dst, src, ACT.Copy, scale=scale).then_inc(L.step, 1)
        L.eng.wait_ge(L.step, L.next_step())
        L.eng.sem_inc(L.bank_free, 1)
        L.eng.sem_inc(m.sem(what), 1)
        L.nth(what)

    for _ in range(10):
        L.next_bank()
    for dst in (B.altok, B.betok, B.katok):
        for lo, hi in TURNS:
            ps = L.next_bank()
            L.eng.wait_ge(L.bank_full, L.fill)
            copy(dst[:, lo * P:hi * P], ps[:, :(hi - lo) * P], 1.0, "turned")
    for hh in range(2):
        ps = L.next_bank()
        L.eng.wait_ge(L.bank_full, L.fill)
        copy(of_head(B.akv, hh), tiled(ps[:, :TT * CH]), 1.0, "turned")
    for lv in LEVELS:
        for _ in range(6 if lv != LEVELS[-1] else 4):
            L.next_bank()
    for hh in range(2):
        for dst in (B.ua, B.uv):
            ps = L.next_bank()
            L.eng.wait_ge(L.bank_full, L.fill)
            copy(of_head(dst, hh), tiled(ps[:, :TT * CH]), -1.0, "solved")
    for _ in range(8 + ALLCH - 1 + 1):
        L.next_bank()


def tile_vector(L, m, B, j, d):
    e = L.eng

    def mask(k):
        return B.masks[:, k * CH:(k + 1) * CH]

    def read(dst, fn):
        ps = L.next_bank()
        L.eng.wait_ge(L.bank_full, L.fill)
        n = dst.shape[1]
        fn(dst, tiled(ps[:, :CH * n]), n).then_inc(L.step, 1)
        L.eng.wait_ge(L.step, L.next_step())
        L.eng.sem_inc(L.bank_free, 1)

    def masked(k):
        return lambda o, ps, n: e.tensor_tensor(o, ps, over(mask(k), n), ALU.mult)

    before, upto = MASK["before"][d], MASK["upto"][d]
    for hh in range(2):
        read(of_head(B.nt, hh), masked(before))
        x, t, nt = [of_head(a, hh) for a in (B.x, B.tt, B.nt)]
        e.tensor_tensor(x, nt, over(mask(4 + 1 - d), TT), ALU.mult).then_inc(L.step, 1)
        L.eng.wait_ge(L.step, L.next_step())
        e.tensor_tensor(t, over(B.eye, TT), x, ALU.subtract).then_inc(L.step, 1)
        L.eng.wait_ge(L.step, L.next_step())
    for hh in range(2):
        x, t = of_head(B.x, hh), of_head(B.ti, hh)
        read(x, masked(4 + d))
        e.tensor_tensor(t, over(B.eye, TT), x, ALU.subtract).then_inc(m.sem("inverse"), 1)
        L.eng.wait_ge(m.sem("inverse"), L.nth("inverse"))
        L.eng.sem_inc(m.sem("inverse"), 1)
        L.nth("inverse")
    for hh in range(2):
        read(of_head(B.akt, hh), masked(before))
        L.eng.sem_inc(m.sem("masked"), 1)
        L.nth("masked")
    for dst in (B.rbt, B.rkt):
        for hh in range(2):
            read(of_head(dst, hh, TX), masked(upto))
    for _ in range(8):
        L.next_bank()
    for i, lv in enumerate(LEVELS):
        for hh in range(2):
            read(of_head(B.x, hh), masked(6 + 2 * i + d))
            L.eng.sem_inc(m.sem("corner"), 1)
            L.nth("corner")
        for hh in range(2):
            for dst in ((B.ti, B.tt) if lv != LEVELS[-1] else (B.tt,)):
                read(of_head(dst, hh), lambda o, ps, n: e.tensor_tensor(o, o, ps, ALU.subtract))
                L.eng.sem_inc(m.sem("inverse"), 1)
                L.nth("inverse")
    for _ in range(4):
        L.next_bank()
    ecol = m.ecol.rearrange("q (t p) -> q t p", p=2)
    for p in range(2):
        read(of_chunk(B.mt, p), lambda o, ps, n: e.tensor_tensor(o, ps, over(B.eye, n), ALU.add))
        read(of_chunk(B.g, p), lambda o, ps, n: e.tensor_tensor(o, ps, bcast(ecol[:, :, p], CH), ALU.mult))
    for p in range(2):
        read(of_chunk(B.rp, p, TX), lambda o, ps, n: e.tensor_tensor(o, ps, of_chunk(B.rh, p, TX), ALU.add))
        y = of_chunk(B.yj, p, TX)
        if d == 0:
            read(y, lambda o, ps, n: e.tensor_copy(o, ps))
        else:
            read(y, lambda o, ps, n: e.tensor_tensor(o, o, ps, ALU.add))
    order = chunk_order(d)
    sl = lambda a, q: a[:, q * CH:(q + 1) * CH]
    e.memset(sl(B.s, order[0]), 0.0).then_inc(m.sem("state"), 1)
    L.eng.wait_ge(m.sem("state"), L.nth("state"))
    for q, nq in zip(order, order[1:]):
        ps = L.next_bank()
        L.eng.wait_ge(L.bank_full, L.fill)
        e.scalar_tensor_tensor(sl(B.s, nq), ps[:, 0:CH], m.ecol[:, q:q + 1], sl(B.g, q), ALU.mult, ALU.add).then_inc(L.step, 1)
        L.eng.wait_ge(L.step, L.next_step())
        L.eng.sem_inc(L.bank_free, 1)
        L.eng.sem_inc(m.sem("state"), 1)
        L.nth("state")
    ps = L.next_bank()
    L.eng.wait_ge(L.bank_full, L.fill)
    e.tensor_tensor(B.yj, B.yj, ps, ALU.add).then_inc(L.step, 1)
    L.eng.wait_ge(L.step, L.next_step())
    L.eng.sem_inc(L.bank_free, 1)


def readout_tensor(L, m, B, j, g2):
    ones = m.tab("heads64")
    ps = L.next_bank()
    for bank_free, count in L.bank_frees:
        L.eng.wait_ge(bank_free, count)
    L.eng.matmul(ps, ones, B.yj, start=True, stop=True).then_inc(L.bank_full, 1)
    L.eng.wait_ge(m.sem("centred_squares"), L.nth("centred_squares"))
    ps = L.next_bank()
    for bank_free, count in L.bank_frees:
        L.eng.wait_ge(bank_free, count)
    L.eng.matmul(ps, ones, B.t2[:, 0:T], start=True, stop=True).then_inc(L.bank_full, 1)
    L.eng.wait_ge(m.sem("bonus"), L.nth("bonus"))
    ps = L.next_bank()
    for bank_free, count in L.bank_frees:
        L.eng.wait_ge(bank_free, count)
    L.eng.matmul(ps, ones, B.bk, start=True, stop=True).then_inc(L.bank_full, 1)
    ps = L.next_bank()
    for bank_free, count in L.bank_frees:
        L.eng.wait_ge(bank_free, count)
    L.eng.matmul(ps, g2[:, j * P:(j + 1) * P], B.tg, start=True, stop=True).then_inc(L.bank_full, 1)


def readout_scalar(L, m, B, j):
    L.next_bank()
    L.eng.wait_ge(m.sem("centred"), L.nth("centred"))
    L.eng.activation(B.t2[:, 0:T], B.yj, ACT.Square).then_inc(m.sem("centred_squares"), 1)
    L.eng.wait_ge(m.sem("centred_squares"), L.nth("centred_squares"))
    ps = L.next_bank()
    L.eng.wait_ge(L.bank_full, L.fill)
    L.eng.activation(B.lw[:, 0:T], ps, ACT.Sqrt, bias=m.tab("gn_eps"), scale=1.0 / 64).then_inc(L.step, 1)
    L.eng.wait_ge(L.step, L.next_step())
    L.eng.sem_inc(L.bank_free, 1)
    L.eng.sem_inc(m.sem("gn_root"), 1)
    L.nth("gn_root")
    L.next_bank()
    L.next_bank()


def readout_vector(L, m, B, j):
    e = L.eng
    p = Pair(B, j)
    r = B.lw[:, 0:T]
    ps = L.next_bank()
    L.eng.wait_ge(L.bank_full, L.fill)
    e.scalar_tensor_tensor(B.yj, ps, -1.0 / 64, B.yj, ALU.mult, ALU.add).then_inc(L.step, 1)
    L.eng.wait_ge(L.step, L.next_step())
    L.eng.sem_inc(L.bank_free, 1)
    L.eng.sem_inc(m.sem("centred"), 1)
    L.nth("centred")
    e.scalar_tensor_tensor(B.bk, B.bk, m.vec("r_k", j), p.r, ALU.mult, ALU.mult).then_inc(m.sem("bonus"), 1)
    L.eng.wait_ge(m.sem("bonus"), L.nth("bonus"))
    L.next_bank()
    L.eng.wait_ge(m.sem("gn_root"), L.nth("gn_root"))
    e.reciprocal(r, r).then_inc(L.step, 1)
    L.eng.wait_ge(L.step, L.next_step())
    e.tensor_tensor(B.yj, B.yj, r, ALU.mult).then_inc(L.step, 1)
    L.eng.wait_ge(L.step, L.next_step())
    e.tensor_scalar(B.yj, B.yj, m.vec("ln_g", j), m.vec("ln_b", j), ALU.mult, ALU.add).then_inc(L.step, 1)
    L.eng.wait_ge(L.step, L.next_step())
    ps = L.next_bank()
    L.eng.wait_ge(L.bank_full, L.fill)
    e.tensor_tensor(r, p.v[:, 0:T], ps, ALU.mult).then_inc(L.step, 1)
    L.eng.wait_ge(L.step, L.next_step())
    L.eng.sem_inc(L.bank_free, 1)
    e.tensor_tensor(B.yj, B.yj, r, ALU.add).then_inc(L.step, 1)
    L.eng.wait_ge(L.step, L.next_step())
    ps = L.next_bank()
    L.eng.wait_ge(L.bank_full, L.fill)
    e.tensor_tensor(B.out[:, j, :], B.yj, ps, ALU.mult).then_inc(L.step, 1)
    L.eng.wait_ge(L.step, L.next_step())
    L.eng.sem_inc(L.bank_free, 1)


def build(nc, a):
    with ExitStack() as ctx:
        m = Mem(nc, ctx)
        ring_place = -(-nc.sbuf_base // 32) * 32
        m.ring = m.sb("ring", [P, SLOTS, SLAB])
        m.low = nc.alloc_sbuf_tensor_at("ring_low", [P, SLOTS, SLAB], F32R, offset=ring_place)
        m.x = m.sb("x_residual", [P, KC, T])
        m.xc = m.sb("ctx_residual", [P, KC, C])
        m.vecs = m.sb("vecs", [P, NVEC])
        m.tabs = m.sb("tabs", [P, RESIDENT])
        m.root = m.sb("root", [P, T])
        m.stat = m.sb("stat", [P, 16])
        m.cond = m.sb("cond", [P, 16])
        m.mod = m.sb("mod", [P, 96])
        m.modg = m.sb("modg", [P, 32])
        m.one_less_ka = m.sb("one_less_ka", [P, 8])
        m.tot, m.mid, m.ecol = [m.sb(n, [P, ALLCH])[:, :] for n in ("chunk_total", "chunk_middle", "chunk_carry")]
        m.cond, m.mod, m.modg, m.root, m.one_less_ka = [t[:, :] for t in (m.cond, m.mod, m.modg, m.root, m.one_less_ka)]
        m.arena_place = -(-nc.sbuf_base // 32) * 32
        m.arena = m.sb("arena", [P, ARENA])
        m.psum = ctx.enter_context(nc.psum_tensor("psum", [P, 8 * BANK], F32))
        m.bank_full = [m.sem(f"bank_full{b}") for b in range(8)]
        m.bank_free = [m.sem(f"bank_free{b}") for b in range(8)]
        m.slab_landed = [m.sem(f"slab_landed{s}") for s in range(SLOTS)]
        m.high = m.rounded("slab_high", HIGH, SLOTS, SLAB)
        B, R = Block1(m), Block2(m)
        wall = a["wall"]

        block = ctx.enter_context(nc.Block())

        @block.sync
        def _(sp):
            for n in range(NSLAB):
                if n >= SLOTS:
                    sp.wait_ge(m.sem("slab_used"), n - SLOTS + 1)
                sp.dma_start(m.ring[:, n % SLOTS, :], wall[n]).then_inc(m.slab_landed[n % SLOTS], 16)

        @block.gpsimd
        def _(pool):
            L = Lane(m, pool, "pool")
            load = lambda dst, src, what: pool.dma_start(dst, src).then_inc(m.sem(what), 16)
            tab = lambda name, n: a["tabs"][:, TCOL[name][0]:TCOL[name][0] + n]
            load(m.vecs[:, :], a["vecs"], "inputs_landed")
            load(m.tabs[:, :], a["tabs"][:, 0:RESIDENT], "inputs_landed")
            load(m.x[:, :, :], a["x"], "inputs_landed")
            load(m.xc[:, :, :], a["ctx"], "inputs_landed")
            load(m.at(28184, 1024), tab("cos96", 1024), "rope96")
            L.eng.wait_ge(m.sem("room_for_dft"), L.nth("room_for_dft"))
            load(B.dft, tab("dft_c", 5248), "dft_landed")
            L.eng.wait_ge(m.sem("room_for_mem"), L.nth("room_for_mem"))
            load(B.mem, a["mem"], "mem_landed")
            split_slabs(L, m, "moe")
            L.eng.wait_ge(m.sem("room_for_rope"), L.nth("room_for_rope"))
            load(R.rope, tab("cos_ax", 1024).rearrange("p (a b) -> p a b", a=2), "rope_ax")
            split_slabs(L, m, "ffn0")
            spill = a["spill"]
            L.eng.wait_ge(m.sem("kv_ready"), L.nth("kv_ready"))
            pool.dma_start(spill[:, :, 0:TC], R.pk).then_inc(m.sem("spilled"), 16)
            pool.dma_start(spill[:, :, TC:2 * TC], R.pv).then_inc(m.sem("spilled"), 16)
            L.eng.wait_ge(m.sem("r_ready"), L.nth("r_ready"))
            pool.dma_start(spill[:, :, 2 * TC:2 * TC + T], R.pr).then_inc(m.sem("spilled"), 16)
            pool.wait_ge(m.sem("spilled"), 48)
            load(R.masks, tab("masks", 1024), "wkv_tables")
            load(R.eye, tab("eye", 64), "wkv_tables")
            load(R.keep, tab("scan_keep", TC), "wkv_tables")
            for j in range(KC):
                if j >= 2:
                    L.eng.wait_ge(m.sem("pair_read_out"), L.nth("pair_read_out"))
                load(R.load[j % 2], spill[:, j, :], f"pair_landed{j % 2}")
            split_slabs(L, m, "ffn1")
            L.eng.wait_ge(m.sem("result"), L.nth("result"))
            pool.dma_start(a["out"], m.x[:, :, :]).then_inc(m.sem("out_stored"), 16)
            pool.wait_ge(m.sem("out_stored"), 16)

        @block.tensor
        def _(pe):
            L = Lane(m, pe, "tensor")
            L.eng.wait_ge(m.sem("inputs_landed"), L.nth("inputs_landed", 64))
            mix_in_tensor(L, m, B)
            pe.wait_ge(m.sem("vector_stage_done"), L.nth("vector_stage_done"))
            pe.wait_ge(m.sem("scalar_stage_done"), L.nth("scalar_stage_done"))
            latent_tensor(L, m, B)
            pe.wait_ge(m.sem("vector_stage_done"), L.nth("vector_stage_done"))
            pe.wait_ge(m.sem("scalar_stage_done"), L.nth("scalar_stage_done"))
            latent_attention_tensor(L, m, B)
            pe.wait_ge(m.sem("vector_stage_done"), L.nth("vector_stage_done"))
            pe.wait_ge(m.sem("scalar_stage_done"), L.nth("scalar_stage_done"))
            norm_tensor(L, m, chunk(B.mix), 4)
            pe.wait_ge(m.sem("vector_stage_done"), L.nth("vector_stage_done"))
            pe.wait_ge(m.sem("scalar_stage_done"), L.nth("scalar_stage_done"))
            conv_turn_tensor(L, m, B)
            pe.wait_ge(m.sem("vector_stage_done"), L.nth("vector_stage_done"))
            pe.wait_ge(m.sem("scalar_stage_done"), L.nth("scalar_stage_done"))
            filter_tensor(L, m, B)
            pe.wait_ge(m.sem("vector_stage_done"), L.nth("vector_stage_done"))
            pe.wait_ge(m.sem("scalar_stage_done"), L.nth("scalar_stage_done"))
            L.eng.drain().then_inc(m.sem("slab_used"), 1)
            L.eng.drain().then_inc(m.sem("slab_used"), 1)
            for order in range(2):
                pe.wait_ge(m.sem("vector_stage_done"), L.nth("vector_stage_done"))
                pe.wait_ge(m.sem("scalar_stage_done"), L.nth("scalar_stage_done"))
                filter_spectrum_tensor(L, m, B, order)
                pe.wait_ge(m.sem("vector_stage_done"), L.nth("vector_stage_done"))
                pe.wait_ge(m.sem("scalar_stage_done"), L.nth("scalar_stage_done"))
                product_tensor(L, m, B)
                pe.wait_ge(m.sem("vector_stage_done"), L.nth("vector_stage_done"))
                pe.wait_ge(m.sem("scalar_stage_done"), L.nth("scalar_stage_done"))
                if order == 0:
                    inverse0_tensor(L, m, B)
                    pe.wait_ge(m.sem("vector_stage_done"), L.nth("vector_stage_done"))
                    pe.wait_ge(m.sem("scalar_stage_done"), L.nth("scalar_stage_done"))
                    L.eng.drain().then_inc(m.sem("slab_used"), 1)
                    turn_tensor(L, m, lambda d, i: B.vt[:, i, d * P:(d + 1) * P], 4)
                    pe.wait_ge(m.sem("vector_stage_done"), L.nth("vector_stage_done"))
                    pe.wait_ge(m.sem("scalar_stage_done"), L.nth("scalar_stage_done"))
            inverse1_tensor(L, m, B)
            pe.wait_ge(m.sem("vector_stage_done"), L.nth("vector_stage_done"))
            pe.wait_ge(m.sem("scalar_stage_done"), L.nth("scalar_stage_done"))
            norm_tensor(L, m, lambda c: B.mix[:, 4 + c, :], 4)
            pe.wait_ge(m.sem("vector_stage_done"), L.nth("vector_stage_done"))
            pe.wait_ge(m.sem("scalar_stage_done"), L.nth("scalar_stage_done"))
            project_tensor(L, m, "out", chunk(B.mix), [(0, T)])
            pe.wait_ge(m.sem("vector_stage_done"), L.nth("vector_stage_done"))
            pe.wait_ge(m.sem("scalar_stage_done"), L.nth("scalar_stage_done"))
            memory_tensor(L, m, B)
            pe.wait_ge(m.sem("vector_stage_done"), L.nth("vector_stage_done"))
            pe.wait_ge(m.sem("scalar_stage_done"), L.nth("scalar_stage_done"))
            memory_attention_tensor(L, m, B)
            pe.wait_ge(m.sem("vector_stage_done"), L.nth("vector_stage_done"))
            pe.wait_ge(m.sem("scalar_stage_done"), L.nth("scalar_stage_done"))
            project_tensor(L, m, "mo", chunk(B.mo), [(0, T)])
            pe.wait_ge(m.sem("vector_stage_done"), L.nth("vector_stage_done"))
            pe.wait_ge(m.sem("scalar_stage_done"), L.nth("scalar_stage_done"))
            route_tensor(L, m, B)
            pe.wait_ge(m.sem("vector_stage_done"), L.nth("vector_stage_done"))
            pe.wait_ge(m.sem("scalar_stage_done"), L.nth("scalar_stage_done"))
            swiglu_tensor(L, m, "moe", GROUPS * EXPERTS, B, [NX], B.cmbt)
            pe.wait_ge(m.sem("vector_stage_done"), L.nth("vector_stage_done"))
            pe.wait_ge(m.sem("scalar_stage_done"), L.nth("scalar_stage_done"))
            norm_tensor(L, m, chunk(B.h), KC)
            pe.wait_ge(m.sem("vector_stage_done"), L.nth("vector_stage_done"))
            pe.wait_ge(m.sem("scalar_stage_done"), L.nth("scalar_stage_done"))

            for i in range(2):
                mod_tensor(L, m, i)
                pe.wait_ge(m.sem("vector_stage_done"), L.nth("vector_stage_done"))
                pe.wait_ge(m.sem("scalar_stage_done"), L.nth("scalar_stage_done"))
                modnorm_tensor(L, m, R)
                pe.wait_ge(m.sem("vector_stage_done"), L.nth("vector_stage_done"))
                pe.wait_ge(m.sem("scalar_stage_done"), L.nth("scalar_stage_done"))
                if i == 0:
                    qkv_tensor(L, m, R)
                    pe.wait_ge(m.sem("vector_stage_done"), L.nth("vector_stage_done"))
                    pe.wait_ge(m.sem("scalar_stage_done"), L.nth("scalar_stage_done"))
                    head_norm_tensor(L, m, R)
                    pe.wait_ge(m.sem("vector_stage_done"), L.nth("vector_stage_done"))
                    pe.wait_ge(m.sem("scalar_stage_done"), L.nth("scalar_stage_done"))
                    for ctx_side in (False, True):
                        gqa_tensor(L, m, R, ctx_side)
                        pe.wait_ge(m.sem("vector_stage_done"), L.nth("vector_stage_done"))
                        pe.wait_ge(m.sem("scalar_stage_done"), L.nth("scalar_stage_done"))
                    project_tensor(L, m, "wo0", chunk(R.o), BOTH)
                    pe.wait_ge(m.sem("vector_stage_done"), L.nth("vector_stage_done"))
                    pe.wait_ge(m.sem("scalar_stage_done"), L.nth("scalar_stage_done"))
                else:
                    pe.wait_ge(m.sem("vector_stage_done"), L.nth("vector_stage_done"))
                    pe.wait_ge(m.sem("scalar_stage_done"), L.nth("scalar_stage_done"))
                    for name in ("rw_k", "rw_v"):
                        L.eng.wait_ge(m.sem("lerped"), L.nth("lerped", KC))
                        project_tensor(L, m, name, chunk(R.lp), BOTH)
                        pe.wait_ge(m.sem("vector_stage_done"), L.nth("vector_stage_done"))
                        pe.wait_ge(m.sem("scalar_stage_done"), L.nth("scalar_stage_done"))
                    w = L.next_slab("lora1")
                    L.eng.wait_ge(L.landed, L.landings)
                    for part in range(2):
                        L.eng.wait_ge(m.sem("lerped"), L.nth("lerped", KC))
                        lora_tensor(L, m, R, w, part * D, BOTH)
                        pe.wait_ge(m.sem("vector_stage_done"), L.nth("vector_stage_done"))
                        pe.wait_ge(m.sem("scalar_stage_done"), L.nth("scalar_stage_done"))
                    L.eng.drain().then_inc(m.sem("slab_used"), 1)
                    w = L.next_slab("g1")
                    L.eng.wait_ge(L.landed, L.landings)
                    L.eng.wait_ge(m.sem("lerped"), L.nth("lerped", KC))
                    lora_tensor(L, m, R, w, 0, [NX])
                    L.eng.drain().then_inc(m.sem("slab_used"), 1)
                    pe.wait_ge(m.sem("vector_stage_done"), L.nth("vector_stage_done"))
                    pe.wait_ge(m.sem("scalar_stage_done"), L.nth("scalar_stage_done"))
                    L.eng.wait_ge(m.sem("lerped"), L.nth("lerped", KC))
                    project_tensor(L, m, "rw_r", chunk(R.lp), [NX])
                    pe.wait_ge(m.sem("vector_stage_done"), L.nth("vector_stage_done"))
                    pe.wait_ge(m.sem("scalar_stage_done"), L.nth("scalar_stage_done"))
                    w2 = L.next_slab("lora2")
                    L.eng.wait_ge(L.landed, L.landings)
                    g2 = L.next_slab("g2")
                    L.eng.wait_ge(L.landed, L.landings)
                    for j in range(KC):
                        pair_tensor(L, m, R, j)
                        pe.wait_ge(m.sem("vector_stage_done"), L.nth("vector_stage_done"))
                        pe.wait_ge(m.sem("scalar_stage_done"), L.nth("scalar_stage_done"))
                        for d in range(2):
                            decay_tensor(L, m, R, j, d, w2)
                            pe.wait_ge(m.sem("vector_stage_done"), L.nth("vector_stage_done"))
                            pe.wait_ge(m.sem("scalar_stage_done"), L.nth("scalar_stage_done"))
                            tile_tensor(L, m, R, j, d)
                            pe.wait_ge(m.sem("vector_stage_done"), L.nth("vector_stage_done"))
                            pe.wait_ge(m.sem("scalar_stage_done"), L.nth("scalar_stage_done"))
                        readout_tensor(L, m, R, j, g2)
                        pe.wait_ge(m.sem("vector_stage_done"), L.nth("vector_stage_done"))
                        pe.wait_ge(m.sem("scalar_stage_done"), L.nth("scalar_stage_done"))
                    L.eng.drain().then_inc(m.sem("slab_used"), 1)
                    L.eng.drain().then_inc(m.sem("slab_used"), 1)
                    project_tensor(L, m, "wo1", chunk(R.out), [NX])
                    pe.wait_ge(m.sem("vector_stage_done"), L.nth("vector_stage_done"))
                    pe.wait_ge(m.sem("scalar_stage_done"), L.nth("scalar_stage_done"))
                modnorm_tensor(L, m, R, i == 0)
                pe.wait_ge(m.sem("vector_stage_done"), L.nth("vector_stage_done"))
                pe.wait_ge(m.sem("scalar_stage_done"), L.nth("scalar_stage_done"))
                swiglu_tensor(L, m, f"ffn{i}", FF // 256, R, BOTH[:2 - i])
                pe.wait_ge(m.sem("vector_stage_done"), L.nth("vector_stage_done"))
                pe.wait_ge(m.sem("scalar_stage_done"), L.nth("scalar_stage_done"))
            norm_tensor(L, m, chunk(R.h, 0, T), KC)
            pe.wait_ge(m.sem("vector_stage_done"), L.nth("vector_stage_done"))
            pe.wait_ge(m.sem("scalar_stage_done"), L.nth("scalar_stage_done"))

        @block.scalar
        def _(act):
            L = Lane(m, act, "scalar")
            L.eng.wait_ge(m.sem("inputs_landed"), L.nth("inputs_landed", 64))

            def copy(dst):
                return lambda g, ps: act.activation(dst(g), ps[:, :dst(g).shape[1]], ACT.Copy)

            mix_in_scalar(L, m, B)
            act.sem_inc(m.sem("scalar_stage_done"), 1)
            act.wait_ge(m.sem("vector_stage_done"), L.nth("vector_stage_done"))
            latent_scalar(L, m, B)
            act.sem_inc(m.sem("scalar_stage_done"), 1)
            act.wait_ge(m.sem("vector_stage_done"), L.nth("vector_stage_done"))
            attention_scalar(L, m, B.att)
            act.sem_inc(m.sem("scalar_stage_done"), 1)
            act.wait_ge(m.sem("vector_stage_done"), L.nth("vector_stage_done"))
            norm_scalar(L, m, chunk(B.o), chunk(B.mix), 4)
            act.sem_inc(m.sem("scalar_stage_done"), 1)
            act.wait_ge(m.sem("vector_stage_done"), L.nth("vector_stage_done"))
            conv_turn_scalar(L, m, B)
            act.sem_inc(m.sem("scalar_stage_done"), 1)
            act.wait_ge(m.sem("vector_stage_done"), L.nth("vector_stage_done"))
            filter_scalar(L, m, B)
            act.sem_inc(m.sem("scalar_stage_done"), 1)
            act.wait_ge(m.sem("vector_stage_done"), L.nth("vector_stage_done"))
            for order in range(2):
                act.sem_inc(m.sem("scalar_stage_done"), 1)
                act.wait_ge(m.sem("vector_stage_done"), L.nth("vector_stage_done"))
                filter_spectrum_scalar(L, m, B)
                act.sem_inc(m.sem("scalar_stage_done"), 1)
                act.wait_ge(m.sem("vector_stage_done"), L.nth("vector_stage_done"))
                read_banks(L, 8, never, None)
                act.sem_inc(m.sem("scalar_stage_done"), 1)
                act.wait_ge(m.sem("vector_stage_done"), L.nth("vector_stage_done"))
                if order == 0:
                    read_banks(L, 4, never, None)
                    act.sem_inc(m.sem("scalar_stage_done"), 1)
                    act.wait_ge(m.sem("vector_stage_done"), L.nth("vector_stage_done"))
                    read_banks(L, 4, always, copy(lambda g: B.z1f[:, g, :]))
                    act.sem_inc(m.sem("scalar_stage_done"), 1)
                    act.wait_ge(m.sem("vector_stage_done"), L.nth("vector_stage_done"))
            read_banks(L, 4, never, None)
            act.sem_inc(m.sem("scalar_stage_done"), 1)
            act.wait_ge(m.sem("vector_stage_done"), L.nth("vector_stage_done"))
            norm_scalar(L, m, chunk(B.z2f), lambda c: B.mix[:, 4 + c, :], 4)
            act.sem_inc(m.sem("scalar_stage_done"), 1)
            act.wait_ge(m.sem("vector_stage_done"), L.nth("vector_stage_done"))
            read_banks(L, 8, never, None)
            act.sem_inc(m.sem("scalar_stage_done"), 1)
            act.wait_ge(m.sem("vector_stage_done"), L.nth("vector_stage_done"))
            memory_scalar(L, m, B)
            act.sem_inc(m.sem("scalar_stage_done"), 1)
            act.wait_ge(m.sem("vector_stage_done"), L.nth("vector_stage_done"))
            attention_scalar(L, m, B.matt)
            act.sem_inc(m.sem("scalar_stage_done"), 1)
            act.wait_ge(m.sem("vector_stage_done"), L.nth("vector_stage_done"))
            read_banks(L, 8, never, None)
            act.sem_inc(m.sem("scalar_stage_done"), 1)
            act.wait_ge(m.sem("vector_stage_done"), L.nth("vector_stage_done"))
            route_scalar(L, m, B)
            act.sem_inc(m.sem("scalar_stage_done"), 1)
            act.wait_ge(m.sem("vector_stage_done"), L.nth("vector_stage_done"))
            swiglu_scalar(L, m, "moe", GROUPS * EXPERTS, B.gate, [NX], B.weight)
            act.sem_inc(m.sem("scalar_stage_done"), 1)
            act.wait_ge(m.sem("vector_stage_done"), L.nth("vector_stage_done"))
            norm_scalar(L, m, chunk(m.x), chunk(B.h), KC)
            act.sem_inc(m.sem("scalar_stage_done"), 1)
            act.wait_ge(m.sem("vector_stage_done"), L.nth("vector_stage_done"))

            for i in range(2):
                mod_scalar(L, m, i)
                act.sem_inc(m.sem("scalar_stage_done"), 1)
                act.wait_ge(m.sem("vector_stage_done"), L.nth("vector_stage_done"))
                modnorm_scalar(L, m, R)
                act.sem_inc(m.sem("scalar_stage_done"), 1)
                act.wait_ge(m.sem("vector_stage_done"), L.nth("vector_stage_done"))
                if i == 0:
                    qkv_read(L, m, R, odd, lambda o, p: act.activation(o, p, ACT.Copy))
                    act.sem_inc(m.sem("scalar_stage_done"), 1)
                    act.wait_ge(m.sem("vector_stage_done"), L.nth("vector_stage_done"))
                    head_norm_scalar(L, m, R)
                    act.sem_inc(m.sem("scalar_stage_done"), 1)
                    act.wait_ge(m.sem("vector_stage_done"), L.nth("vector_stage_done"))
                    for att in (R.att, R.catt):
                        attention_scalar(L, m, att)
                        act.sem_inc(m.sem("scalar_stage_done"), 1)
                        act.wait_ge(m.sem("vector_stage_done"), L.nth("vector_stage_done"))
                    read_banks(L, 16, never, None)
                    act.sem_inc(m.sem("scalar_stage_done"), 1)
                    act.wait_ge(m.sem("vector_stage_done"), L.nth("vector_stage_done"))
                else:
                    act.sem_inc(m.sem("scalar_stage_done"), 1)
                    act.wait_ge(m.sem("vector_stage_done"), L.nth("vector_stage_done"))
                    for dst in (R.pk, R.pv):
                        read_banks(L, 16, always, copy(lambda g: chunk(dst, *BOTH[g % 2])(g // 2)))
                        act.sem_inc(m.sem("scalar_stage_done"), 1)
                        act.wait_ge(m.sem("vector_stage_done"), L.nth("vector_stage_done"))
                    for dst, f in ((R.tw, ACT.Tanh), (R.ta, ACT.Copy)):
                        read_banks(L, 2, always, lambda g, ps: act.activation(
                            dst[:, BOTH[g][0]:BOTH[g][0] + BOTH[g][1]], ps[:, :BOTH[g][1]], f))
                        act.sem_inc(m.sem("scalar_stage_done"), 1)
                        act.wait_ge(m.sem("vector_stage_done"), L.nth("vector_stage_done"))
                    read_banks(L, 1, always, lambda g, ps: act.activation(R.tg, ps, ACT.Sigmoid))
                    act.sem_inc(m.sem("scalar_stage_done"), 1)
                    act.wait_ge(m.sem("vector_stage_done"), L.nth("vector_stage_done"))
                    act.wait_ge(m.sem("spilled"), 32)
                    read_banks(L, 8, always, copy(lambda g: R.pr[:, g, :]))
                    act.sem_inc(m.sem("scalar_stage_done"), 1)
                    act.wait_ge(m.sem("vector_stage_done"), L.nth("vector_stage_done"))
                    for j in range(KC):
                        pair_scalar(L, m, R, j)
                        act.sem_inc(m.sem("scalar_stage_done"), 1)
                        act.wait_ge(m.sem("vector_stage_done"), L.nth("vector_stage_done"))
                        for d in range(2):
                            decay_scalar(L, m, R, j, d)
                            act.sem_inc(m.sem("scalar_stage_done"), 1)
                            act.wait_ge(m.sem("vector_stage_done"), L.nth("vector_stage_done"))
                            tile_scalar(L, m, R, j, d)
                            act.sem_inc(m.sem("scalar_stage_done"), 1)
                            act.wait_ge(m.sem("vector_stage_done"), L.nth("vector_stage_done"))
                        readout_scalar(L, m, R, j)
                        act.sem_inc(m.sem("scalar_stage_done"), 1)
                        act.wait_ge(m.sem("vector_stage_done"), L.nth("vector_stage_done"))
                    read_banks(L, 8, never, None)
                    act.sem_inc(m.sem("scalar_stage_done"), 1)
                    act.wait_ge(m.sem("vector_stage_done"), L.nth("vector_stage_done"))
                modnorm_scalar(L, m, R, i == 0)
                act.sem_inc(m.sem("scalar_stage_done"), 1)
                act.wait_ge(m.sem("vector_stage_done"), L.nth("vector_stage_done"))
                swiglu_scalar(L, m, f"ffn{i}", FF // 256, R.gate, BOTH[:2 - i])
                act.sem_inc(m.sem("scalar_stage_done"), 1)
                act.wait_ge(m.sem("vector_stage_done"), L.nth("vector_stage_done"))
            norm_scalar(L, m, chunk(m.x), chunk(R.h, 0, T), KC)
            act.sem_inc(m.sem("scalar_stage_done"), 1)
            act.wait_ge(m.sem("vector_stage_done"), L.nth("vector_stage_done"))

        @block.vector
        def _(dve):
            L = Lane(m, dve, "vector")
            L.eng.wait_ge(m.sem("inputs_landed"), L.nth("inputs_landed", 64))
            mix_in_vector(L, m, B)
            dve.sem_inc(m.sem("vector_stage_done"), 1)
            dve.wait_ge(m.sem("scalar_stage_done"), L.nth("scalar_stage_done"))
            latent_vector(L, m, B)
            dve.sem_inc(m.sem("vector_stage_done"), 1)
            dve.wait_ge(m.sem("scalar_stage_done"), L.nth("scalar_stage_done"))
            latent_attention_vector(L, m, B)
            dve.sem_inc(m.sem("vector_stage_done"), 1)
            dve.wait_ge(m.sem("scalar_stage_done"), L.nth("scalar_stage_done"))
            norm_vector(L, m, chunk(B.o), chunk(B.mix), 4, gains(m, "aout_g"))
            conv_vector(L, m, B)
            dve.sem_inc(m.sem("vector_stage_done"), 1)
            dve.wait_ge(m.sem("scalar_stage_done"), L.nth("scalar_stage_done"))
            read_banks(L, 8, never, None)
            dve.sem_inc(m.sem("vector_stage_done"), 1)
            dve.wait_ge(m.sem("scalar_stage_done"), L.nth("scalar_stage_done"))
            L.eng.sem_inc(m.sem("room_for_dft"), 1)
            L.nth("room_for_dft")
            filter_vector(L, m, B)
            dve.sem_inc(m.sem("vector_stage_done"), 1)
            dve.wait_ge(m.sem("scalar_stage_done"), L.nth("scalar_stage_done"))
            for order in range(2):
                parts_vector(L, m, B, order)
                dve.sem_inc(m.sem("vector_stage_done"), 1)
                dve.wait_ge(m.sem("scalar_stage_done"), L.nth("scalar_stage_done"))
                read_banks(L, 8, never, None)
                dve.sem_inc(m.sem("vector_stage_done"), 1)
                dve.wait_ge(m.sem("scalar_stage_done"), L.nth("scalar_stage_done"))
                product_vector(L, m, B)
                dve.sem_inc(m.sem("vector_stage_done"), 1)
                dve.wait_ge(m.sem("scalar_stage_done"), L.nth("scalar_stage_done"))
                if order == 0:
                    inverse0_vector(L, m, B)
                    dve.sem_inc(m.sem("vector_stage_done"), 1)
                    dve.wait_ge(m.sem("scalar_stage_done"), L.nth("scalar_stage_done"))
                    read_banks(L, 4, never, None)
                    dve.sem_inc(m.sem("vector_stage_done"), 1)
                    dve.wait_ge(m.sem("scalar_stage_done"), L.nth("scalar_stage_done"))
            inverse1_vector(L, m, B)
            dve.sem_inc(m.sem("vector_stage_done"), 1)
            dve.wait_ge(m.sem("scalar_stage_done"), L.nth("scalar_stage_done"))
            norm_vector(L, m, chunk(B.z2f), lambda c: B.mix[:, 4 + c, :], 4, gains(m, "hyout_g"))
            dve.sem_inc(m.sem("vector_stage_done"), 1)
            dve.wait_ge(m.sem("scalar_stage_done"), L.nth("scalar_stage_done"))
            read_banks(L, 8, always, add_to_x(L, m))
            dve.sem_inc(m.sem("vector_stage_done"), 1)
            dve.wait_ge(m.sem("scalar_stage_done"), L.nth("scalar_stage_done"))
            L.eng.sem_inc(m.sem("room_for_mem"), 1)
            L.nth("room_for_mem")
            memory_vector(L, m, B)
            dve.sem_inc(m.sem("vector_stage_done"), 1)
            dve.wait_ge(m.sem("scalar_stage_done"), L.nth("scalar_stage_done"))
            attention_vector(L, m, B.matt, lambda h, mt: B.mo[:, 2 * h + mt, :])
            dve.sem_inc(m.sem("vector_stage_done"), 1)
            dve.wait_ge(m.sem("scalar_stage_done"), L.nth("scalar_stage_done"))
            read_banks(L, 8, always, add_to_x(L, m))
            dve.sem_inc(m.sem("vector_stage_done"), 1)
            dve.wait_ge(m.sem("scalar_stage_done"), L.nth("scalar_stage_done"))
            route_vector(L, m, B)
            dve.sem_inc(m.sem("vector_stage_done"), 1)
            dve.wait_ge(m.sem("scalar_stage_done"), L.nth("scalar_stage_done"))
            add = add_to_x(L, m)
            swiglu_vector(L, m, GROUPS * EXPERTS, B, [NX], lambda c, g, ps: add(c, ps), B.weight)
            dve.sem_inc(m.sem("vector_stage_done"), 1)
            dve.wait_ge(m.sem("scalar_stage_done"), L.nth("scalar_stage_done"))
            norm_vector(L, m, chunk(m.x), chunk(m.x), KC, gains(m, "fin_g"))
            dve.sem_inc(m.sem("vector_stage_done"), 1)
            dve.wait_ge(m.sem("scalar_stage_done"), L.nth("scalar_stage_done"))

            for i in range(2):
                mod_vector(L, m, i)
                dve.sem_inc(m.sem("vector_stage_done"), 1)
                dve.wait_ge(m.sem("scalar_stage_done"), L.nth("scalar_stage_done"))
                modnorm_vector(L, m, R, 0)
                dve.sem_inc(m.sem("vector_stage_done"), 1)
                dve.wait_ge(m.sem("scalar_stage_done"), L.nth("scalar_stage_done"))
                if i == 0:
                    L.eng.sem_inc(m.sem("room_for_rope"), 1)
                    L.nth("room_for_rope")
                    qkv_read(L, m, R, even, lambda o, p: dve.tensor_copy(o, p))
                    dve.sem_inc(m.sem("vector_stage_done"), 1)
                    dve.wait_ge(m.sem("scalar_stage_done"), L.nth("scalar_stage_done"))
                    head_norm_vector(L, m, R)
                    dve.sem_inc(m.sem("vector_stage_done"), 1)
                    dve.wait_ge(m.sem("scalar_stage_done"), L.nth("scalar_stage_done"))
                    for ctx_side in (False, True):
                        gqa_vector(L, m, R, ctx_side)
                        dve.sem_inc(m.sem("vector_stage_done"), 1)
                        dve.wait_ge(m.sem("scalar_stage_done"), L.nth("scalar_stage_done"))
                    add2 = gated_add(L, m, 2)
                    read_banks(L, 16, always, lambda g, ps: add2(g // 2, g % 2, ps))
                    dve.sem_inc(m.sem("vector_stage_done"), 1)
                    dve.wait_ge(m.sem("scalar_stage_done"), L.nth("scalar_stage_done"))
                else:
                    shift_vector(L, m, R)
                    dve.sem_inc(m.sem("vector_stage_done"), 1)
                    dve.wait_ge(m.sem("scalar_stage_done"), L.nth("scalar_stage_done"))
                    for which, banks in ((2, 16), (3, 16), (1, 2), (4, 2), (5, 1), (0, 8)):
                        lerp_vector(L, m, R, which)
                        read_banks(L, banks, never, None)
                        dve.sem_inc(m.sem("vector_stage_done"), 1)
                        dve.wait_ge(m.sem("scalar_stage_done"), L.nth("scalar_stage_done"))
                        if which == 3:
                            L.eng.sem_inc(m.sem("kv_ready"), 1)
                            L.nth("kv_ready")
                    L.eng.sem_inc(m.sem("r_ready"), 1)
                    L.nth("r_ready")
                    L.eng.wait_ge(m.sem("wkv_tables"), L.nth("wkv_tables", 48))
                    for j in range(KC):
                        pair_vector(L, m, R, j)
                        dve.sem_inc(m.sem("vector_stage_done"), 1)
                        dve.wait_ge(m.sem("scalar_stage_done"), L.nth("scalar_stage_done"))
                        for d in range(2):
                            decay_vector(L, m, R, j, d)
                            dve.sem_inc(m.sem("vector_stage_done"), 1)
                            dve.wait_ge(m.sem("scalar_stage_done"), L.nth("scalar_stage_done"))
                            tile_vector(L, m, R, j, d)
                            dve.sem_inc(m.sem("vector_stage_done"), 1)
                            dve.wait_ge(m.sem("scalar_stage_done"), L.nth("scalar_stage_done"))
                        readout_vector(L, m, R, j)
                        dve.sem_inc(m.sem("vector_stage_done"), 1)
                        dve.wait_ge(m.sem("scalar_stage_done"), L.nth("scalar_stage_done"))
                        if j < KC - 2:
                            L.eng.sem_inc(m.sem("pair_read_out"), 1)
                            L.nth("pair_read_out")
                    read_banks(L, 8, always, add_to_x(L, m, mod_col(m, 2, 0)))
                    dve.sem_inc(m.sem("vector_stage_done"), 1)
                    dve.wait_ge(m.sem("scalar_stage_done"), L.nth("scalar_stage_done"))
                modnorm_vector(L, m, R, 1, i == 0)
                dve.sem_inc(m.sem("vector_stage_done"), 1)
                dve.wait_ge(m.sem("scalar_stage_done"), L.nth("scalar_stage_done"))
                swiglu_vector(L, m, FF // 256, R, BOTH[:2 - i], gated_add(L, m, 5))
                dve.sem_inc(m.sem("vector_stage_done"), 1)
                dve.wait_ge(m.sem("scalar_stage_done"), L.nth("scalar_stage_done"))
            norm_vector(L, m, chunk(m.x), chunk(m.x), KC, gains(m, "fin2_g"))
            dve.sem_inc(m.sem("vector_stage_done"), 1)
            dve.wait_ge(m.sem("scalar_stage_done"), L.nth("scalar_stage_done"))
            L.eng.sem_inc(m.sem("result"), 1)
            L.nth("result")


def kernel(**inputs):
    import numpy as _np
    import concourse.bacc as _bacc
    from concourse.bass_utils import run_bass_kernel_spmd as _run

    a = {k: _np.asarray(v) for k, v in inputs.items()}
    arrays = {"wall": pack_slabs(a), "vecs": pack_vectors(a), "tabs": tables(), "x": feature_major(a["x"][0]),
              "ctx": feature_major(a["ctx_2"][0]), "mem": feature_major(a["mem"][0])}
    nc = _bacc.Bacc("TRN2", target_bir_lowering=False, num_devices=1)
    dram = {k: nc.dram_tensor(f"in_{k}", v.shape, F32, kind="ExternalInput").ap() for k, v in arrays.items()}
    dram["out"] = nc.dram_tensor("out_0", (P, KC, T), F32, kind="ExternalOutput").ap()
    dram["spill"] = nc.dram_tensor("spill", (P, KC, 2048), F32).ap()
    build(nc, dram)
    r = _run(nc, [{f"in_{k}": v for k, v in arrays.items()}], core_ids=[0])
    out = r.results[0]["out_0"]
    return _np.ascontiguousarray(out.transpose(2, 1, 0).reshape(1, T, D))
```

```python
from contextlib import ExitStack

import numpy as np

import concourse.bass as bass
from concourse import mybir
from concourse.alu_op_type import AluOpType as ALU

F32R = mybir.dt.float32r
F32 = mybir.dt.float32
ACT = mybir.ActivationFunctionType
AX = mybir.AxisListType.X

P = 128
D = 1024
KC = D // P
T = 512
C = 256
TC = T + C
EPS = 1e-6
BANK = 512
SLAB = 2048
SLOTS = 5

NH1, NOPE, ROT, DV = 8, 64, 32, 64
QK = NOPE + ROT
QR, KVR = 256, 128
HW = 512
L2 = 2 * T
GROUPS, EXPERTS = 4, 8
MEM_H, MEM_D = 4, 256
QH, KVH, HD = 16, 4, 64
FF = 2816
CH = 64
DECAY_SCALE = -float(np.exp(-0.5))
GN_EPS = 64e-5


def vector_columns():
    at, out = 0, {}
    for name, n in [("mix_g", 8), ("qn_g", 2), ("kvn_g", 1), ("aout_g", 4), ("hyout_g", 4), ("cross_g", 8),
                    ("mem_g", 8), ("ffn_g", 8), ("fin_g", 8), ("conv_w", 36), ("conv_b", 12), ("hb1", 1),
                    ("hf0", 1), ("hb2", 1), ("hf1", 1), ("skip1", 4), ("hw1", 64), ("hw2", 64),
                    ("b_route", 36), ("cond", 16), ("mod_b", 96), ("n1_g", 16), ("n2_g", 16), ("q_gain", 1),
                    ("k_gain", 1), ("lerp", 48), ("w0", 16), ("a0", 16), ("k_k", 8), ("k_a", 8), ("r_k", 8),
                    ("ln_g", 8), ("ln_b", 8), ("fin2_g", 8)]:
        out[name] = (at, n)
        at += n
    return out, at


VCOL, NVEC = vector_columns()


def table_columns():
    at, out = 0, {}
    for name, n in [("ident", 128), ("ones", 128), ("heads64", 128), ("swap16", 128), ("pick2", 2), ("eps", 1), ("gn_eps", 1),
                    ("kk_eps", 1), ("dft_scale", 2), ("t01", 4), ("expert_rank", 8), ("resident", 0),
                    ("cos96", 512), ("sin96", 512),
                    ("dft_c", 2048), ("dft_s", 2048), ("alt_col", 128), ("alt_row", 512), ("zemb", 512),
                    ("cos_ax", 512), ("sin_ax", 512),
                    ("eye", 64), ("masks", 16 * 64), ("scan_keep", TC)]:
        out[name] = (at, n)
        at += n
    return out, at


TCOL, NTAB = table_columns()
RESIDENT = TCOL["resident"][0]


def tables():
    t = np.zeros((P, NTAB), np.float32)

    def put(name, a):
        c, n = TCOL[name]
        a = np.asarray(a, np.float64)
        t[:a.shape[0], c:c + n] = a.reshape(a.shape[0], n)

    r = np.arange(P)
    put("ident", np.eye(P))
    put("ones", np.ones((P, P)))
    put("heads64", (r[:, None] // 64 == r[None] // 64))
    put("swap16", (r[:, None] == (r[None] ^ 16)))
    put("pick2", r[:, None] % 32 == np.arange(2)[None])
    put("eps", np.full((P, 1), EPS))
    put("gn_eps", np.full((P, 1), GN_EPS))
    put("kk_eps", np.full((P, 1), 1e-24))
    sc = np.full((P, 2), 2.0 / L2)
    sc[0, 0] = 1.0 / L2
    put("dft_scale", sc)
    put("t01", -(np.arange(T).reshape(4, P).T / T))
    put("expert_rank", np.tile(8.0 - np.arange(8), (P, 1)))
    half = ROT // 2
    f32 = np.float32
    inv = f32(10000.0) ** (-np.arange(half, dtype=f32) / f32(half))
    ang = (np.arange(T, dtype=f32)[:, None] * inv[None]).astype(np.float64)
    co, si = np.ones((QK, T)), np.zeros((QK, T))
    co[NOPE:NOPE + half] = co[NOPE + half:] = np.cos(ang).T
    si[NOPE:NOPE + half], si[NOPE + half:] = -np.sin(ang).T, np.sin(ang).T
    put("cos96", co)
    put("sin96", si)
    k = np.arange(T)
    w = 2 * np.pi * ((k[:, None] * k[None]) % L2) / L2
    put("dft_c", np.cos(w).reshape(4, P, T).transpose(1, 0, 2))
    put("dft_s", -np.sin(w).reshape(4, P, T).transpose(1, 0, 2))
    alt = 1.0 - 2.0 * (np.arange(T) % 2)
    a = np.zeros((P, P))
    a[:, 0] = alt[:P]
    put("alt_col", a)
    a = np.zeros((P, T))
    a[0] = alt
    put("alt_row", a)
    bands = np.linspace(1e-4, 15, 16, dtype=f32)
    tt = np.arange(T, dtype=f32)
    an = (f32(2.0 * np.pi) * tt[:, None] * bands[None] / f32(T)).astype(np.float64)
    put("zemb", np.concatenate([(tt / T)[:, None], np.cos(an), -np.sin(an)], 1).T)
    inv = f32(10000.0) ** (-np.arange(16, dtype=f32) / f32(16))
    row, col = (np.arange(T) // 64).astype(f32), (np.arange(T) % 64).astype(f32)
    co, si = np.zeros((P, T)), np.zeros((P, T))
    for p in range(P):
        an = ((row, col)[p % 64 // 32] * inv[p % 16]).astype(np.float64)
        co[p], si[p] = np.cos(an), np.sin(an) * (1 if p % 32 // 16 else -1)
    put("cos_ax", co)
    put("sin_ax", si)
    ri, ci = (r % 64)[:, None], np.arange(64)[None]
    put("eye", ri == ci)
    ms = [ri < ci, ri > ci, ri <= ci, ri >= ci]
    for m in (1, 2, 4, 8, 16, 32):
        low = (ri // (2 * m) == ci // (2 * m)) & (ri % (2 * m) >= m) & (ci % (2 * m) < m)
        up = (ri // (2 * m) == ci // (2 * m)) & (ci % (2 * m) >= m) & (ri % (2 * m) < m)
        ms += [low, up]
    put("masks", np.stack(ms, 1))
    put("scan_keep", np.tile((np.arange(TC) % CH != 0), (P, 1)))
    return t


SWAP_ROT = list(range(NOPE)) + list(range(NOPE + 16, NOPE + 32)) + list(range(NOPE, NOPE + 16))


GUESTS = {"moe": GROUPS * EXPERTS + 1, "wo0": 3, "ffn0": FF // 256 + 1}
assert sum(GUESTS.values()) == 48


def slab_layout():
    at = {}
    total = 0

    def use(name):
        nonlocal total
        at.setdefault(name, []).append(total)
        total += 1

    def plain(*runs):
        for name, n in runs:
            for i in range(n):
                use(name)
                if i < GUESTS.get(name, 0):
                    use("mod")

    def swiglu(name, n):
        for i in range(n + 1):
            if i < n:
                use(name + "_gate")
                use(name + "_up")
            if i > 0:
                use(name + "_down")
            if i < GUESTS.get(name, 0):
                use("mod")

    plain(("in_q", 1), ("in_kv", 1), ("in_krs", 1), ("in_hy", 6), ("uq", 1), ("uqs", 1), ("ukv", 1), ("decay", 1),
          ("hw3", 1), ("skip0", 1), ("out", 4), ("mk", 4), ("mv", 4), ("mq", 4), ("mo", 4), ("route", 1))
    swiglu("moe", GROUPS * EXPERTS)
    plain(("qkv_q", 4), ("qkv_k", 2), ("qkv_v", 1), ("wo0", 4))
    swiglu("ffn0", FF // 256)
    plain(("rw_k", 4), ("rw_v", 4), ("lora1", 1), ("g1", 1), ("rw_r", 4), ("lora2", 1), ("g2", 1), ("wo1", 4))
    swiglu("ffn1", FF // 256)
    return at, total


SLABS, NSLAB = slab_layout()


def pack_slabs(a):
    wall = np.zeros((NSLAB, P, SLAB), np.float32)

    def put(name, i, w, col=0):
        k, m = w.shape
        kc = -(-k // P)
        if k % P:
            wall[SLABS[name][i], :k, col:col + m] = w
        else:
            wall[SLABS[name][i], :, col:col + kc * m] = w.reshape(kc, P, m).transpose(1, 0, 2).reshape(P, kc * m)

    def put_all(name, w, cols=256):
        for i in range(w.shape[1] // cols):
            put(name, i, w[:, i * cols:(i + 1) * cols])

    def put_swiglu(name, i, wg, wu, wd):
        put(name + "_gate", i, wg)
        put(name + "_up", i, wu)
        put(name + "_down", i, wd)

    w = a["w_in"][0]
    put("in_q", 0, w[:, :QR])
    put("in_kv", 0, w[:, QR:QR + KVR])
    kr = w[:, QR + KVR - NOPE:QR + KVR + ROT]
    put("in_kv", 0, kr, KC * KVR)
    put("in_krs", 0, kr[:, SWAP_ROT])
    put_all("in_hy", w[:, QR + KVR + ROT:])
    uq = a["w_uq"][0].reshape(QR, NH1, QK)
    put("uq", 0, uq.reshape(QR, -1))
    put("uqs", 0, uq[:, :, SWAP_ROT].reshape(QR, -1))
    ukv = a["w_ukv"][0].reshape(KVR, NH1, 2, 64).transpose(0, 2, 1, 3)
    put("ukv", 0, ukv.reshape(KVR, -1))
    put("decay", 0, np.broadcast_to(a["hy_decay"][0], (P, 2048)))
    put("hw3", 0, np.concatenate([a["hy_w3"][0], a["hy_b3"]], 0))
    put("skip0", 0, np.broadcast_to(a["hy_skip"][0, 0], (P, HW)))
    put_all("out", a["w_out"][0])
    put_all("mk", a["w_mkv"][0][:, :D])
    put_all("mv", a["w_mkv"][0][:, D:])
    put_all("mq", a["w_mq"][0])
    put_all("mo", a["w_mo"][0])
    put("route", 0, np.concatenate([a["w_route_group"][0], a["w_route_expert"][0]], 1))
    for e in range(GROUPS * EXPERTS):
        g, x = divmod(e, EXPERTS)
        put_swiglu("moe", e, a["w_gate"][0, g, x], a["w_up"][0, g, x], a["w_down"][0, g, x])
    for i in range(2):
        for s in range(24):
            put("mod", 24 * i + s, a["mod_w_2"][i][:, s * 256:(s + 1) * 256])
        for j in range(FF // 256):
            s = slice(256 * j, 256 * j + 256)
            put_swiglu(f"ffn{i}", j, a["ffn_wg_2"][i][:, s], a["ffn_wu_2"][i][:, s], a["ffn_wd_2"][i][s])
    w = a["attn_wqkv_2"][0]
    put_all("qkv_q", w[:, :D])
    k2 = np.repeat(w[:, D:D + 256].reshape(D, KVH, 1, HD), 2, 2).reshape(D, 512)
    put_all("qkv_k", k2)
    put_all("qkv_v", w[:, D + 256:])
    put_all("wo0", a["attn_wo_2"][0])
    put_all("rw_r", a["rwkv_wrkv_2"][0, 0])
    put_all("rw_k", a["rwkv_wrkv_2"][0, 1])
    put_all("rw_v", a["rwkv_wrkv_2"][0, 2])
    put("lora1", 0, a["rwkv_w1_2"][0].transpose(1, 0, 2).reshape(D, P))
    put("lora1", 0, a["rwkv_a1_2"][0].transpose(1, 0, 2).reshape(D, P), D)
    put("g1", 0, a["rwkv_g1_2"][0])
    put("lora2", 0, a["rwkv_w2_2"][0].reshape(P, D))
    put("lora2", 0, a["rwkv_a2_2"][0].reshape(P, D), D)
    put("g2", 0, a["rwkv_g2_2"][0])
    put_all("wo1", a["rwkv_wo_2"][0])
    return wall


def pack_vectors(a):
    v = np.zeros((P, NVEC), np.float32)

    def put(name, x, at=0):
        x = np.asarray(x)
        c = VCOL[name][0] + at
        if x.ndim == 1:
            x = x.reshape(-1, P).T if x.size >= P else x[:, None]
        v[:x.shape[0], c:c + x.shape[1]] = x

    for name, src in [("mix_g", "mix_norm_g"), ("qn_g", "q_norm_g"), ("kvn_g", "kv_norm_g"), ("aout_g", "attn_out_g"),
                      ("hyout_g", "hy_out_g"), ("cross_g", "cross_norm_g"), ("mem_g", "mem_norm_g"),
                      ("ffn_g", "ffn_norm_g"), ("conv_b", "hy_conv_b"), ("hb1", "hy_b1"), ("hb2", "hy_b2"),
                      ("k_k", "rwkv_k_k_2"), ("k_a", "rwkv_k_a_2"),
                      ("ln_g", "rwkv_ln_g_2"), ("ln_b", "rwkv_ln_b_2")]:
        put(name, a[src][0])
    put("r_k", a["rwkv_r_k_2"][0].reshape(-1))
    put("fin_g", a["final_norm_g"])
    put("fin2_g", a["final_g_2"])
    for j in range(3):
        put("conv_w", a["hy_conv_w"][0, j], 12 * j)
    put("hf0", a["hy_freq"][0, 0])
    put("hf1", a["hy_freq"][0, 1])
    put("skip1", a["hy_skip"][0, 1])
    put("hw1", a["hy_w1"][0])
    put("hw2", a["hy_w2"][0])
    put("b_route", np.broadcast_to(np.concatenate([a["b_route_group"][0], a["b_route_expert"][0]]), (P, 36)))
    put("cond", np.stack([a["c_2"][0].reshape(KC, P), a["c_ctx_2"].reshape(KC, P)], 2).transpose(1, 0, 2).reshape(P, 16))
    for i in range(2):
        put("mod_b", a["mod_b_2"][i], 48 * i)
        put("n1_g", a["norm1_g_2"][i], 8 * i)
        put("n2_g", a["norm2_g_2"][i], 8 * i)
        put("w0", a["rwkv_w0_2"][0, i], 8 * i)
        put("a0", a["rwkv_a0_2"][0, i], 8 * i)
    put("q_gain", np.concatenate([a["attn_q_gain_2"][0]] * 2))
    put("k_gain", np.concatenate([a["attn_k_gain_2"][0]] * 2))
    for j in range(6):
        put("lerp", a["rwkv_mix_2"][0, j], 8 * j)
    return v


def feature_major(x):
    return np.ascontiguousarray(x.T.reshape(KC, P, -1).transpose(1, 0, 2))


class Lane:

    def __init__(self, m, eng, name):
        self.m, self.eng, self.name = m, eng, name
        self.step, self.steps = m.sem(f"{name}_step"), 0
        self.counts = {}
        self.bank_at, self.filled, self.freed = 0, [0] * 8, [0] * 8
        self.slab_at, self.mods = 0, 0

    def next_step(self):
        self.steps += 1
        return self.steps

    def nth(self, what, n=1):
        self.counts[what] = self.counts.get(what, 0) + n
        return self.counts[what]

    def next_bank(self, n=1):
        if n == 2 and self.bank_at % 8 == 7:
            self.bank_at += 1
        b = self.bank_at % 8
        self.bank_at += n
        self.bank_full, self.bank_free = self.m.bank_full[b], self.m.bank_free[b]
        self.bank_free2 = self.m.bank_free[(b + 1) % 8]
        self.bank_frees = [(self.m.bank_free[b + i], self.freed[b + i]) for i in range(n) if self.freed[b + i]]
        self.filled[b] += 1
        for i in range(n):
            self.freed[b + i] += 1
        self.fill = self.filled[b]
        return self.m.psum[:, b * BANK:(b + n) * BANK]

    def next_slab(self, name, i=0):
        n = self.slab_at
        assert n == SLABS[name][i], (name, i, n)
        self.slab_at += 1
        self.landed, self.landings = self.m.slab_landed[n % SLOTS], 16 * (n // SLOTS + 1)
        self.high, self.low = self.m.high[:, n % SLOTS, :], self.m.low[:, n % SLOTS, :]
        return self.m.ring[:, n % SLOTS, :]


class Mem:

    def __init__(self, nc, ctx):
        self.nc, self.ctx, self.sems = nc, ctx, {}

    def sem(self, name):
        if name not in self.sems:
            self.sems[name] = self.ctx.enter_context(self.nc.semaphore(name))
        return self.sems[name]

    def sb(self, name, shape):
        return self.ctx.enter_context(self.nc.sbuf_tensor(name, shape, F32))

    def rounded(self, name, off, *shape):
        assert off + int(np.prod(shape)) <= ARENA, (name, off)
        return self.nc.alloc_sbuf_tensor_at(name, [P, *shape], F32R, offset=self.arena_place + 4 * off)

    def at(self, off, *shape, parts=P):
        n = int(np.prod(shape))
        assert off + n <= ARENA, (off, shape)
        v = self.arena[0:parts, off:off + n]
        if len(shape) == 2:
            v = v.rearrange("p (a b) -> p a b", a=shape[0])
        if len(shape) == 3:
            v = v.rearrange("p (a b c) -> p a b c", a=shape[0], b=shape[1])
        return v

    def slab_of(self, L, name):
        n = SLABS[name][0]
        L.eng.wait_ge(self.slab_landed[n % SLOTS], 16 * (n // SLOTS + 1))
        return self.ring[:, n % SLOTS, :]

    def vec(self, name, i=0, n=1, parts=P):
        c = VCOL[name][0] + i
        return self.vecs[0:parts, c:c + n]

    def tab(self, name, i=0, n=None, parts=P):
        c, w = TCOL[name]
        return self.tabs[0:parts, c + i:c + i + (w if n is None else n)]


ARENA = 34624
HIGH = ARENA - SLOTS * SLAB - 832
NX, NC_ = (0, T), (T, C)


def matmuls(L, out, pairs):
    for i, (a, b) in enumerate(pairs):
        last = L.eng.matmul(out, a, b, start=(i == 0), stop=(i == len(pairs) - 1))
    return last


def split_matmuls(L, m, out, terms, ready=None):
    for i, (a_hi, a_lo, b_hi, b_lo) in enumerate(terms):
        if ready is not None:
            L.eng.wait_ge(m.sem(ready), L.nth(ready))
        L.eng.matmul(out, a_hi, b_hi, start=(i == 0), stop=False)
        L.eng.matmul(out, a_hi, b_lo, start=False, stop=False)
        last = L.eng.matmul(out, a_lo, b_hi, start=False, stop=(i == len(terms) - 1))
    return last


def round_slab(L, m, n):
    L.eng.wait_ge(m.slab_landed[n % SLOTS], 16 * (n // SLOTS + 1))
    L.eng.activation(m.high[:, n % SLOTS, :], m.ring[:, n % SLOTS, :], ACT.Copy).then_inc(m.sem("slab_rounded"), 1)


def split_slabs(L, m, name):
    for n in sorted(SLABS[name + "_gate"] + SLABS[name + "_up"] + SLABS[name + "_down"]):
        L.eng.wait_ge(m.sem("slab_rounded"), L.nth("slab_rounded"))
        L.eng.tensor_tensor(m.low[:, n % SLOTS, :], m.ring[:, n % SLOTS, :], m.high[:, n % SLOTS, :].bitcast(F32),
                            ALU.subtract).then_inc(m.sem("slab_split"), 1)


def split_h_vector(L, m, S, lo, wd):
    h = slice(lo, lo + wd)
    for c in range(KC):
        split_vector(L, m, S.h[:, c, h], S.h_high[:, c, h], S.h_low[:, c, h], "h_split")


def split_vector(L, m, x, high, low, what):
    L.eng.tensor_copy(high, x).then_inc(L.step, 1)
    L.eng.wait_ge(L.step, L.next_step())
    L.eng.tensor_tensor(low, x, high.bitcast(F32), ALU.subtract).then_inc(m.sem(what), 1)
    L.nth(what)


def norm_tensor(L, m, sq, n, lo=0):
    ps = L.next_bank()
    for bank_free, count in L.bank_frees:
        L.eng.wait_ge(bank_free, count)
    w = sq(0).shape[1]
    for c in range(n):
        L.eng.wait_ge(m.sem("squares"), L.nth("squares"))
        last = L.eng.matmul(ps[:, :w], m.tab("ones"), sq(c), start=(c == 0), stop=(c == n - 1))
    last.then_inc(L.bank_full, 1)


def norm_scalar(L, m, src, sq, n, eps="eps", root_used=False):
    for c in range(n):
        L.eng.activation(sq(c), src(c), ACT.Square).then_inc(m.sem("squares"), 1)
        L.eng.wait_ge(m.sem("squares"), L.nth("squares"))
    w = sq(0).shape[1]
    ps = L.next_bank()
    L.eng.wait_ge(L.bank_full, L.fill)
    if root_used:
        L.eng.wait_ge(m.sem("root_used"), L.nth("root_used"))
    L.eng.activation(m.root[:, :w], ps[:, :w], ACT.Sqrt, bias=m.tab(eps), scale=1.0 / (n * P)).then_inc(L.step, 1)
    L.eng.wait_ge(L.step, L.next_step())
    L.eng.sem_inc(L.bank_free, 1)
    L.eng.sem_inc(m.sem("root"), 1)
    L.nth("root")


def norm_vector(L, m, src, dst, n, gain, bias=None, each=False):
    L.next_bank()
    w = src(0).shape[1]
    L.eng.wait_ge(m.sem("root"), L.nth("root"))
    L.eng.reciprocal(m.root[:, :w], m.root[:, :w]).then_inc(L.step, 1)
    L.eng.wait_ge(L.step, L.next_step())
    for c in range(n):
        L.eng.scalar_tensor_tensor(dst(c), src(c), gain(c), m.root[:, :w], ALU.mult, ALU.mult).then_inc(L.step, 1)
        L.eng.wait_ge(L.step, L.next_step())
        if bias:
            L.eng.tensor_scalar(dst(c), dst(c), bias(c), None, ALU.add).then_inc(L.step, 1)
            L.eng.wait_ge(L.step, L.next_step())
        if each:
            L.eng.sem_inc(m.sem("chunk_ready"), 1)
            L.nth("chunk_ready")


def ready_matmuls(L, m, out, pairs, what="chunk_ready"):
    for i, (a, b) in enumerate(pairs):
        L.eng.wait_ge(m.sem(what), L.nth(what))
        last = L.eng.matmul(out, a, b, start=(i == 0), stop=(i == len(pairs) - 1))
    return last


def project_tensor(L, m, name, rhs, groups, kc=KC, cols=256, n=None, ready=0):
    for i in range(len(SLABS[name]) if n is None else n):
        w = L.next_slab(name, i)
        L.eng.wait_ge(L.landed, L.landings)
        for t in range(cols // P):
            for lo, wd in groups:
                ps = L.next_bank()
                for bank_free, count in L.bank_frees:
                    L.eng.wait_ge(bank_free, count)
                pairs = [(w[:, k * cols + t * P:k * cols + (t + 1) * P], rhs(k)[:, lo:lo + wd]) for k in range(kc)]
                if i == t == 0 and ready > 0:
                    ready -= 1
                    ready_matmuls(L, m, ps[:, :wd], pairs).then_inc(L.bank_full, 1)
                else:
                    matmuls(L, ps[:, :wd], pairs).then_inc(L.bank_full, 1)
        L.eng.drain().then_inc(m.sem("slab_used"), 1)
        if i < GUESTS.get(name, 0):
            mod_tensor(L, m, i == 0, i == GUESTS[name] - 1)


def read_banks(L, count, mine, fn):
    for g in range(count):
        if mine(g):
            ps = L.next_bank()
            L.eng.wait_ge(L.bank_full, L.fill)
            fn(g, ps).then_inc(L.step, 1)
            L.eng.wait_ge(L.step, L.next_step())
            L.eng.sem_inc(L.bank_free, 1)
        else:
            L.next_bank()


def even(g):
    return g % 2 == 0


def odd(g):
    return g % 2 == 1


def never(g):
    return False


def always(g):
    return True


LAG = 2
NPROB = 3


def attention_order(heads, qts):
    return [(h, q) for h in range(heads) for q in range(qts)]


def attention_tensor(L, m, A, score, value):
    tiles = attention_order(A.heads, A.qts)
    n, nb = len(tiles), (A.keys + BANK - 1) // BANK
    for i in range(n + LAG + 1):
        if i < n:
            ps = L.next_bank(nb)
            for bank_free, count in L.bank_frees:
                L.eng.wait_ge(bank_free, count)
            score(ps, *tiles[i]).then_inc(L.bank_full, 1)
        if LAG <= i < n + LAG:
            j = i - LAG
            L.eng.wait_ge(m.sem("probs"), L.nth("probs"))
            ps = L.next_bank(nb)
            for bank_free, count in L.bank_frees:
                L.eng.wait_ge(bank_free, count)
            for kt in range(A.keys // P):
                last = L.eng.transpose(ps[:, kt * P:(kt + 1) * P], A.probs[:, j % NPROB, kt * P:(kt + 1) * P],
                                       m.tab("ident"))
            last.then_inc(L.bank_full, 1)
        if i > LAG and (i - LAG) % A.qts == 0:
            h = tiles[i - LAG - 1][0]
            L.eng.wait_ge(m.sem("probs_turned"), L.nth("probs_turned", A.qts))
            for mt in range(A.mts):
                ps = L.next_bank()
                for bank_free, count in L.bank_frees:
                    L.eng.wait_ge(bank_free, count)
                matmuls(L, ps[0:A.vd, 0:A.qts * P], [(value(h, kt, mt), A.turned[:, h % 2, kt, :])
                                                          for kt in range(A.keys // P)]).then_inc(L.bank_full, 1)


def attention_scalar(L, m, A):
    tiles = attention_order(A.heads, A.qts)
    n, nb = len(tiles), (A.keys + BANK - 1) // BANK
    for i in range(n + LAG + 1):
        if i < n:
            ps = L.next_bank(nb)
            L.eng.wait_ge(L.bank_full, L.fill)
            L.eng.wait_ge(m.sem("row_max"), L.nth("row_max"))
            L.eng.activation(A.probs[:, i % NPROB, :], ps[:, :A.keys], ACT.Exp, bias=m.stat[:, i % NPROB:i % NPROB + 1],
                                  scale=A.scale, accum_out=m.stat[:, 4 + i % NPROB:5 + i % NPROB]).then_inc(L.step, 1)
            L.eng.wait_ge(L.step, L.next_step())
            L.eng.sem_inc(L.bank_free, 1)
            if nb == 2:
                L.eng.sem_inc(L.bank_free2, 1)
            L.eng.sem_inc(m.sem("exps"), 1)
            L.nth("exps")
        if LAG <= i < n + LAG:
            h, q = tiles[i - LAG]
            if q == 0 and h >= 2:
                L.eng.wait_ge(m.sem("head_out"), L.nth("head_out"))
            ps = L.next_bank(nb)
            L.eng.wait_ge(L.bank_full, L.fill)
            L.eng.activation(A.turned[:, h % 2, :, q * P:(q + 1) * P],
                                  ps[:, :A.keys].rearrange("p (a b) -> p a b", b=P), ACT.Copy).then_inc(L.step, 1)
            L.eng.wait_ge(L.step, L.next_step())
            L.eng.sem_inc(L.bank_free, 1)
            if nb == 2:
                L.eng.sem_inc(L.bank_free2, 1)
            L.eng.sem_inc(m.sem("probs_turned"), 1)
            L.nth("probs_turned")
        if i > LAG and (i - LAG) % A.qts == 0:
            L.next_bank(1)
            for _ in range(A.mts - 1):
                L.next_bank(1)
    L.eng.wait_ge(m.sem("head_out"), L.nth("head_out", min(2, A.heads)))


def attention_vector(L, m, A, out):
    tiles = attention_order(A.heads, A.qts)
    n, nb = len(tiles), (A.keys + BANK - 1) // BANK
    for i in range(n + LAG + 1):
        if i < n:
            s = i % NPROB
            ps = L.next_bank(nb)
            L.eng.wait_ge(L.bank_full, L.fill)
            L.eng.tensor_reduce(m.stat[:, 8 + s:9 + s], ps[:, :A.keys], AX, ALU.max).then_inc(L.step, 1)
            L.eng.wait_ge(L.step, L.next_step())
            L.eng.tensor_scalar(m.stat[:, s:s + 1], m.stat[:, 8 + s:9 + s], -A.scale, None, ALU.mult).then_inc(m.sem("row_max"), 1)
            L.eng.wait_ge(m.sem("row_max"), L.nth("row_max"))
        if LAG <= i < n + LAG:
            L.next_bank(nb)
        if 1 <= i <= n:
            s = (i - 1) % NPROB
            L.eng.wait_ge(m.sem("exps"), L.nth("exps"))
            L.eng.reciprocal(m.stat[:, 12 + s:13 + s], m.stat[:, 4 + s:5 + s]).then_inc(L.step, 1)
            L.eng.wait_ge(L.step, L.next_step())
            L.eng.tensor_scalar(A.probs[:, s, :], A.probs[:, s, :], m.stat[:, 12 + s:13 + s], None, ALU.mult).then_inc(m.sem("probs"), 1)
            L.eng.wait_ge(m.sem("probs"), L.nth("probs"))
        if i > LAG and (i - LAG) % A.qts == 0:
            h = tiles[i - LAG - 1][0]
            for mt in range(A.mts):
                ps = L.next_bank()
                L.eng.wait_ge(L.bank_full, L.fill)
                L.eng.tensor_copy(out(h, mt), ps[0:A.vd, 0:A.qts * P]).then_inc(L.step, 1)
                L.eng.wait_ge(L.step, L.next_step())
                L.eng.sem_inc(L.bank_free, 1)
            L.eng.sem_inc(m.sem("head_out"), 1)
            L.nth("head_out")


class Attention:
    def __init__(self, m, heads, qts, keys, scale, vd, mts, at):
        self.heads, self.qts, self.keys, self.scale, self.vd, self.mts = heads, qts, keys, scale, vd, mts
        self.probs = m.at(at, NPROB, keys)
        self.turned = m.at(at + NPROB * keys, 2 * (keys // P), qts * P).rearrange("p (a b) c -> p a b c", a=2)


def swiglu_tensor(L, m, name, n, S, groups, combine=None):
    for i in range(n + 1):
        if i < n:
            L.next_slab(name + "_gate", i)
            gate_slab = L.high, L.low
            L.eng.wait_ge(m.sem("slab_split"), L.nth("slab_split"))
            L.next_slab(name + "_up", i)
            up_slab = L.high, L.low
            L.eng.wait_ge(m.sem("slab_split"), L.nth("slab_split"))
            if combine is not None:
                ps = L.next_bank()
                for bank_free, count in L.bank_frees:
                    L.eng.wait_ge(bank_free, count)
                L.eng.matmul(ps[:, :T], m.tab("ident", i, 1, parts=32).to_broadcast([32, P]), combine,
                                    start=True, stop=True).then_inc(L.bank_full, 1)
            for t in range(2):
                for lo, wd in groups:
                    for high, low in (gate_slab, up_slab):
                        ps = L.next_bank()
                        for bank_free, count in L.bank_frees:
                            L.eng.wait_ge(bank_free, count)
                        split_matmuls(L, m, ps[:, :wd], [
                            (high[:, k * 256 + t * P:k * 256 + (t + 1) * P], low[:, k * 256 + t * P:k * 256 + (t + 1) * P],
                             S.h_high[:, k, lo:lo + wd], S.h_low[:, k, lo:lo + wd]) for k in range(KC)],
                            "h_split" if i == t == 0 and high is gate_slab[0] else None).then_inc(L.bank_full, 1)
            L.eng.drain().then_inc(m.sem("slab_used"), 1)
            L.eng.drain().then_inc(m.sem("slab_used"), 1)
        if i > 0:
            L.next_slab(name + "_down", i - 1)
            L.eng.wait_ge(m.sem("slab_split"), L.nth("slab_split"))
            L.eng.wait_ge(m.sem("hidden"), L.nth("hidden", 2 * len(groups)))
            for c in range(KC):
                for lo, wd in groups:
                    ps = L.next_bank()
                    for bank_free, count in L.bank_frees:
                        L.eng.wait_ge(bank_free, count)
                    split_matmuls(L, m, ps[:, :wd], [
                        (L.high[:, k * D + c * P:k * D + (c + 1) * P], L.low[:, k * D + c * P:k * D + (c + 1) * P],
                         S.hidden_high[:, (i - 1) % 2, k, lo:lo + wd], S.hidden_low[:, (i - 1) % 2, k, lo:lo + wd])
                        for k in range(2)]).then_inc(L.bank_full, 1)
            L.eng.drain().then_inc(m.sem("slab_used"), 1)
        if i < GUESTS.get(name, 0):
            mod_tensor(L, m, i == 0, i == GUESTS[name] - 1)


def swiglu_first_scalar(L, m, name):
    round_slab(L, m, SLABS[name + "_gate"][0])
    round_slab(L, m, SLABS[name + "_up"][0])


def swiglu_scalar(L, m, name, n, gate, groups, weight=None):
    for i in range(n + 1):
        if i > 0:
            round_slab(L, m, SLABS[name + "_down"][i - 1])
        if i + 1 < n:
            round_slab(L, m, SLABS[name + "_gate"][i + 1])
        if i < n:
            if weight is not None:
                if i >= 2:
                    L.eng.wait_ge(m.sem("weight_used"), L.nth("weight_used"))
                ps = L.next_bank()
                L.eng.wait_ge(L.bank_full, L.fill)
                L.eng.activation(weight[:, i % 2, :], ps[:, :T], ACT.Copy).then_inc(L.step, 1)
                L.eng.wait_ge(L.step, L.next_step())
                L.eng.sem_inc(L.bank_free, 1)
                L.eng.sem_inc(m.sem("weight"), 1)
                L.nth("weight")
            for t in range(2):
                for lo, wd in groups:
                    ps = L.next_bank()
                    L.eng.wait_ge(L.bank_full, L.fill)
                    if i >= 1:
                        L.eng.wait_ge(m.sem("gate_used"), L.nth("gate_used"))
                    L.eng.activation(gate[:, t, lo:lo + wd], ps[:, :wd], ACT.Silu).then_inc(L.step, 1)
                    L.eng.wait_ge(L.step, L.next_step())
                    L.eng.sem_inc(L.bank_free, 1)
                    L.eng.sem_inc(m.sem("gate"), 1)
                    L.nth("gate")
                    L.next_bank()
        if i + 1 < n:
            round_slab(L, m, SLABS[name + "_up"][i + 1])
        if i > 0:
            for _ in range(KC * len(groups)):
                L.next_bank()
        if i < GUESTS.get(name, 0):
            mod_scalar(L, m, i == 0, i == GUESTS[name] - 1)
    L.eng.wait_ge(m.sem("gate_used"), L.nth("gate_used", 2 * len(groups)))
    if weight is not None:
        L.eng.wait_ge(m.sem("weight_used"), L.nth("weight_used", 2))


def swiglu_vector(L, m, name, n, S, groups, add, weight=None):
    gate, hidden = S.gate, S.hidden
    for i in range(n + 1):
        if i < n:
            if weight is not None:
                L.next_bank()
                L.eng.wait_ge(m.sem("weight"), L.nth("weight"))
            for t in range(2):
                for lo, wd in groups:
                    L.next_bank()
                    ps = L.next_bank()
                    L.eng.wait_ge(L.bank_full, L.fill)
                    L.eng.wait_ge(m.sem("gate"), L.nth("gate"))
                    o = hidden[:, i % 2, t, lo:lo + wd]
                    L.eng.tensor_tensor(o, gate[:, t, lo:lo + wd], ps[:, :wd], ALU.mult).then_inc(L.step, 1)
                    L.eng.wait_ge(L.step, L.next_step())
                    L.eng.sem_inc(L.bank_free, 1)
                    L.eng.sem_inc(m.sem("gate_used"), 1)
                    L.nth("gate_used")
                    if weight is not None:
                        L.eng.tensor_tensor(o, o, weight[:, i % 2, :], ALU.mult).then_inc(L.step, 1)
                        L.eng.wait_ge(L.step, L.next_step())
                    split_vector(L, m, o, S.hidden_high[:, i % 2, t, lo:lo + wd], S.hidden_low[:, i % 2, t, lo:lo + wd], "hidden")
            if weight is not None:
                L.eng.sem_inc(m.sem("weight_used"), 1)
                L.nth("weight_used")
        if i > 0:
            for c in range(KC):
                for g in range(len(groups)):
                    ps = L.next_bank()
                    L.eng.wait_ge(L.bank_full, L.fill)
                    add(c, g, ps).then_inc(L.step, 1)
                    L.eng.wait_ge(L.step, L.next_step())
                    L.eng.sem_inc(L.bank_free, 1)
        if i < GUESTS.get(name, 0):
            mod_vector(L, m, i == 0, i == GUESTS[name] - 1)


def bcast(ap, n):
    return ap.unsqueeze(2).to_broadcast([ap.shape[0], ap.shape[1], n])


H1, MIX = 0, 4096
U0 = 8192


class Block1:

    def __init__(self, m):
        self.h = m.at(H1, KC, T)
        self.mix = m.at(MIX, KC, T)
        self.u = m.at(U0, 12, T + 2)
        self.aq = m.at(14360, 2, T)
        self.akv = m.at(15384, 1, T)
        self.kr = m.at(15896, T, parts=QK)
        self.aqn = m.at(16408, 2, T)
        self.akvn = m.at(17432, 1, T)
        self.q = m.at(17944, NH1, T, parts=QK)
        self.k = m.at(22040, NH1, T, parts=QK)
        self.v = m.at(26136, 4, HW)
        self.att = Attention(m, NH1, 4, T, QK ** -0.5, DV, 1, 28184)
        self.cos = m.at(28184, T, parts=QK)
        self.sin = m.at(28696, T, parts=QK)
        self.rot_a = m.at(1024, T, parts=QK)
        self.o = m.at(1536, 4, T)
        self.hu = m.at(14360, 12, T)
        self.vt = m.at(8192, 4, HW)
        self.x1t = m.at(10240, 4, HW)
        self.x2f = m.at(16408, 4, T)
        self.y = m.at(12288, 8, HW)
        self.dft = m.at(18456, 5248)
        self.dc = self.dft[:, 0:2048].rearrange("p (a b) -> p a b", a=4)
        self.ds = self.dft[:, 2048:4096].rearrange("p (a b) -> p a b", a=4)
        self.alt_col = self.dft[:, 4096:4224]
        self.alt_row = self.dft[:, 4224:4736]
        self.zemb = self.dft[0:33, 4736:5248]
        self.h1 = m.at(6144, T, parts=64)
        self.h2 = m.at(6656, T, parts=65)
        self.ang = m.at(7168, T, parts=64)
        self.turn = m.at(7680, T, parts=64)
        self.tmp = m.at(23704, 2, T)
        self.nyq = m.at(24728, T, parts=1)
        self.filt = m.at(25808, 4, 2048)
        self.kf = m.at(0, 8, HW)
        self.z1f = m.at(10240, 4, T)
        self.z2f = m.at(8192, 4, T)
        self.mem = m.at(4096, KC, C)
        self.hm = m.at(6144, KC, C)
        self.mk = m.at(8192, KC, C)
        self.mv = m.at(10240, 2, D)
        self.mq = m.at(12288, KC, T)
        self.mo = m.at(16384, KC, T)
        self.matt = Attention(m, MEM_H, 4, C, MEM_D ** -0.5, P, 2, 20480)
        self.logit = m.at(4096, 4, 36)
        self.cmb = m.at(4352, 4, 32)
        self.small = lambda i: m.at(4608 + 128 * i, 128)
        self.cmbt = m.at(8192, T, parts=32)
        self.gate = m.at(8704, 2, TC)
        self.hidden = m.at(10240, 4, TC).rearrange("p (a b) c -> p a b c", a=2)
        self.weight = m.at(13312, 2, T)
        self.hidden_low = m.rounded("moe_hidden_low", 10240, 2, 2, TC)
        self.hidden_high = m.rounded("moe_hidden_high", 14336, 2, 2, TC)
        self.h_low = m.rounded("moe_h_low", H1, KC, T)
        self.h_high = m.rounded("moe_h_high", 17408, KC, T)


def chunk(t, lo=0, n=None):
    return lambda c: t[:, c, lo:(t.shape[2] if n is None else lo + n)]


def gains(m, name, at=0):
    return lambda c: m.vec(name, at + c)


def mix_in_tensor(L, m, B):
    h = chunk(B.h)
    norm_tensor(L, m, h, KC)
    project_tensor(L, m, "in_q", h, [(0, T)], ready=1)
    w = L.next_slab("in_kv")
    L.eng.wait_ge(L.landed, L.landings)
    ps = L.next_bank()
    for bank_free, count in L.bank_frees:
        L.eng.wait_ge(bank_free, count)
    matmuls(L, ps, [(w[:, k * P:(k + 1) * P], h(k)) for k in range(KC)]).then_inc(L.bank_full, 1)
    ps = L.next_bank()
    for bank_free, count in L.bank_frees:
        L.eng.wait_ge(bank_free, count)
    matmuls(L, ps[0:QK], [(w[:, KC * P + k * QK:KC * P + (k + 1) * QK], h(k)) for k in range(KC)]).then_inc(L.bank_full, 1)
    L.eng.drain().then_inc(m.sem("slab_used"), 1)
    w = L.next_slab("in_krs")
    L.eng.wait_ge(L.landed, L.landings)
    ps = L.next_bank()
    for bank_free, count in L.bank_frees:
        L.eng.wait_ge(bank_free, count)
    matmuls(L, ps[0:QK], [(w[:, k * QK:(k + 1) * QK], h(k)) for k in range(KC)]).then_inc(L.bank_full, 1)
    L.eng.drain().then_inc(m.sem("slab_used"), 1)
    project_tensor(L, m, "in_hy", h, [(0, T)])


def mix_in_scalar(L, m, B):
    norm_scalar(L, m, chunk(m.x), chunk(B.h), KC)
    for c in range(2):
        ps = L.next_bank()
        L.eng.wait_ge(L.bank_full, L.fill)
        L.eng.activation(B.aq[:, c, :], ps, ACT.Copy).then_inc(L.step, 1)
        L.eng.wait_ge(L.step, L.next_step())
        L.eng.sem_inc(L.bank_free, 1)
    ps = L.next_bank()
    L.eng.wait_ge(L.bank_full, L.fill)
    L.eng.activation(B.akv[:, 0, :], ps, ACT.Copy).then_inc(L.step, 1)
    L.eng.wait_ge(L.step, L.next_step())
    L.eng.sem_inc(L.bank_free, 1)
    L.next_bank()
    L.next_bank()
    read_banks(L, 12, odd, lambda g, ps: L.eng.activation(B.u[:, g, 1:T + 1], ps, ACT.Copy))


def mix_in_vector(L, m, B):
    L.eng.memset(B.u[:, :, 0:1], 0.0).then_inc(L.step, 1)
    L.eng.wait_ge(L.step, L.next_step())
    L.eng.memset(B.u[:, :, T + 1:T + 2], 0.0).then_inc(L.step, 1)
    L.eng.wait_ge(L.step, L.next_step())
    norm_vector(L, m, chunk(m.x), chunk(B.h), KC, gains(m, "mix_g"), each=True)
    L.next_bank()
    L.next_bank()
    L.next_bank()
    a = L.next_bank()
    L.eng.wait_ge(L.bank_full, L.fill)
    L.eng.wait_ge(m.sem("rope96"), L.nth("rope96", 16))
    L.eng.tensor_tensor(B.kr, a[0:QK], B.cos, ALU.mult).then_inc(L.step, 1)
    L.eng.wait_ge(L.step, L.next_step())
    L.eng.sem_inc(L.bank_free, 1)
    b = L.next_bank()
    L.eng.wait_ge(L.bank_full, L.fill)
    L.eng.tensor_tensor(B.q[:, 0, :], b[0:QK], B.sin, ALU.mult).then_inc(L.step, 1)
    L.eng.wait_ge(L.step, L.next_step())
    L.eng.sem_inc(L.bank_free, 1)
    L.eng.tensor_tensor(B.kr, B.kr, B.q[:, 0, :], ALU.add).then_inc(L.step, 1)
    L.eng.wait_ge(L.step, L.next_step())
    read_banks(L, 12, even, lambda g, ps: L.eng.tensor_copy(B.u[:, g, 1:T + 1], ps))


def latent_tensor(L, m, B):
    norm_tensor(L, m, chunk(B.aqn), 2)
    norm_tensor(L, m, chunk(B.akvn), 1)
    L.eng.wait_ge(m.sem("normed"), L.nth("normed", 2))
    w = L.next_slab("uq")
    L.eng.wait_ge(L.landed, L.landings)
    ws = L.next_slab("uqs")
    L.eng.wait_ge(L.landed, L.landings)
    for h in range(NH1):
        for a in (w, ws):
            ps = L.next_bank()
            for bank_free, count in L.bank_frees:
                L.eng.wait_ge(bank_free, count)
            matmuls(L, ps[0:QK], [(a[:, k * NH1 * QK + h * QK:k * NH1 * QK + (h + 1) * QK], B.aqn[:, k, :])
                                         for k in range(2)]).then_inc(L.bank_full, 1)
    L.eng.drain().then_inc(m.sem("slab_used"), 1)
    L.eng.drain().then_inc(m.sem("slab_used"), 1)
    w = L.next_slab("ukv")
    L.eng.wait_ge(L.landed, L.landings)
    for h in range(NH1):
        ps = L.next_bank()
        for bank_free, count in L.bank_frees:
            L.eng.wait_ge(bank_free, count)
        matmuls(L, ps[0:NOPE], [(w[:, h * NOPE:(h + 1) * NOPE], B.akvn[:, 0, :])]).then_inc(L.bank_full, 1)
    for t in range(4):
        ps = L.next_bank()
        for bank_free, count in L.bank_frees:
            L.eng.wait_ge(bank_free, count)
        matmuls(L, ps, [(B.akvn[:, 0, t * P:(t + 1) * P], w[:, 512:1024])]).then_inc(L.bank_full, 1)
    L.eng.drain().then_inc(m.sem("slab_used"), 1)


def latent_scalar(L, m, B):
    norm_scalar(L, m, chunk(B.aq), chunk(B.aqn), 2)
    L.eng.wait_ge(m.sem("root_used"), L.nth("root_used"))
    norm_scalar(L, m, chunk(B.akv), chunk(B.akvn), 1)
    for h in range(NH1):
        L.next_bank()
        L.next_bank()
    for h in range(NH1):
        ps = L.next_bank()
        L.eng.wait_ge(L.bank_full, L.fill)
        L.eng.activation(B.k[0:NOPE, h, :], ps[0:NOPE], ACT.Copy).then_inc(L.step, 1)
        L.eng.wait_ge(L.step, L.next_step())
        L.eng.sem_inc(L.bank_free, 1)
        L.eng.activation(B.k[NOPE:QK, h, :], B.kr[NOPE:QK], ACT.Copy).then_inc(L.step, 1)
        L.eng.wait_ge(L.step, L.next_step())
    for t in range(4):
        ps = L.next_bank()
        L.eng.wait_ge(L.bank_full, L.fill)
        L.eng.activation(B.v[:, t, :], ps, ACT.Copy).then_inc(L.step, 1)
        L.eng.wait_ge(L.step, L.next_step())
        L.eng.sem_inc(L.bank_free, 1)


def latent_vector(L, m, B):
    norm_vector(L, m, chunk(B.aq), chunk(B.aqn), 2, gains(m, "qn_g"))
    L.eng.sem_inc(m.sem("normed"), 1)
    L.nth("normed")
    L.eng.sem_inc(m.sem("root_used"), 1)
    L.nth("root_used")
    norm_vector(L, m, chunk(B.akv), chunk(B.akvn), 1, gains(m, "kvn_g"))
    L.eng.sem_inc(m.sem("normed"), 1)
    L.nth("normed")
    for h in range(NH1):
        ps = L.next_bank()
        L.eng.wait_ge(L.bank_full, L.fill)
        L.eng.tensor_tensor(B.q[:, h, :], ps[0:QK], B.cos, ALU.mult).then_inc(L.step, 1)
        L.eng.wait_ge(L.step, L.next_step())
        L.eng.sem_inc(L.bank_free, 1)
        ps = L.next_bank()
        L.eng.wait_ge(L.bank_full, L.fill)
        L.eng.tensor_tensor(B.rot_a, ps[0:QK], B.sin, ALU.mult).then_inc(L.step, 1)
        L.eng.wait_ge(L.step, L.next_step())
        L.eng.sem_inc(L.bank_free, 1)
        L.eng.tensor_tensor(B.q[:, h, :], B.q[:, h, :], B.rot_a, ALU.add).then_inc(L.step, 1)
        L.eng.wait_ge(L.step, L.next_step())
    for _ in range(NH1 + 4):
        L.next_bank()


def latent_attention_tensor(L, m, B):
    def score(ps, h, q):
        return matmuls(L, ps, [(B.q[:, h, q * P:(q + 1) * P], B.k[:, h, :])])
    attention_tensor(L, m, B.att, score, lambda h, kt, mt: B.v[:, kt, h * DV:(h + 1) * DV])


def latent_attention_vector(L, m, B):
    attention_vector(L, m, B.att, lambda h, mt: B.o[64 * (h % 2):64 * (h % 2) + 64, h // 2, :])


def conv_vector(L, m, B):
    for c in range(12):
        o, u = B.hu[:, c, :], B.u[:, c, :]
        L.eng.tensor_scalar(o, u[:, 0:T], m.vec("conv_w", c), m.vec("conv_b", c), ALU.mult, ALU.add).then_inc(L.step, 1)
        L.eng.wait_ge(L.step, L.next_step())
        L.eng.scalar_tensor_tensor(o, u[:, 1:T + 1], m.vec("conv_w", 12 + c), o, ALU.mult, ALU.add).then_inc(L.step, 1)
        L.eng.wait_ge(L.step, L.next_step())
        L.eng.scalar_tensor_tensor(o, u[:, 2:T + 2], m.vec("conv_w", 24 + c), o, ALU.mult, ALU.add).then_inc(L.step, 1)
        L.eng.wait_ge(L.step, L.next_step())


def turn_tensor(L, m, src, dst_chunks):
    for d in range(dst_chunks):
        ps = L.next_bank()
        for bank_free, count in L.bank_frees:
            L.eng.wait_ge(bank_free, count)
        for i in range(4):
            last = L.eng.transpose(ps[:, i * P:(i + 1) * P], src(d, i), m.tab("ident"))
        last.then_inc(L.bank_full, 1)


def conv_turn_tensor(L, m, B):
    for first in (8, 0):
        turn_tensor(L, m, lambda d, i: B.hu[:, first + i, d * P:(d + 1) * P], 4)


def conv_turn_scalar(L, m, B):
    read_banks(L, 8, always, lambda g, ps: L.eng.activation((B.vt, B.x1t)[g // 4][:, g % 4, :], ps, ACT.Copy))


def filter_tensor(L, m, B):
    L.eng.wait_ge(m.sem("dft_landed"), L.nth("dft_landed", 16))
    ps = L.next_bank()
    for bank_free, count in L.bank_frees:
        L.eng.wait_ge(bank_free, count)
    matmuls(L, ps[0:64], [(m.vec("hw1", 0, 64, parts=33), B.zemb)]).then_inc(L.bank_full, 1)
    L.eng.wait_ge(m.sem("sine"), L.nth("sine"))
    ps = L.next_bank()
    for bank_free, count in L.bank_frees:
        L.eng.wait_ge(bank_free, count)
    matmuls(L, ps[0:64], [(m.vec("hw2", 0, 64, parts=64), B.h1)]).then_inc(L.bank_full, 1)
    L.eng.wait_ge(m.sem("sine"), L.nth("sine"))
    L.next_slab("decay")
    L.eng.wait_ge(L.landed, L.landings)
    w = L.next_slab("hw3")
    L.eng.wait_ge(L.landed, L.landings)
    L.next_slab("skip0")
    L.eng.wait_ge(L.landed, L.landings)
    for q in range(4):
        for t in range(4):
            ps = L.next_bank()
            for bank_free, count in L.bank_frees:
                L.eng.wait_ge(bank_free, count)
            matmuls(L, ps, [(B.h2[:, t * P:(t + 1) * P], w[0:65, q * HW:(q + 1) * HW])]).then_inc(L.bank_full, 1)


def filter_vector(L, m, B):
    L.eng.memset(B.h2[64:65], 1.0).then_inc(L.step, 1)
    L.eng.wait_ge(L.step, L.next_step())
    for b, f in (("hb1", "hf0"), ("hb2", "hf1")):
        ps = L.next_bank()
        L.eng.wait_ge(L.bank_full, L.fill)
        L.eng.tensor_scalar(B.ang, ps[0:64], m.vec(b, parts=64), m.vec(f, parts=64), ALU.add, ALU.mult).then_inc(L.step, 1)
        L.eng.wait_ge(L.step, L.next_step())
        L.eng.sem_inc(L.bank_free, 1)
        L.eng.tensor_scalar(B.turn, B.ang, float(1 / (2 * np.pi)), 12582912.0, ALU.mult, ALU.add).then_inc(L.step, 1)
        L.eng.wait_ge(L.step, L.next_step())
        L.eng.tensor_scalar(B.turn, B.turn, -12582912.0, None, ALU.add).then_inc(L.step, 1)
        L.eng.wait_ge(L.step, L.next_step())
        L.eng.scalar_tensor_tensor(B.ang, B.turn, -6.28125, B.ang, ALU.mult, ALU.add).then_inc(L.step, 1)
        L.eng.wait_ge(L.step, L.next_step())
        L.eng.scalar_tensor_tensor(B.ang, B.turn, -0.0019353071795864769, B.ang, ALU.mult, ALU.add).then_inc(L.step, 1)
        L.eng.wait_ge(L.step, L.next_step())
        L.eng.tensor_scalar(B.ang, B.ang, 3.1415925, -3.1415925, ALU.min, ALU.max).then_inc(m.sem("angle"), 1)
        L.eng.wait_ge(m.sem("angle"), L.nth("angle"))
    for q in range(4):
        for t in range(4):
            ps = L.next_bank()
            L.eng.wait_ge(L.bank_full, L.fill)
            L.eng.wait_ge(m.sem("window"), L.nth("window"))
            L.eng.tensor_tensor(B.filt[:, t, q * HW:(q + 1) * HW], ps, B.tmp[:, t % 2, :], ALU.mult).then_inc(L.step, 1)
            L.eng.wait_ge(L.step, L.next_step())
            L.eng.sem_inc(L.bank_free, 1)
            L.eng.sem_inc(m.sem("window_used"), 1)
            L.nth("window_used")
    for q in (1, 3):
        L.eng.memset(B.filt[0:1, 0, q * HW:(q + 1) * HW], 0.0).then_inc(L.step, 1)
        L.eng.wait_ge(L.step, L.next_step())


def filter_scalar(L, m, B):
    L.next_bank()
    L.eng.wait_ge(m.sem("angle"), L.nth("angle"))
    L.eng.activation(B.h1, B.ang, ACT.Sin).then_inc(m.sem("sine"), 1)
    L.eng.wait_ge(m.sem("sine"), L.nth("sine"))
    L.next_bank()
    L.eng.wait_ge(m.sem("angle"), L.nth("angle"))
    L.eng.activation(B.h2[0:64], B.ang, ACT.Sin).then_inc(m.sem("sine"), 1)
    L.eng.wait_ge(m.sem("sine"), L.nth("sine"))
    dec = m.slab_of(L, "decay")
    L.eng.activation(dec, dec, ACT.Abs).then_inc(L.step, 1)
    L.eng.wait_ge(L.step, L.next_step())
    n = 0
    for q in range(4):
        for t in range(4):
            L.next_bank()
            if n >= 2:
                L.eng.wait_ge(m.sem("window_used"), L.nth("window_used"))
            L.eng.activation(B.tmp[:, t % 2, :], dec[:, q * HW:(q + 1) * HW], ACT.Exp, scale=m.tab("t01", t, 1)).then_inc(m.sem("window"), 1)
            L.eng.wait_ge(m.sem("window"), L.nth("window"))
            n += 1
    L.eng.wait_ge(m.sem("window_used"), L.nth("window_used", 2))


def parts_vector(L, m, B, order):
    f, b = [B.filt[:, :, (2 * order + d) * HW:(2 * order + d + 1) * HW] for d in (0, 1)]
    e = B.y[:, 0:4, :]
    L.eng.tensor_tensor(e, f, b, ALU.add).then_inc(L.step, 1)
    L.eng.wait_ge(L.step, L.next_step())
    L.eng.tensor_tensor(f, f, b, ALU.subtract).then_inc(L.step, 1)
    L.eng.wait_ge(L.step, L.next_step())


def spectrum_tensor(L, m, B, even_part, odd_part, pairs):
    order = [(f, s) for f in range(4) for s in (0, 1)] if pairs else [(f, s) for s in (0, 1) for f in range(4)]
    for f, s in order:
        ps = L.next_bank()
        for bank_free, count in L.bank_frees:
            L.eng.wait_ge(bank_free, count)
        if s == 0:
            ops = [(B.dc[:, t, f * P:(f + 1) * P], even_part(t)) for t in range(4)]
        else:
            ops = [(B.ds[:, t, f * P:(f + 1) * P], odd_part(t)) for t in range(4)]
            if f == 0:
                ops += [(B.alt_col, even_part(t)) for t in range(4)]
        matmuls(L, ps, ops).then_inc(L.bank_full, 1)


def filter_spectrum_tensor(L, m, B, order):
    spectrum_tensor(L, m, B, lambda t: B.y[:, t, :], lambda t: B.filt[:, t, 2 * order * HW:(2 * order + 1) * HW], False)


def filter_spectrum_scalar(L, m, B):
    read_banks(L, 8, always, lambda g, ps: L.eng.activation(
        B.kf[:, g, :], ps, ACT.Copy, scale=m.tab("dft_scale", 0 if g % 4 == 0 else 1, 1)))


def product_tensor(L, m, B):
    spectrum_tensor(L, m, B, lambda t: B.vt[:, t, :], lambda t: B.vt[:, t, :], True)


def product_vector(L, m, B):
    for f in range(4):
        re, im, kr, ki = B.y[:, f, :], B.y[:, 4 + f, :], B.kf[:, f, :], B.kf[:, 4 + f, :]
        t1, t2 = B.tmp[:, 0, :], B.tmp[:, 1, :]
        zr = L.next_bank()
        L.eng.wait_ge(L.bank_full, L.fill)
        zr_free = L.bank_free
        zi = L.next_bank()
        L.eng.wait_ge(L.bank_full, L.fill)
        L.eng.tensor_tensor(re, zr, kr, ALU.mult).then_inc(L.step, 1)
        L.eng.wait_ge(L.step, L.next_step())
        L.eng.tensor_tensor(im, zr, ki, ALU.mult).then_inc(L.step, 1)
        L.eng.wait_ge(L.step, L.next_step())
        L.eng.sem_inc(zr_free, 1)
        L.eng.tensor_tensor(t1, zi, ki, ALU.mult).then_inc(L.step, 1)
        L.eng.wait_ge(L.step, L.next_step())
        L.eng.tensor_tensor(t2, zi, kr, ALU.mult).then_inc(L.step, 1)
        L.eng.wait_ge(L.step, L.next_step())
        L.eng.sem_inc(L.bank_free, 1)
        if f == 0:
            L.eng.tensor_copy(B.nyq, t1[0:1]).then_inc(L.step, 1)
            L.eng.wait_ge(L.step, L.next_step())
            L.eng.memset(t1[0:1], 0.0).then_inc(L.step, 1)
            L.eng.wait_ge(L.step, L.next_step())
        L.eng.tensor_tensor(re, re, t1, ALU.subtract).then_inc(L.step, 1)
        L.eng.wait_ge(L.step, L.next_step())
        L.eng.tensor_tensor(im, im, t2, ALU.add).then_inc(L.step, 1)
        L.eng.wait_ge(L.step, L.next_step())
        if f == 0:
            L.eng.tensor_copy(im[0:1], B.nyq).then_inc(L.step, 1)
            L.eng.wait_ge(L.step, L.next_step())


def inverse0_tensor(L, m, B):
    for t in range(4):
        s = slice(t * P, (t + 1) * P)
        ps = L.next_bank()
        for bank_free, count in L.bank_frees:
            L.eng.wait_ge(bank_free, count)
        matmuls(L, ps, [(B.dc[:, f, s], B.y[:, f, :]) for f in range(4)] +
                       [(B.ds[:, f, s], B.y[:, 4 + f, :]) for f in range(4)] + [(B.alt_row[:, s], B.y[:, 4, :])]).then_inc(L.bank_full, 1)


def inverse0_vector(L, m, B):
    skip = m.slab_of(L, "skip0")[:, 0:HW]
    for t in range(4):
        t1 = B.tmp[:, 0, :]
        L.eng.tensor_tensor(t1, B.vt[:, t, :], skip, ALU.mult).then_inc(L.step, 1)
        L.eng.wait_ge(L.step, L.next_step())
        ps = L.next_bank()
        L.eng.wait_ge(L.bank_full, L.fill)
        L.eng.tensor_tensor(t1, t1, ps, ALU.add).then_inc(L.step, 1)
        L.eng.wait_ge(L.step, L.next_step())
        L.eng.sem_inc(L.bank_free, 1)
        L.eng.tensor_tensor(B.vt[:, t, :], t1, B.x1t[:, t, :], ALU.mult).then_inc(L.step, 1)
        L.eng.wait_ge(L.step, L.next_step())


def inverse1_tensor(L, m, B):
    for c in range(4):
        s = slice(c * P, (c + 1) * P)
        ps = L.next_bank()
        for bank_free, count in L.bank_frees:
            L.eng.wait_ge(bank_free, count)
        matmuls(L, ps, [(B.y[:, f, s], B.dc[:, f, :]) for f in range(4)] +
                       [(B.y[:, 4 + f, s], B.ds[:, f, :]) for f in range(4)] + [(B.y[:, 4, s], B.alt_row)]).then_inc(L.bank_full, 1)


def inverse1_vector(L, m, B):
    for c in range(4):
        t1 = B.tmp[:, 0, :]
        ps = L.next_bank()
        L.eng.wait_ge(L.bank_full, L.fill)
        L.eng.scalar_tensor_tensor(t1, B.z1f[:, c, :], m.vec("skip1", c), ps, ALU.mult, ALU.add).then_inc(L.step, 1)
        L.eng.wait_ge(L.step, L.next_step())
        L.eng.sem_inc(L.bank_free, 1)
        L.eng.tensor_tensor(B.z2f[:, c, :], t1, B.x2f[:, c, :], ALU.mult).then_inc(L.step, 1)
        L.eng.wait_ge(L.step, L.next_step())


def add_to_x(L, m, col=None, lo=0, w=T):
    def fn(c, ps):
        o = m.x[:, c, :]
        if col is None:
            return L.eng.tensor_tensor(o, o, ps[:, :w], ALU.add)
        return L.eng.scalar_tensor_tensor(o, ps[:, :w], col(c), o, ALU.mult, ALU.add)
    return fn


def memory_tensor(L, m, B):
    norm_tensor(L, m, chunk(B.hm), KC)
    norm_tensor(L, m, chunk(B.h), KC)
    project_tensor(L, m, "mk", chunk(B.hm), [(0, C)], ready=1)
    for i in range(4):
        w = L.next_slab("mv", i)
        L.eng.wait_ge(L.landed, L.landings)
        for t in range(2):
            ps = L.next_bank()
            for bank_free, count in L.bank_frees:
                L.eng.wait_ge(bank_free, count)
            matmuls(L, ps[:, :256], [(B.hm[:, k, t * P:(t + 1) * P], w[:, k * 256:(k + 1) * 256]) for k in range(KC)]).then_inc(L.bank_full, 1)
        L.eng.drain().then_inc(m.sem("slab_used"), 1)
    project_tensor(L, m, "mq", chunk(B.h), [(0, T)], ready=1)


def memory_scalar(L, m, B):
    L.eng.wait_ge(m.sem("mem_landed"), L.nth("mem_landed", 16))
    norm_scalar(L, m, chunk(B.mem), chunk(B.hm), KC)
    norm_scalar(L, m, chunk(m.x), chunk(B.h), KC, root_used=True)
    read_banks(L, 8, odd, lambda g, ps: L.eng.activation(B.mk[:, g, :], ps[:, :C], ACT.Copy))
    read_banks(L, 8, odd, lambda g, ps: L.eng.activation(
        B.mv[:, g % 2, g // 2 * 256:g // 2 * 256 + 256], ps[:, :256], ACT.Copy))
    read_banks(L, 8, odd, lambda g, ps: L.eng.activation(B.mq[:, g, :], ps, ACT.Copy))


def memory_vector(L, m, B):
    norm_vector(L, m, chunk(B.mem), chunk(B.hm), KC, gains(m, "mem_g"), each=True)
    L.eng.sem_inc(m.sem("root_used"), 1)
    L.nth("root_used")
    norm_vector(L, m, chunk(m.x), chunk(B.h), KC, gains(m, "cross_g"), each=True)
    read_banks(L, 8, even, lambda g, ps: L.eng.tensor_copy(B.mk[:, g, :], ps[:, :C]))
    read_banks(L, 8, even, lambda g, ps: L.eng.tensor_copy(
        B.mv[:, g % 2, g // 2 * 256:g // 2 * 256 + 256], ps[:, :256]))
    read_banks(L, 8, even, lambda g, ps: L.eng.tensor_copy(B.mq[:, g, :], ps))


def memory_attention_tensor(L, m, B):
    def score(ps, h, q):
        return matmuls(L, ps[:, :C], [(B.mq[:, 2 * h + k, q * P:(q + 1) * P], B.mk[:, 2 * h + k, :]) for k in range(2)])
    attention_tensor(L, m, B.matt, score,
                     lambda h, kt, mt: B.mv[:, kt, h * MEM_D + mt * P:h * MEM_D + (mt + 1) * P])


def route_tensor(L, m, B):
    norm_tensor(L, m, chunk(B.h), KC)
    L.eng.wait_ge(m.sem("normed"), L.nth("normed"))
    w = L.next_slab("route")
    L.eng.wait_ge(L.landed, L.landings)
    ps = L.next_bank()
    for bank_free, count in L.bank_frees:
        L.eng.wait_ge(bank_free, count)
    for t in range(4):
        last = matmuls(L, ps[:, t * 36:(t + 1) * 36], [(B.h[:, k, t * P:(t + 1) * P], w[:, k * 36:(k + 1) * 36])
                                                       for k in range(KC)])
    last.then_inc(L.bank_full, 1)
    L.eng.drain().then_inc(m.sem("slab_used"), 1)
    L.eng.wait_ge(m.sem("combined"), L.nth("combined"))
    ps = L.next_bank()
    for bank_free, count in L.bank_frees:
        L.eng.wait_ge(bank_free, count)
    for t in range(4):
        last = L.eng.transpose(ps[0:32, t * P:(t + 1) * P], B.cmb[:, t, :], m.tab("ident"))
    last.then_inc(L.bank_full, 1)


def route_scalar(L, m, B):
    norm_scalar(L, m, chunk(m.x), chunk(B.h), KC)
    L.next_bank()
    for i in range(2):
        L.eng.wait_ge(m.sem("gap"), L.nth("gap"))
        s = B.small(i)
        L.eng.activation(s[:, 0:16], s[:, 0:16], ACT.Exp).then_inc(m.sem("gap_exp"), 1)
        L.eng.wait_ge(m.sem("gap_exp"), L.nth("gap_exp"))
    ps = L.next_bank()
    L.eng.wait_ge(L.bank_full, L.fill)
    L.eng.activation(B.cmbt, ps[0:32], ACT.Copy).then_inc(L.step, 1)
    L.eng.wait_ge(L.step, L.next_step())
    L.eng.sem_inc(L.bank_free, 1)


def first_best(L, m, v, best, hot, tmp, n):
    a = v.shape[1]
    rank = m.tab("expert_rank", 0, n).unsqueeze(1).to_broadcast([P, a, n])
    L.eng.tensor_reduce(best, v, AX, ALU.max).then_inc(L.step, 1)
    L.eng.wait_ge(L.step, L.next_step())
    L.eng.tensor_tensor(hot, v, bcast(best, n), ALU.is_equal).then_inc(L.step, 1)
    L.eng.wait_ge(L.step, L.next_step())
    L.eng.tensor_tensor(hot, hot, rank, ALU.mult).then_inc(L.step, 1)
    L.eng.wait_ge(L.step, L.next_step())
    L.eng.tensor_reduce(tmp, hot, AX, ALU.max).then_inc(L.step, 1)
    L.eng.wait_ge(L.step, L.next_step())
    L.eng.tensor_tensor(hot, hot, bcast(tmp, n), ALU.is_equal).then_inc(L.step, 1)
    L.eng.wait_ge(L.step, L.next_step())


def route_vector(L, m, B):
    norm_vector(L, m, chunk(m.x), chunk(B.h), KC, gains(m, "ffn_g"))
    L.eng.sem_inc(m.sem("normed"), 1)
    L.nth("normed")
    ps = L.next_bank()
    L.eng.wait_ge(L.bank_full, L.fill)
    e = L.eng
    e.tensor_tensor(B.logit, ps[:, :144].rearrange("p (a b) -> p a b", a=4),
                         m.vec("b_route", 0, 36).unsqueeze(1).to_broadcast([P, 4, 36]), ALU.add).then_inc(L.step, 1)
    L.eng.wait_ge(L.step, L.next_step())
    L.eng.sem_inc(L.bank_free, 1)
    gap, x = B.small(0)[:, 0:16], B.small(1)[:, 0:16]
    s2, s3 = B.small(2), B.small(3)
    g = B.logit[:, :, 0:4]
    ghot = B.small(4)[:, 0:16].rearrange("p (a b) -> p a b", a=4)
    gmax, tmp4, pg, tmp16 = s2[:, 0:4], s2[:, 4:8], s2[:, 8:12], s2[:, 16:32]
    first_best(L, m, g, gmax, ghot, tmp4, 4)
    gap3 = gap.rearrange("p (a b) -> p a b", a=4)
    e.tensor_tensor(gap3, g, bcast(gmax, 4), ALU.subtract).then_inc(m.sem("gap"), 1)
    L.eng.wait_ge(m.sem("gap"), L.nth("gap"))
    L.eng.wait_ge(m.sem("gap_exp"), L.nth("gap_exp"))
    e.tensor_reduce(pg, gap3, AX, ALU.add).then_inc(L.step, 1)
    L.eng.wait_ge(L.step, L.next_step())
    e.reciprocal(pg, pg).then_inc(L.step, 1)
    L.eng.wait_ge(L.step, L.next_step())
    e.tensor_tensor(ghot, ghot, bcast(pg, 4), ALU.mult).then_inc(L.step, 1)
    L.eng.wait_ge(L.step, L.next_step())
    ex, hot1, hot2 = [B.small(i).rearrange("p (a b) -> p a b", a=16) for i in (5, 6, 7)]
    e.tensor_copy(B.small(5).rearrange("p (a b) -> p a b", a=4), B.logit[:, :, 4:36]).then_inc(L.step, 1)
    L.eng.wait_ge(L.step, L.next_step())
    b1, b2 = s3[:, 0:16], s3[:, 16:32]
    first_best(L, m, ex, b1, hot1, tmp16, 8)
    e.scalar_tensor_tensor(ex, hot1, -1e30, ex, ALU.mult, ALU.add).then_inc(L.step, 1)
    L.eng.wait_ge(L.step, L.next_step())
    first_best(L, m, ex, b2, hot2, tmp16, 8)
    e.tensor_tensor(x, b2, b1, ALU.subtract).then_inc(m.sem("gap"), 1)
    L.eng.wait_ge(m.sem("gap"), L.nth("gap"))
    L.eng.wait_ge(m.sem("gap_exp"), L.nth("gap_exp"))
    p1 = s3[:, 32:48]
    e.tensor_scalar(p1, x, 1.0, None, ALU.add).then_inc(L.step, 1)
    L.eng.wait_ge(L.step, L.next_step())
    e.reciprocal(p1, p1).then_inc(L.step, 1)
    L.eng.wait_ge(L.step, L.next_step())
    e.tensor_tensor(p1, p1, ghot.rearrange("p a b -> p (a b)"), ALU.mult).then_inc(L.step, 1)
    L.eng.wait_ge(L.step, L.next_step())
    e.tensor_tensor(x, x, p1, ALU.mult).then_inc(L.step, 1)
    L.eng.wait_ge(L.step, L.next_step())
    e.tensor_tensor(hot1, hot1, bcast(p1, 8), ALU.mult).then_inc(L.step, 1)
    L.eng.wait_ge(L.step, L.next_step())
    e.tensor_tensor(hot2, hot2, bcast(x, 8), ALU.mult).then_inc(L.step, 1)
    L.eng.wait_ge(L.step, L.next_step())
    c = B.cmb.rearrange("p a (b c) -> p (a b) c", b=4)
    e.tensor_tensor(c, hot1, hot2, ALU.add).then_inc(m.sem("combined"), 1)
    L.eng.wait_ge(m.sem("combined"), L.nth("combined"))
    L.next_bank()


BOTH = [NX, NC_]
XCH, ALLCH = T // CH, TC // CH
MASK = {"before": (0, 1), "upto": (2, 3)}


class Block2:

    def __init__(self, m):
        self.h = m.at(0, KC, TC)
        self.q = m.at(6144, KC, TC)
        self.k = m.at(12288, 4, TC)
        self.v = m.at(15360, 6, 256)
        self.att = Attention(m, QH, 4, TC, HD ** -0.5, HD, 1, 16896)
        self.catt = Attention(m, QH, 2, C, HD ** -0.5, HD, 1, 16896)
        self.o = m.at(25344, KC, TC)
        self.rope = m.at(31488, 2, T)
        self.sq = m.at(16896, 2, TC)
        self.root2 = m.at(18432, 2, TC)
        self.rot = m.at(19968, T)
        self.gate = m.at(6144, 2, TC)
        self.hidden = m.at(7680, 4, TC).rearrange("p (a b) c -> p a b c", a=2)
        self.hidden_low = m.rounded("ffn_hidden_low", 7680, 2, 2, TC)
        self.hidden_high = m.rounded("ffn_hidden_high", 10752, 2, 2, TC)
        self.h_low = m.rounded("h_low", 0, KC, TC)
        self.h_high = m.rounded("h_high", 13824, KC, TC)
        self.xx = m.at(6144, KC, TC)
        self.lp = m.at(12288, KC, TC)
        self.pk = m.at(18432, KC, TC)
        self.pv = m.at(24576, KC, TC)
        self.pr = m.at(18432, KC, T)
        self.tw = m.at(30720, TC)
        self.ta = m.at(31488, TC)
        self.tg = m.at(32256, T)
        self.out = m.at(26624, KC, T)
        self.load = [m.at(2048 * i, 2048) for i in range(2)]
        at = [4096]

        def new(n=TC):
            at[0] += n
            return m.at(at[0] - n, n)

        self.kk, self.lw, self.cm = new(), new(), new()
        self.al, self.be, self.ka, self.rh = [[new(n), new(n)] for n in (TC, TC, TC, T)]
        self.bk = [new(T), m.root]
        self.ecol = m.ecol
        self.vtok, self.altok, self.betok, self.katok = new(), new(), new(), new()
        self.nt, self.ti, self.tt, self.x, self.akt, self.rbt, self.rkt = [new() for _ in range(7)]
        self.akv, self.ua, self.uv = new(), new(), new()
        self.rp, self.yj = new(T), new(T)
        self.mt, self.g, self.s = new(), new(), new()
        assert at[0] <= 26624, at
        at[0] = 32768
        self.masks = new(16 * CH)
        self.eye = new(CH)
        self.keep = new()


def mod_tensor(L, m, first, last):
    w = L.next_slab("mod", L.mods)
    L.eng.wait_ge(L.landed, L.landings)
    if L.mods == 0:
        L.eng.wait_ge(m.sem("cond"), L.nth("cond"))
    ps = L.next_bank()
    for bank_free, count in L.bank_frees:
        L.eng.wait_ge(bank_free, count)
    for half in range(2):
        for g in range(4):
            k = 4 * half + g
            done = L.eng.matmul(ps[32 * g:32 * g + 32, 0:256], m.cond[:, k, :], w[:, k * 256:(k + 1) * 256],
                                start=(half == 0), stop=(half == 1), tile_position=(0, 32 * g))
    done.then_inc(L.bank_full, 1)
    L.eng.drain().then_inc(m.sem("slab_used"), 1)
    L.mods += 1
    for s in range(L.mods - 1 - (not first), L.mods - (not last)):
        L.eng.wait_ge(m.sem("mod_rows"), L.nth("mod_rows"))
        ps = L.next_bank()
        for bank_free, count in L.bank_frees:
            L.eng.wait_ge(bank_free, count)
        for t in range(2):
            done = L.eng.matmul(ps[:, 2 * t:2 * t + 2], m.mod_rows[:, s % 2, t * P:(t + 1) * P], m.tab("pick2"),
                                start=True, stop=True)
        done.then_inc(L.bank_full, 1)


def mod_scalar(L, m, first, last):
    ps = L.next_bank()
    L.eng.wait_ge(L.bank_full, L.fill)
    L.eng.activation(m.mod_rows[:, L.mods % 2, :], ps[:, :256], ACT.Copy).then_inc(L.step, 1)
    L.eng.wait_ge(L.step, L.next_step())
    L.eng.sem_inc(L.bank_free, 1)
    L.eng.sem_inc(m.sem("mod_rows"), 1)
    L.nth("mod_rows")
    L.mods += 1
    for s in range(L.mods - 1 - (not first), L.mods - (not last)):
        L.next_bank()


def mod_vector(L, m, first, last):
    L.next_bank()
    L.mods += 1
    for n in range(L.mods - 1 - (not first), L.mods - (not last)):
        ps = L.next_bank()
        L.eng.wait_ge(L.bank_full, L.fill)
        i, s = divmod(n, 24)
        L.eng.tensor_tensor(m.mods[i][:, 4 * s:4 * s + 4].rearrange("p (a b) -> p a b", b=2),
                            ps[:, :4].rearrange("p (a b) -> p a b", b=2),
                            bcast(m.vec("mod_b", 48 * i + 2 * s, 2), 2), ALU.add).then_inc(L.step, 1)
        L.eng.wait_ge(L.step, L.next_step())
        L.eng.sem_inc(L.bank_free, 1)


def mod_gains_vector(L, m, i):
    mod = m.mods[i].rearrange("p (a b) -> p a b", b=2)
    for n, g in ((0, "n1_g"), (1, "n2_g")):
        src = mod[:, 8 * (3 * n + 1):8 * (3 * n + 2), :]
        dst = m.modg[:, 16 * n:16 * n + 16].rearrange("p (a b) -> p a b", b=2)
        L.eng.tensor_scalar(dst, src, 1.0, None, ALU.add).then_inc(L.step, 1)
        L.eng.wait_ge(L.step, L.next_step())
        L.eng.tensor_tensor(dst, dst, bcast(m.vec(g, 8 * i, 8), 2), ALU.mult).then_inc(L.step, 1)
        L.eng.wait_ge(L.step, L.next_step())


def mod_col(m, i, part, w):
    return lambda c: m.mods[i][:, 2 * (8 * part + c) + w:2 * (8 * part + c) + w + 1]


def modnorm_tensor(L, m, B, ctx=True):
    norm_tensor(L, m, chunk(B.h, 0, T), KC)
    if ctx:
        norm_tensor(L, m, chunk(B.h, T, C), KC)


def modnorm_scalar(L, m, B, ctx=True):
    norm_scalar(L, m, chunk(m.x), chunk(B.h, 0, T), KC)
    if ctx:
        norm_scalar(L, m, chunk(m.xc), chunk(B.h, T, C), KC, root_used=True)


def modnorm_vector(L, m, B, i, n, ctx=True):
    for w, x in enumerate((m.x, m.xc)[:1 + ctx]):
        norm_vector(L, m, chunk(x), chunk(B.h, *BOTH[w]), KC,
                    lambda c: m.modg[:, 16 * n + 2 * c + w:16 * n + 2 * c + w + 1], mod_col(m, i, 3 * n, w), each=(i == n == 0))
        if w == 0 and ctx:
            L.eng.sem_inc(m.sem("root_used"), 1)
            L.nth("root_used")
        if n == 1:
            split_h_vector(L, m, B, *BOTH[w])


CHUNKS = KC + 4


def head_chunk(B, c):
    return B.q[:, c, :] if c < KC else B.k[:, c - KC, :]


def qkv_tensor(L, m, B):
    for c in range(CHUNKS + 2):
        if c < CHUNKS:
            if c % 2 == 0:
                w = L.next_slab(*(("qkv_q", c // 2) if c < KC else ("qkv_k", (c - KC) // 2)))
                L.eng.wait_ge(L.landed, L.landings)
            for lo, wd in BOTH:
                ps = L.next_bank()
                for bank_free, count in L.bank_frees:
                    L.eng.wait_ge(bank_free, count)
                pairs = [(w[:, k * 256 + c % 2 * P:k * 256 + c % 2 * P + P], B.h[:, k, lo:lo + wd]) for k in range(KC)]
                if c == 0:
                    ready_matmuls(L, m, ps[:, :wd], pairs).then_inc(L.bank_full, 1)
                else:
                    matmuls(L, ps[:, :wd], pairs).then_inc(L.bank_full, 1)
            if c % 2 == 1:
                L.eng.drain().then_inc(m.sem("slab_used"), 1)
        if c == CHUNKS:
            w = L.next_slab("qkv_v")
            L.eng.wait_ge(L.landed, L.landings)
            for t in range(6):
                ps = L.next_bank()
                for bank_free, count in L.bank_frees:
                    L.eng.wait_ge(bank_free, count)
                matmuls(L, ps[:, :256], [(B.h[:, k, t * P:(t + 1) * P], w[:, k * 256:(k + 1) * 256])
                                         for k in range(KC)]).then_inc(L.bank_full, 1)
            L.eng.drain().then_inc(m.sem("slab_used"), 1)
        if 1 <= c <= CHUNKS:
            L.eng.wait_ge(m.sem("squares"), L.nth("squares"))
            ps = L.next_bank(2)
            for bank_free, count in L.bank_frees:
                L.eng.wait_ge(bank_free, count)
            for lo, wd in BOTH:
                last = L.eng.matmul(ps[:, lo:lo + wd], m.tab("heads64"), B.sq[:, (c - 1) % 2, lo:lo + wd], start=True, stop=True)
            last.then_inc(L.bank_full, 1)
        if c >= 2:
            L.eng.wait_ge(m.sem("head_normed"), L.nth("head_normed"))
            ps = L.next_bank()
            for bank_free, count in L.bank_frees:
                L.eng.wait_ge(bank_free, count)
            L.eng.matmul(ps, m.tab("swap16"), head_chunk(B, c - 2)[:, 0:T], start=True, stop=True).then_inc(L.bank_full, 1)


def qkv_scalar(L, m, B):
    for c in range(CHUNKS + 2):
        if c < CHUNKS:
            L.next_bank()
            ps = L.next_bank()
            L.eng.wait_ge(L.bank_full, L.fill)
            L.eng.activation(head_chunk(B, c)[:, T:TC], ps[:, :C], ACT.Copy).then_inc(L.step, 1)
            L.eng.wait_ge(L.step, L.next_step())
            L.eng.sem_inc(L.bank_free, 1)
        if c == CHUNKS:
            read_banks(L, 6, odd, lambda g, ps: L.eng.activation(B.v[:, g, :], ps[:, :256], ACT.Copy))
        if 1 <= c <= CHUNKS:
            i = c - 1
            L.eng.wait_ge(m.sem("projected"), L.nth("projected"))
            L.eng.activation(B.sq[:, i % 2, :], head_chunk(B, i), ACT.Square).then_inc(m.sem("squares"), 1)
            L.eng.wait_ge(m.sem("squares"), L.nth("squares"))
            ps = L.next_bank(2)
            L.eng.wait_ge(L.bank_full, L.fill)
            if i >= 2:
                L.eng.wait_ge(m.sem("root_used"), L.nth("root_used"))
            L.eng.activation(B.root2[:, i % 2, :], ps[:, :TC], ACT.Sqrt, bias=m.tab("eps"), scale=1.0 / HD).then_inc(L.step, 1)
            L.eng.wait_ge(L.step, L.next_step())
            L.eng.sem_inc(L.bank_free, 1)
            L.eng.sem_inc(L.bank_free2, 1)
            L.eng.sem_inc(m.sem("root"), 1)
            L.nth("root")
        if c >= 2:
            L.next_bank()
    L.eng.wait_ge(m.sem("root_used"), L.nth("root_used", 2))


def qkv_vector(L, m, B):
    L.eng.wait_ge(m.sem("rope_ax"), L.nth("rope_ax", 16))
    for c in range(CHUNKS + 2):
        if c < CHUNKS:
            ps = L.next_bank()
            L.eng.wait_ge(L.bank_full, L.fill)
            L.eng.tensor_copy(head_chunk(B, c)[:, 0:T], ps).then_inc(m.sem("projected"), 1)
            L.eng.wait_ge(m.sem("projected"), L.nth("projected"))
            L.eng.sem_inc(L.bank_free, 1)
            L.next_bank()
        if c == CHUNKS:
            read_banks(L, 6, even, lambda g, ps: L.eng.tensor_copy(B.v[:, g, :], ps[:, :256]))
        if 1 <= c <= CHUNKS:
            x = head_chunk(B, c - 1)
            L.next_bank(2)
            L.eng.wait_ge(m.sem("root"), L.nth("root"))
            r = B.root2[:, (c - 1) % 2, :]
            L.eng.reciprocal(r, r).then_inc(L.step, 1)
            L.eng.wait_ge(L.step, L.next_step())
            L.eng.scalar_tensor_tensor(x, x, m.vec("q_gain" if c - 1 < KC else "k_gain"), r, ALU.mult, ALU.mult).then_inc(m.sem("root_used"), 1)
            L.eng.wait_ge(m.sem("root_used"), L.nth("root_used"))
            L.eng.sem_inc(m.sem("head_normed"), 1)
            L.nth("head_normed")
        if c >= 2:
            x = head_chunk(B, c - 2)[:, 0:T]
            ps = L.next_bank()
            L.eng.wait_ge(L.bank_full, L.fill)
            L.eng.tensor_tensor(B.rot, ps, B.rope[:, 1, :], ALU.mult).then_inc(L.step, 1)
            L.eng.wait_ge(L.step, L.next_step())
            L.eng.sem_inc(L.bank_free, 1)
            L.eng.tensor_tensor(x, x, B.rope[:, 0, :], ALU.mult).then_inc(L.step, 1)
            L.eng.wait_ge(L.step, L.next_step())
            L.eng.tensor_tensor(x, x, B.rot, ALU.add).then_inc(L.step, 1)
            L.eng.wait_ge(L.step, L.next_step())


def gqa_tensor(L, m, B, ctx):
    def score(ps, h, q):
        r = slice(64 * (h % 2), 64 * (h % 2) + 64)
        lo = T if ctx else 0
        lhs = B.q[r, h // 2, lo + q * P:lo + (q + 1) * P]
        for klo, w in ([NC_] if ctx else BOTH):
            o = klo - lo if ctx else klo
            last = L.eng.matmul(ps[:, o:o + w], lhs, B.k[r, h // 4, klo:klo + w], start=True, stop=True)
        return last
    first = 4 if ctx else 0
    attention_tensor(L, m, B.catt if ctx else B.att, score,
                     lambda h, kt, mt: B.v[:, first + kt, (h // 4) * HD:(h // 4 + 1) * HD])


def gqa_vector(L, m, B, ctx):
    lo, w = NC_ if ctx else NX
    attention_vector(L, m, B.catt if ctx else B.att,
                     lambda h, mt: B.o[64 * (h % 2):64 * (h % 2) + 64, h // 2, lo:lo + w])


def gated_add(L, m, i, part):
    def add(c, g, ps):
        w = BOTH[g][1]
        o = (m.x, m.xc)[g][:, c, :]
        return L.eng.scalar_tensor_tensor(o, ps[:, :w], mod_col(m, i, part, g)(c), o, ALU.mult, ALU.add)
    return add


def shift_vector(L, m, B):
    e = L.eng
    for lo, w in BOTH:
        h, x = B.h[:, :, lo:lo + w], B.xx[:, :, lo:lo + w]
        e.tensor_tensor(x[:, :, 1:w - 1], h[:, :, 0:w - 2], h[:, :, 2:w], ALU.add).then_inc(L.step, 1)
        L.eng.wait_ge(L.step, L.next_step())
        e.tensor_copy(x[:, :, 0:1], h[:, :, 1:2]).then_inc(L.step, 1)
        L.eng.wait_ge(L.step, L.next_step())
        e.tensor_copy(x[:, :, w - 1:w], h[:, :, w - 2:w - 1]).then_inc(L.step, 1)
        L.eng.wait_ge(L.step, L.next_step())
    for c in range(KC):
        e.scalar_tensor_tensor(B.xx[:, c, :], B.xx[:, c, :], 0.5, B.h[:, c, :], ALU.mult, ALU.subtract).then_inc(L.step, 1)
        L.eng.wait_ge(L.step, L.next_step())
    e.tensor_scalar(m.one_less_ka, m.vec("k_a", 0, 8), -1.0, 1.0, ALU.mult, ALU.add).then_inc(L.step, 1)
    L.eng.wait_ge(L.step, L.next_step())


def lerp_vector(L, m, B, j):
    for c in range(KC):
        L.eng.scalar_tensor_tensor(B.lp[:, c, :], B.xx[:, c, :], m.vec("lerp", 8 * j + c), B.h[:, c, :],
                                        ALU.mult, ALU.add).then_inc(m.sem("chunk_ready"), 1)
        L.eng.wait_ge(m.sem("chunk_ready"), L.nth("chunk_ready"))


def lora_tensor(L, m, B, w, at, groups):
    for i, (lo, wd) in enumerate(groups):
        ps = L.next_bank()
        for bank_free, count in L.bank_frees:
            L.eng.wait_ge(bank_free, count)
        pairs = [(w[:, at + k * P:at + (k + 1) * P], B.lp[:, k, lo:lo + wd]) for k in range(KC)]
        if i == 0:
            ready_matmuls(L, m, ps[:, :wd], pairs).then_inc(L.bank_full, 1)
        else:
            matmuls(L, ps[:, :wd], pairs).then_inc(L.bank_full, 1)


TT = TC // P
TX = T // P


def square(a, hh, tt, p):
    c = (TT * hh + tt) * CH
    return a[64 * p:64 * p + 64, c:c + CH]


def tok(a, hh, tt, p):
    return a[64 * p:64 * p + 64, tt * P + 64 * hh:tt * P + 64 * hh + 64]


def feat(a, hh, tt, p):
    return a[64 * hh:64 * hh + 64, tt * P + 64 * p:tt * P + 64 * p + 64]


def squares_tensor(L, hh, pairs, n=TT):
    ps = L.next_bank()
    for bank_free, count in L.bank_frees:
        L.eng.wait_ge(bank_free, count)
    for tt in range(n):
        for p in range(2):
            last = matmuls(L, ps[64 * p:64 * p + 64, tt * CH:(tt + 1) * CH], pairs(hh, tt, p))
    last.then_inc(L.bank_full, 1)


def feats_tensor(L, p, pairs, n=TT):
    ps = L.next_bank()
    for bank_free, count in L.bank_frees:
        L.eng.wait_ge(bank_free, count)
    for tt in range(n):
        for hh in range(2):
            last = matmuls(L, ps[64 * hh:64 * hh + 64, tt * CH:(tt + 1) * CH], pairs(hh, tt, p))
    last.then_inc(L.bank_full, 1)


TURNS = [(0, 4), (4, 6)]


def turn_pair_tensor(L, m, src, tiles):
    lo, hi = tiles
    ps = L.next_bank()
    for bank_free, count in L.bank_frees:
        L.eng.wait_ge(bank_free, count)
    for t in range(lo, hi):
        last = L.eng.transpose(ps[:, (t - lo) * P:(t - lo + 1) * P], src[:, t * P:(t + 1) * P], m.tab("ident"))
    last.then_inc(L.bank_full, 1)


def of_head(a, hh, n=TT):
    return a[:, TT * CH * hh:(TT * hh + n) * CH].rearrange("q (t c) -> q t c", c=CH)


def of_chunk(a, p, n=TT):
    return a[:, 0:n * P].rearrange("q (t p c) -> q t p c", p=2, c=CH)[:, :, p, :]


def tiled(a):
    return a.rearrange("p (a b) -> p a b", b=CH)


def over(mask, n):
    return mask.unsqueeze(1).to_broadcast([P, n, CH])


class Unit:

    def __init__(self, B, n):
        self.n, self.j, self.d = n, n // 2, n % 2
        d, j = self.d, self.j
        self.al, self.be, self.ka, self.rh = B.al[d], B.be[d], B.ka[d], B.rh[d]
        self.bk, self.ecol = B.bk[j % 2], B.ecol[d]
        b = B.load[j % 2]
        self.k, self.v, self.r = b[:, 0:TC], b[:, TC:2 * TC], b[:, 2 * TC:2 * TC + T]


UNITS = 2 * KC


def removal_raw_vector(L, m, B, u):
    L.eng.wait_ge(m.sem(f"pair_landed{u.j % 2}"), L.nth(f"pair_landed{u.j % 2}", 16))
    L.eng.tensor_scalar(B.lw, u.k, m.vec("k_k", u.j), None, ALU.mult).then_inc(m.sem("kk_raw"), 1)
    L.eng.wait_ge(m.sem("kk_raw"), L.nth("kk_raw"))


def removal_square_scalar(L, m, B, u):
    L.eng.wait_ge(m.sem("kk_raw"), L.nth("kk_raw"))
    L.eng.activation(B.cm, B.lw, ACT.Square).then_inc(m.sem("kk_squares"), 1)
    L.eng.wait_ge(m.sem("kk_squares"), L.nth("kk_squares"))


def removal_sum_tensor(L, m, B, u):
    L.eng.wait_ge(m.sem("kk_squares"), L.nth("kk_squares"))
    ps = L.next_bank(2)
    for bank_free, count in L.bank_frees:
        L.eng.wait_ge(bank_free, count)
    for lo, w in BOTH:
        last = L.eng.matmul(ps[:, lo:lo + w], m.tab("heads64"), B.cm[:, lo:lo + w], start=True, stop=True)
    last.then_inc(L.bank_full, 1)


def removal_floor_vector(L, m, B, u, ps, full, fill, free, free2):
    L.eng.wait_ge(full, fill)
    L.eng.tensor_scalar(B.cm, ps[:, :TC], 1e-24, None, ALU.max).then_inc(L.step, 1)
    L.eng.wait_ge(L.step, L.next_step())
    L.eng.sem_inc(free, 1)
    L.eng.sem_inc(free2, 1)
    L.eng.sem_inc(m.sem("kk_floor"), 1)
    L.nth("kk_floor")


def removal_root_scalar(L, m, B, u):
    L.eng.wait_ge(m.sem("kk_floor"), L.nth("kk_floor"))
    L.eng.activation(B.cm, B.cm, ACT.Sqrt).then_inc(m.sem("kk_root"), 1)
    L.eng.wait_ge(m.sem("kk_root"), L.nth("kk_root"))


def removal_key_vector(L, m, B, u):
    L.eng.wait_ge(m.sem("kk_root"), L.nth("kk_root"))
    L.eng.reciprocal(B.cm, B.cm).then_inc(L.step, 1)
    L.eng.wait_ge(L.step, L.next_step())
    L.eng.tensor_tensor(B.kk, B.lw, B.cm, ALU.mult).then_inc(m.sem("kk_done"), 1)
    L.eng.wait_ge(m.sem("kk_done"), L.nth("kk_done"))


def gates_tensor(L, m, B, u, w):
    r = slice(64 * u.d, 64 * u.d + 64)
    for at, src in ((0, B.tw), (D, B.ta)):
        ps = L.next_bank(2)
        for bank_free, count in L.bank_frees:
            L.eng.wait_ge(bank_free, count)
        for lo, wd in BOTH:
            last = L.eng.matmul(ps[:, lo:lo + wd], w[r, at + u.j * P:at + (u.j + 1) * P], src[r, lo:lo + wd],
                                start=True, stop=True)
        last.then_inc(L.bank_full, 1)


def gates_scalar(L, m, B, u):
    if u.n > 0:
        L.eng.wait_ge(m.sem("prepared"), L.nth("prepared"))
    if u.d == 0:
        L.eng.wait_ge(m.sem("kk_done"), L.nth("kk_done"))
    for dst, b in ((B.lw, "w0"), (u.be, "a0")):
        ps = L.next_bank(2)
        L.eng.wait_ge(L.bank_full, L.fill)
        L.eng.activation(dst, ps[:, :TC], ACT.Sigmoid, bias=m.vec(b, 8 * u.d + u.j)).then_inc(L.step, 1)
        L.eng.wait_ge(L.step, L.next_step())
        L.eng.sem_inc(L.bank_free, 1)
        L.eng.sem_inc(L.bank_free2, 1)
        L.eng.sem_inc(m.sem("gate_sigmoid"), 1)
        L.nth("gate_sigmoid")


def decay_sum_vector(L, m, B, u):
    e = L.eng
    L.eng.wait_ge(m.sem("gate_sigmoid"), L.nth("gate_sigmoid", 2))
    e.tensor_scalar(B.lw, B.lw, DECAY_SCALE, None, ALU.mult).then_inc(L.step, 1)
    L.eng.wait_ge(L.step, L.next_step())
    e.tensor_tensor_scan(u.al, B.keep, B.lw, 0.0, ALU.mult, ALU.add).then_inc(L.step, 1)
    L.eng.wait_ge(L.step, L.next_step())
    ci = tiled(u.al)
    e.tensor_copy(m.tot, ci[:, :, CH - 1:CH].rearrange("p a b -> p (a b)")).then_inc(L.step, 1)
    L.eng.wait_ge(L.step, L.next_step())
    if u.d == 1:
        e.tensor_tensor(u.al, B.lw, u.al, ALU.subtract).then_inc(L.step, 1)
        L.eng.wait_ge(L.step, L.next_step())
        e.tensor_tensor(ci, ci, bcast(m.tot, CH), ALU.add).then_inc(L.step, 1)
        L.eng.wait_ge(L.step, L.next_step())
    e.tensor_scalar(m.mid, m.tot, 0.5, None, ALU.mult).then_inc(L.step, 1)
    L.eng.wait_ge(L.step, L.next_step())


def decay_middle_vector(L, m, B, u):
    e = L.eng
    e.tensor_tensor(tiled(B.cm), tiled(u.al), bcast(m.mid, CH), ALU.subtract).then_inc(L.step, 1)
    L.eng.wait_ge(L.step, L.next_step())
    e.tensor_tensor(u.al, B.cm, B.lw, ALU.subtract).then_inc(L.step, 1)
    L.eng.wait_ge(L.step, L.next_step())
    e.memset(u.ecol, 0.0).then_inc(L.step, 1)
    L.eng.wait_ge(L.step, L.next_step())
    mid, n, x = m.mid, ALLCH, XCH
    spans = [((x, n - 1), (x + 1, n)), ((n - 1, n), (0, 1)), ((0, x - 1), (1, x))]
    if u.d == 1:
        spans = [((x + 1, n), (x, n - 1)), ((x, x + 1), (x - 1, x)), ((1, x), (0, x - 1))]
    for (a, b), (c, f) in spans:
        e.tensor_tensor(u.ecol[:, a:b], mid[:, a:b], mid[:, c:f], ALU.add).then_inc(L.step, 1)
        L.eng.wait_ge(L.step, L.next_step())
    L.eng.sem_inc(m.sem("decay_sum"), 1)
    L.nth("decay_sum")


def decay_exp_scalar(L, m, B, u):
    e = L.eng
    L.eng.wait_ge(m.sem("decay_sum"), L.nth("decay_sum"))
    e.activation(u.rh, B.cm[:, 0:T], ACT.Exp).then_inc(L.step, 1)
    L.eng.wait_ge(L.step, L.next_step())
    e.activation(B.cm, B.cm, ACT.Exp, scale=-1.0).then_inc(L.step, 1)
    L.eng.wait_ge(L.step, L.next_step())
    e.activation(u.al, u.al, ACT.Exp).then_inc(L.step, 1)
    L.eng.wait_ge(L.step, L.next_step())
    e.activation(u.ecol, u.ecol, ACT.Exp).then_inc(m.sem("decay_exp"), 1)
    L.eng.wait_ge(m.sem("decay_exp"), L.nth("decay_exp"))


def keys_vector(L, m, B, u):
    e = L.eng
    e.tensor_scalar(u.ka, u.be, m.vec("k_a", u.j), m.one_less_ka[:, u.j:u.j + 1], ALU.mult, ALU.add).then_inc(L.step, 1)
    L.eng.wait_ge(L.step, L.next_step())
    e.tensor_tensor(u.ka, u.ka, u.k, ALU.mult).then_inc(L.step, 1)
    L.eng.wait_ge(L.step, L.next_step())
    if u.d == 0:
        e.tensor_copy(u.bk, u.ka[:, 0:T]).then_inc(L.step, 1)
        L.eng.wait_ge(L.step, L.next_step())
    else:
        e.tensor_tensor(u.bk, u.bk, u.ka[:, 0:T], ALU.add).then_inc(L.step, 1)
        L.eng.wait_ge(L.step, L.next_step())
    e.tensor_tensor(u.be, B.kk, u.be, ALU.mult).then_inc(L.step, 1)
    L.eng.wait_ge(L.step, L.next_step())


def operands_vector(L, m, B, u, which):
    e = L.eng
    if which == 0:
        L.eng.wait_ge(m.sem("decay_exp"), L.nth("decay_exp"))
        e.tensor_tensor(u.al, B.kk, u.al, ALU.mult).then_inc(L.step, 1)
        L.eng.wait_ge(L.step, L.next_step())
    if which == 1:
        e.tensor_tensor(u.be, u.be, B.cm, ALU.mult).then_inc(L.step, 1)
        L.eng.wait_ge(L.step, L.next_step())
    if which == 2:
        e.tensor_tensor(u.ka, u.ka, B.cm, ALU.mult).then_inc(L.step, 1)
        L.eng.wait_ge(L.step, L.next_step())
    if which == 3:
        e.tensor_tensor(u.rh, u.r, u.rh, ALU.mult).then_inc(m.sem("prepared"), 1)
        L.eng.wait_ge(m.sem("prepared"), L.nth("prepared"))


def prepare_tensor(L, m, B, u, w):
    removal_sum_tensor(L, m, B, u)
    gates_tensor(L, m, B, u, w)


def prepare_scalar(L, m, B, u):
    removal_square_scalar(L, m, B, u)
    L.next_bank(2)
    removal_root_scalar(L, m, B, u)
    gates_scalar(L, m, B, u)
    decay_exp_scalar(L, m, B, u)


def prepare_vector(L, m, B, u):
    removal_raw_vector(L, m, B, u)
    ps = L.next_bank(2)
    removal_floor_vector(L, m, B, u, ps, L.bank_full, L.fill, L.bank_free, L.bank_free2)
    removal_key_vector(L, m, B, u)
    L.next_bank(2)
    L.next_bank(2)
    decay_sum_vector(L, m, B, u)
    decay_middle_vector(L, m, B, u)
    keys_vector(L, m, B, u)
    for which in range(4):
        operands_vector(L, m, B, u, which)


def chunk_order(d):
    x, c = list(range(XCH)), list(range(XCH, ALLCH))
    return c + x if d == 0 else c[::-1] + x[::-1]


def chain_tensor(L, m, B, u, i):
    L.eng.wait_ge(m.sem("state"), L.nth("state"))
    ps = L.next_bank()
    for bank_free, count in L.bank_frees:
        L.eng.wait_ge(bank_free, count)
    if i < ALLCH - 1:
        q = chunk_order(u.d)[i]
        for hh in range(2):
            r = slice(64 * hh, 64 * hh + 64)
            last = L.eng.matmul(ps[r, 0:CH], B.mt[r, q * CH:(q + 1) * CH], B.s[r, q * CH:(q + 1) * CH], start=True, stop=True)
    else:
        for q in range(XCH):
            for hh in range(2):
                at = (hh, q // 2, q % 2)
                last = L.eng.matmul(feat(ps, *at), feat(B.s, *at), feat(B.rp, *at), start=True, stop=True)
    last.then_inc(L.bank_full, 1)


def chain_start_vector(L, m, B, u):
    q = chunk_order(u.d)[0]
    L.eng.memset(B.s[:, q * CH:(q + 1) * CH], 0.0).then_inc(m.sem("state"), 1)
    L.eng.wait_ge(m.sem("state"), L.nth("state"))


def chain_vector(L, m, B, u, i):
    ps = L.next_bank()
    L.eng.wait_ge(L.bank_full, L.fill)
    if i < ALLCH - 1:
        q, nq = chunk_order(u.d)[i:i + 2]
        L.eng.scalar_tensor_tensor(B.s[:, nq * CH:(nq + 1) * CH], ps[:, 0:CH], u.ecol[:, q:q + 1],
                                   B.g[:, q * CH:(q + 1) * CH], ALU.mult, ALU.add).then_inc(m.sem("state"), 1)
        L.eng.wait_ge(m.sem("state"), L.nth("state"))
    else:
        L.eng.tensor_tensor(B.yj, B.yj, ps, ALU.add).then_inc(m.sem("read_out"), 1)
        L.eng.wait_ge(m.sem("read_out"), L.nth("read_out"))
    L.eng.sem_inc(L.bank_free, 1)


LEVELS = (2, 4, 8, 16, 32)
FIRST = 10


def unit_tensor(L, m, B, u, before, done, after, w2, g2):
    L.eng.wait_ge(m.sem("prepared"), L.nth("prepared"))
    at_bank = 0
    for lhs, rhs, n in ((u.be, u.al, TT), (u.al, u.be, TT), (u.ka, u.al, TT), (u.be, u.rh, TX), (u.ka, u.rh, TX)):
        for hh in range(2):
            squares_tensor(L, hh, lambda *at: [(feat(lhs, *at), feat(rhs, *at))], n)
            if before is not None:
                chain_tensor(L, m, B, before, at_bank)
            at_bank += 1
    if u.d == 0:
        for tiles in TURNS:
            turn_pair_tensor(L, m, u.v, tiles)
    for k, src in enumerate((u.al, u.be, u.ka)):
        for tiles in TURNS:
            turn_pair_tensor(L, m, src, tiles)
        if before is not None and k < 2:
            chain_tensor(L, m, B, before, FIRST + k)
    if done is not None:
        readout_mean_tensor(L, m, B)
    if u.d == 0:
        L.eng.wait_ge(m.sem("values_turned"), L.nth("values_turned", 2))
    for hh in range(2):
        L.eng.wait_ge(m.sem("masked"), L.nth("masked"))
        squares_tensor(L, hh, lambda *at: [(square(B.akt, *at), tok(B.vtok, *at))])
    if done is not None:
        readout_tensor(L, m, B, done, g2)
    if after is not None and after.d == 0:
        removal_sum_tensor(L, m, B, after)
    for lv in LEVELS:
        for hh in range(2):
            L.eng.wait_ge(m.sem("inverse"), L.nth("inverse", 2))
            squares_tensor(L, hh, lambda *at: [(square(B.nt, *at), square(B.ti, *at))])
        for hh in range(2):
            L.eng.wait_ge(m.sem("corner"), L.nth("corner"))
            if lv != LEVELS[-1]:
                squares_tensor(L, hh, lambda *at: [(square(B.tt, *at), square(B.x, *at))])
            squares_tensor(L, hh, lambda *at: [(square(B.x, *at), square(B.tt, *at))])
        if after is not None and lv == LEVELS[1]:
            gates_tensor(L, m, B, after, w2)
    L.eng.wait_ge(m.sem("turned"), L.nth("turned", 8))
    for hh in range(2):
        L.eng.wait_ge(m.sem("inverse"), L.nth("inverse"))
        squares_tensor(L, hh, lambda *at: [(square(B.tt, *at), tok(B.altok, *at))])
        squares_tensor(L, hh, lambda *at: [(square(B.tt, *at), square(B.akv, *at))])
    L.eng.wait_ge(m.sem("solved"), L.nth("solved", 4))
    for p in range(2):
        feats_tensor(L, p, lambda *at: [(square(B.ua, *at), tok(B.betok, *at))])
        feats_tensor(L, p, lambda *at: [(tok(B.betok, *at), square(B.uv, *at)), (tok(B.katok, *at), tok(B.vtok, *at))])
    for p in range(2):
        feats_tensor(L, p, lambda *at: [(square(B.ua, *at), square(B.rbt, *at))], TX)
        feats_tensor(L, p, lambda *at: [(square(B.uv, *at), square(B.rbt, *at)), (tok(B.vtok, *at), square(B.rkt, *at))], TX)


def unit_scalar(L, m, B, u, before, done, after):
    def copy(dst, src, scale, what):
        L.eng.activation(dst, src, ACT.Copy, scale=scale).then_inc(L.step, 1)
        L.eng.wait_ge(L.step, L.next_step())
        L.eng.sem_inc(L.bank_free, 1)
        L.eng.sem_inc(m.sem(what), 1)
        L.nth(what)

    for _ in range(FIRST * (1 if before is None else 2)):
        L.next_bank()
    for k, (dst, what) in enumerate(([(B.vtok, "values_turned")] if u.d == 0 else []) +
                                    [(B.altok, "turned"), (B.betok, "turned"), (B.katok, "turned")]):
        for lo, hi in TURNS:
            ps = L.next_bank()
            L.eng.wait_ge(L.bank_full, L.fill)
            copy(dst[:, lo * P:hi * P], ps[:, :(hi - lo) * P], 1.0, what)
        if before is not None and (dst is B.altok or dst is B.betok):
            L.next_bank()
    if after is not None and after.d == 0:
        removal_square_scalar(L, m, B, after)
    if done is not None:
        L.next_bank()
        readout_squares_scalar(L, m, B)
    for hh in range(2):
        ps = L.next_bank()
        L.eng.wait_ge(L.bank_full, L.fill)
        copy(of_head(B.akv, hh), tiled(ps[:, :TT * CH]), 1.0, "turned")
    if done is not None:
        readout_root_scalar(L, m, B)
    if after is not None and after.d == 0:
        L.next_bank(2)
        removal_root_scalar(L, m, B, after)
    for lv in LEVELS:
        for _ in range(6 if lv != LEVELS[-1] else 4):
            L.next_bank()
        if after is not None and lv == LEVELS[1]:
            gates_scalar(L, m, B, after)
    if after is not None:
        decay_exp_scalar(L, m, B, after)
    for hh in range(2):
        for dst in (B.ua, B.uv):
            ps = L.next_bank()
            L.eng.wait_ge(L.bank_full, L.fill)
            copy(of_head(dst, hh), tiled(ps[:, :TT * CH]), -1.0, "solved")
    for _ in range(8):
        L.next_bank()


def unit_vector(L, m, B, u, before, done, after):
    e = L.eng
    d = u.d

    def mask(k):
        return B.masks[:, k * CH:(k + 1) * CH]

    def read(dst, fn):
        ps = L.next_bank()
        L.eng.wait_ge(L.bank_full, L.fill)
        n = dst.shape[1]
        fn(dst, tiled(ps[:, :CH * n]), n).then_inc(L.step, 1)
        L.eng.wait_ge(L.step, L.next_step())
        L.eng.sem_inc(L.bank_free, 1)

    def masked(k):
        return lambda o, ps, n: e.tensor_tensor(o, ps, over(mask(k), n), ALU.mult)

    def chain(i):
        if before is not None:
            chain_vector(L, m, B, before, i)

    first, upto = MASK["before"][d], MASK["upto"][d]
    if before is not None:
        chain_start_vector(L, m, B, before)
    for hh in range(2):
        read(of_head(B.nt, hh), masked(first))
        x, t, nt = [of_head(a, hh) for a in (B.x, B.tt, B.nt)]
        chain(hh)
        e.tensor_tensor(x, nt, over(mask(4 + 1 - d), TT), ALU.mult).then_inc(L.step, 1)
        L.eng.wait_ge(L.step, L.next_step())
        e.tensor_tensor(t, over(B.eye, TT), x, ALU.subtract).then_inc(L.step, 1)
        L.eng.wait_ge(L.step, L.next_step())
    for hh in range(2):
        x, t = of_head(B.x, hh), of_head(B.ti, hh)
        read(x, masked(4 + d))
        chain(2 + hh)
        e.tensor_tensor(t, over(B.eye, TT), x, ALU.subtract).then_inc(m.sem("inverse"), 1)
        L.eng.wait_ge(m.sem("inverse"), L.nth("inverse"))
        L.eng.sem_inc(m.sem("inverse"), 1)
        L.nth("inverse")
    for hh in range(2):
        read(of_head(B.akt, hh), masked(first))
        L.eng.sem_inc(m.sem("masked"), 1)
        L.nth("masked")
        chain(4 + hh)
    for k, dst in enumerate((B.rbt, B.rkt)):
        for hh in range(2):
            read(of_head(dst, hh, TX), masked(upto))
            chain(6 + 2 * k + hh)
    if u.d == 0:
        L.next_bank()
        L.next_bank()
    for k in range(3):
        L.next_bank()
        L.next_bank()
        if k < 2:
            chain(FIRST + k)
    if after is not None and after.d == 0:
        removal_raw_vector(L, m, B, after)
    if done is not None:
        readout_centre_vector(L, m, B, done)
    L.next_bank()
    L.next_bank()
    if done is not None:
        L.next_bank()
        bonus = L.next_bank(), L.bank_full, L.fill, L.bank_free
        gate = L.next_bank(), L.bank_full, L.fill, L.bank_free
    if after is not None and after.d == 0:
        norm = L.next_bank(2), L.bank_full, L.fill, L.bank_free, L.bank_free2
    for i, lv in enumerate(LEVELS):
        for hh in range(2):
            read(of_head(B.x, hh), masked(6 + 2 * i + d))
            L.eng.sem_inc(m.sem("corner"), 1)
            L.nth("corner")
        if lv == LEVELS[0]:
            if done is not None:
                readout_vector(L, m, B, done, bonus, gate)
            if after is not None and after.d == 0:
                removal_floor_vector(L, m, B, after, *norm)
        for hh in range(2):
            for dst in ((B.ti, B.tt) if lv != LEVELS[-1] else (B.tt,)):
                read(of_head(dst, hh), lambda o, ps, n: e.tensor_tensor(o, o, ps, ALU.subtract))
                L.eng.sem_inc(m.sem("inverse"), 1)
                L.nth("inverse")
        if after is not None:
            if lv == LEVELS[1]:
                if after.d == 0:
                    removal_key_vector(L, m, B, after)
                L.next_bank(2)
                L.next_bank(2)
            if lv == LEVELS[2]:
                decay_sum_vector(L, m, B, after)
            if lv == LEVELS[3]:
                decay_middle_vector(L, m, B, after)
    for _ in range(4):
        L.next_bank()
    if after is not None:
        keys_vector(L, m, B, after)
    ecol = u.ecol.rearrange("q (t p) -> q t p", p=2)
    for p in range(2):
        read(of_chunk(B.mt, p), lambda o, ps, n: e.tensor_tensor(o, ps, over(B.eye, n), ALU.add))
        read(of_chunk(B.g, p), lambda o, ps, n: e.tensor_tensor(o, ps, bcast(ecol[:, :, p], CH), ALU.mult))
        if after is not None:
            operands_vector(L, m, B, after, 2 * p)
            operands_vector(L, m, B, after, 2 * p + 1)
    for p in range(2):
        read(of_chunk(B.rp, p, TX), lambda o, ps, n: e.tensor_tensor(o, ps, of_chunk(u.rh, p, TX), ALU.add))
        y = of_chunk(B.yj, p, TX)
        if d == 0:
            read(y, lambda o, ps, n: e.tensor_copy(o, ps))
        else:
            read(y, lambda o, ps, n: e.tensor_tensor(o, o, ps, ALU.add))


def readout_mean_tensor(L, m, B):
    L.eng.wait_ge(m.sem("read_out"), L.nth("read_out", 2))
    ps = L.next_bank()
    for bank_free, count in L.bank_frees:
        L.eng.wait_ge(bank_free, count)
    L.eng.matmul(ps, m.tab("heads64"), B.yj, start=True, stop=True).then_inc(L.bank_full, 1)


def readout_tensor(L, m, B, u, g2):
    ones = m.tab("heads64")
    L.eng.wait_ge(m.sem("centred_squares"), L.nth("centred_squares"))
    ps = L.next_bank()
    for bank_free, count in L.bank_frees:
        L.eng.wait_ge(bank_free, count)
    L.eng.matmul(ps, ones, B.ua[:, 0:T], start=True, stop=True).then_inc(L.bank_full, 1)
    L.eng.wait_ge(m.sem("bonus"), L.nth("bonus"))
    ps = L.next_bank()
    for bank_free, count in L.bank_frees:
        L.eng.wait_ge(bank_free, count)
    L.eng.matmul(ps, ones, u.bk, start=True, stop=True).then_inc(L.bank_full, 1)
    ps = L.next_bank()
    for bank_free, count in L.bank_frees:
        L.eng.wait_ge(bank_free, count)
    L.eng.matmul(ps, g2[:, u.j * P:(u.j + 1) * P], B.tg, start=True, stop=True).then_inc(L.bank_full, 1)


def readout_squares_scalar(L, m, B):
    L.eng.wait_ge(m.sem("centred"), L.nth("centred"))
    L.eng.activation(B.ua[:, 0:T], B.yj, ACT.Square).then_inc(m.sem("centred_squares"), 1)
    L.eng.wait_ge(m.sem("centred_squares"), L.nth("centred_squares"))


def readout_root_scalar(L, m, B):
    ps = L.next_bank()
    L.eng.wait_ge(L.bank_full, L.fill)
    L.eng.activation(B.uv[:, 0:T], ps, ACT.Sqrt, bias=m.tab("gn_eps"), scale=1.0 / 64).then_inc(L.step, 1)
    L.eng.wait_ge(L.step, L.next_step())
    L.eng.sem_inc(L.bank_free, 1)
    L.eng.sem_inc(m.sem("gn_root"), 1)
    L.nth("gn_root")
    L.next_bank()
    L.next_bank()


def readout_centre_vector(L, m, B, u):
    ps = L.next_bank()
    L.eng.wait_ge(L.bank_full, L.fill)
    L.eng.scalar_tensor_tensor(B.yj, ps, -1.0 / 64, B.yj, ALU.mult, ALU.add).then_inc(L.step, 1)
    L.eng.wait_ge(L.step, L.next_step())
    L.eng.sem_inc(L.bank_free, 1)
    L.eng.sem_inc(m.sem("centred"), 1)
    L.nth("centred")
    L.eng.scalar_tensor_tensor(u.bk, u.bk, m.vec("r_k", u.j), u.r, ALU.mult, ALU.mult).then_inc(m.sem("bonus"), 1)
    L.eng.wait_ge(m.sem("bonus"), L.nth("bonus"))


def readout_vector(L, m, B, u, bonus, gate):
    e = L.eng
    r, b = B.uv[:, 0:T], B.ua[:, 0:T]
    L.eng.wait_ge(m.sem("gn_root"), L.nth("gn_root"))
    ps, full, fill, free = bonus
    L.eng.wait_ge(full, fill)
    e.tensor_tensor(b, u.v[:, 0:T], ps, ALU.mult).then_inc(L.step, 1)
    L.eng.wait_ge(L.step, L.next_step())
    L.eng.sem_inc(free, 1)
    e.reciprocal(r, r).then_inc(L.step, 1)
    L.eng.wait_ge(L.step, L.next_step())
    e.tensor_tensor(B.yj, B.yj, r, ALU.mult).then_inc(L.step, 1)
    L.eng.wait_ge(L.step, L.next_step())
    e.tensor_scalar(B.yj, B.yj, m.vec("ln_g", u.j), m.vec("ln_b", u.j), ALU.mult, ALU.add).then_inc(L.step, 1)
    L.eng.wait_ge(L.step, L.next_step())
    e.tensor_tensor(B.yj, B.yj, b, ALU.add).then_inc(L.step, 1)
    L.eng.wait_ge(L.step, L.next_step())
    ps, full, fill, free = gate
    L.eng.wait_ge(full, fill)
    e.tensor_tensor(B.out[:, u.j, :], B.yj, ps, ALU.mult).then_inc(L.step, 1)
    L.eng.wait_ge(L.step, L.next_step())
    L.eng.sem_inc(free, 1)
    L.eng.sem_inc(m.sem("pair_read_out"), 1)
    L.nth("pair_read_out")


def around(B, n):
    unit = lambda k: Unit(B, k) if 0 <= k < UNITS else None
    u = unit(n)
    return u, unit(n - 1), (unit(n - 1) if u.d == 0 else None), unit(n + 1)


def recurrence_tensor(L, m, B, w2, g2):
    prepare_tensor(L, m, B, Unit(B, 0), w2)
    for n in range(UNITS):
        unit_tensor(L, m, B, *around(B, n), w2, g2)
    last = Unit(B, UNITS - 1)
    for i in range(ALLCH):
        chain_tensor(L, m, B, last, i)
    readout_mean_tensor(L, m, B)
    readout_tensor(L, m, B, last, g2)


def recurrence_scalar(L, m, B):
    prepare_scalar(L, m, B, Unit(B, 0))
    for n in range(UNITS):
        unit_scalar(L, m, B, *around(B, n))
    for i in range(ALLCH + 1):
        L.next_bank()
    readout_squares_scalar(L, m, B)
    readout_root_scalar(L, m, B)


def recurrence_vector(L, m, B):
    prepare_vector(L, m, B, Unit(B, 0))
    for n in range(UNITS):
        unit_vector(L, m, B, *around(B, n))
    last = Unit(B, UNITS - 1)
    chain_start_vector(L, m, B, last)
    for i in range(ALLCH):
        chain_vector(L, m, B, last, i)
    readout_centre_vector(L, m, B, last)
    L.next_bank()
    bonus = L.next_bank(), L.bank_full, L.fill, L.bank_free
    gate = L.next_bank(), L.bank_full, L.fill, L.bank_free
    readout_vector(L, m, B, last, bonus, gate)


def build(nc, a):
    with ExitStack() as ctx:
        m = Mem(nc, ctx)
        ring_place = -(-nc.sbuf_base // 32) * 32
        m.ring = m.sb("ring", [P, SLOTS, SLAB])
        m.low = nc.alloc_sbuf_tensor_at("ring_low", [P, SLOTS, SLAB], F32R, offset=ring_place)
        m.x = m.sb("x_residual", [P, KC, T])
        m.xc = m.sb("ctx_residual", [P, KC, C])
        m.vecs = m.sb("vecs", [P, NVEC])
        m.tabs = m.sb("tabs", [P, RESIDENT])
        m.root = m.sb("root", [P, T])
        m.stat = m.sb("stat", [P, 16])
        m.cond = m.sb("cond", [P, KC, 32])
        m.mods = [m.sb(f"mod{i}", [P, 96])[:, :] for i in range(2)]
        m.modg = m.sb("modg", [P, 32])
        m.one_less_ka = m.sb("one_less_ka", [P, 8])
        m.tot, m.mid = [m.sb(n, [P, ALLCH])[:, :] for n in ("chunk_total", "chunk_middle")]
        m.ecol = [m.sb(f"chunk_carry{d}", [P, ALLCH])[:, :] for d in range(2)]
        m.modg, m.root, m.one_less_ka = [t[:, :] for t in (m.modg, m.root, m.one_less_ka)]
        m.arena_place = -(-nc.sbuf_base // 32) * 32
        m.arena = m.sb("arena", [P, ARENA])
        m.psum = ctx.enter_context(nc.psum_tensor("psum", [P, 8 * BANK], F32))
        m.bank_full = [m.sem(f"bank_full{b}") for b in range(8)]
        m.bank_free = [m.sem(f"bank_free{b}") for b in range(8)]
        m.slab_landed = [m.sem(f"slab_landed{s}") for s in range(SLOTS)]
        m.mod_rows = m.at(HIGH - 512, 2, 256)
        m.high = m.rounded("slab_high", HIGH, SLOTS, SLAB)
        B, R = Block1(m), Block2(m)
        wall = a["wall"]

        block = ctx.enter_context(nc.Block())

        @block.sync
        def _(sp):
            sp.dma_start(m.x[:, 0:KC // 2, :], a["x"][:, 0:KC // 2, :]).then_inc(m.sem("x_landed"), 16)
            for n in range(NSLAB):
                if n >= SLOTS:
                    sp.wait_ge(m.sem("slab_used"), n - SLOTS + 1)
                sp.dma_start(m.ring[:, n % SLOTS, :], wall[n]).then_inc(m.slab_landed[n % SLOTS], 16)

        @block.gpsimd
        def _(pool):
            L = Lane(m, pool, "pool")
            load = lambda dst, src, what: pool.dma_start(dst, src).then_inc(m.sem(what), 16)
            tab = lambda name, n: a["tabs"][:, TCOL[name][0]:TCOL[name][0] + n]
            load(m.vecs[:, :], a["vecs"], "inputs_landed")
            load(m.tabs[:, :], a["tabs"][:, 0:RESIDENT], "inputs_landed")
            load(m.xc[:, :, :], a["ctx"], "inputs_landed")
            load(m.at(28184, 1024), tab("cos96", 1024), "rope96")
            L.eng.wait_ge(m.sem("room_for_dft"), L.nth("room_for_dft"))
            load(B.dft, tab("dft_c", 5248), "dft_landed")
            L.eng.wait_ge(m.sem("room_for_mem"), L.nth("room_for_mem"))
            load(B.mem, a["mem"], "mem_landed")
            split_slabs(L, m, "moe")
            L.eng.wait_ge(m.sem("room_for_rope"), L.nth("room_for_rope"))
            load(R.rope, tab("cos_ax", 1024).rearrange("p (a b) -> p a b", a=2), "rope_ax")
            split_slabs(L, m, "ffn0")
            spill = a["spill"]
            L.eng.wait_ge(m.sem("kv_ready"), L.nth("kv_ready"))
            pool.dma_start(spill[:, :, 0:TC], R.pk).then_inc(m.sem("spilled"), 16)
            pool.dma_start(spill[:, :, TC:2 * TC], R.pv).then_inc(m.sem("spilled"), 16)
            L.eng.wait_ge(m.sem("r_ready"), L.nth("r_ready"))
            pool.dma_start(spill[:, :, 2 * TC:2 * TC + T], R.pr).then_inc(m.sem("spilled"), 16)
            pool.wait_ge(m.sem("spilled"), 48)
            load(R.masks, tab("masks", 1024), "wkv_tables")
            load(R.eye, tab("eye", 64), "wkv_tables")
            load(R.keep, tab("scan_keep", TC), "wkv_tables")
            for j in range(KC):
                if j >= 2:
                    L.eng.wait_ge(m.sem("pair_read_out"), L.nth("pair_read_out"))
                load(R.load[j % 2], spill[:, j, :], f"pair_landed{j % 2}")
            split_slabs(L, m, "ffn1")
            L.eng.wait_ge(m.sem("result"), L.nth("result"))
            pool.dma_start(a["out"], m.x[:, :, :]).then_inc(m.sem("out_stored"), 16)
            pool.wait_ge(m.sem("out_stored"), 16)

        @block.tensor
        def _(pe):
            L = Lane(m, pe, "tensor")
            L.eng.wait_ge(m.sem("inputs_landed"), L.nth("inputs_landed", 48))
            mix_in_tensor(L, m, B)
            pe.wait_ge(m.sem("vector_stage_done"), L.nth("vector_stage_done"))
            pe.wait_ge(m.sem("scalar_stage_done"), L.nth("scalar_stage_done"))
            latent_tensor(L, m, B)
            pe.wait_ge(m.sem("vector_stage_done"), L.nth("vector_stage_done"))
            pe.wait_ge(m.sem("scalar_stage_done"), L.nth("scalar_stage_done"))
            latent_attention_tensor(L, m, B)
            pe.wait_ge(m.sem("vector_stage_done"), L.nth("vector_stage_done"))
            pe.wait_ge(m.sem("scalar_stage_done"), L.nth("scalar_stage_done"))
            norm_tensor(L, m, chunk(B.mix), 4)
            pe.wait_ge(m.sem("vector_stage_done"), L.nth("vector_stage_done"))
            pe.wait_ge(m.sem("scalar_stage_done"), L.nth("scalar_stage_done"))
            conv_turn_tensor(L, m, B)
            pe.wait_ge(m.sem("vector_stage_done"), L.nth("vector_stage_done"))
            pe.wait_ge(m.sem("scalar_stage_done"), L.nth("scalar_stage_done"))
            filter_tensor(L, m, B)
            pe.wait_ge(m.sem("vector_stage_done"), L.nth("vector_stage_done"))
            pe.wait_ge(m.sem("scalar_stage_done"), L.nth("scalar_stage_done"))
            L.eng.drain().then_inc(m.sem("slab_used"), 1)
            L.eng.drain().then_inc(m.sem("slab_used"), 1)
            for order in range(2):
                pe.wait_ge(m.sem("vector_stage_done"), L.nth("vector_stage_done"))
                pe.wait_ge(m.sem("scalar_stage_done"), L.nth("scalar_stage_done"))
                filter_spectrum_tensor(L, m, B, order)
                pe.wait_ge(m.sem("vector_stage_done"), L.nth("vector_stage_done"))
                pe.wait_ge(m.sem("scalar_stage_done"), L.nth("scalar_stage_done"))
                product_tensor(L, m, B)
                pe.wait_ge(m.sem("vector_stage_done"), L.nth("vector_stage_done"))
                pe.wait_ge(m.sem("scalar_stage_done"), L.nth("scalar_stage_done"))
                if order == 0:
                    inverse0_tensor(L, m, B)
                    pe.wait_ge(m.sem("vector_stage_done"), L.nth("vector_stage_done"))
                    pe.wait_ge(m.sem("scalar_stage_done"), L.nth("scalar_stage_done"))
                    L.eng.drain().then_inc(m.sem("slab_used"), 1)
                    turn_tensor(L, m, lambda d, i: B.vt[:, i, d * P:(d + 1) * P], 4)
                    pe.wait_ge(m.sem("vector_stage_done"), L.nth("vector_stage_done"))
                    pe.wait_ge(m.sem("scalar_stage_done"), L.nth("scalar_stage_done"))
            inverse1_tensor(L, m, B)
            pe.wait_ge(m.sem("vector_stage_done"), L.nth("vector_stage_done"))
            pe.wait_ge(m.sem("scalar_stage_done"), L.nth("scalar_stage_done"))
            norm_tensor(L, m, lambda c: B.mix[:, 4 + c, :], 4)
            pe.wait_ge(m.sem("vector_stage_done"), L.nth("vector_stage_done"))
            pe.wait_ge(m.sem("scalar_stage_done"), L.nth("scalar_stage_done"))
            project_tensor(L, m, "out", chunk(B.mix), [(0, T)])
            pe.wait_ge(m.sem("vector_stage_done"), L.nth("vector_stage_done"))
            pe.wait_ge(m.sem("scalar_stage_done"), L.nth("scalar_stage_done"))
            memory_tensor(L, m, B)
            pe.wait_ge(m.sem("vector_stage_done"), L.nth("vector_stage_done"))
            pe.wait_ge(m.sem("scalar_stage_done"), L.nth("scalar_stage_done"))
            memory_attention_tensor(L, m, B)
            pe.wait_ge(m.sem("vector_stage_done"), L.nth("vector_stage_done"))
            pe.wait_ge(m.sem("scalar_stage_done"), L.nth("scalar_stage_done"))
            project_tensor(L, m, "mo", chunk(B.mo), [(0, T)])
            pe.wait_ge(m.sem("vector_stage_done"), L.nth("vector_stage_done"))
            pe.wait_ge(m.sem("scalar_stage_done"), L.nth("scalar_stage_done"))
            route_tensor(L, m, B)
            pe.wait_ge(m.sem("vector_stage_done"), L.nth("vector_stage_done"))
            pe.wait_ge(m.sem("scalar_stage_done"), L.nth("scalar_stage_done"))
            swiglu_tensor(L, m, "moe", GROUPS * EXPERTS, B, [NX], B.cmbt)
            pe.wait_ge(m.sem("vector_stage_done"), L.nth("vector_stage_done"))
            pe.wait_ge(m.sem("scalar_stage_done"), L.nth("scalar_stage_done"))
            norm_tensor(L, m, chunk(B.h), KC)
            pe.wait_ge(m.sem("vector_stage_done"), L.nth("vector_stage_done"))
            pe.wait_ge(m.sem("scalar_stage_done"), L.nth("scalar_stage_done"))

            for i in range(2):
                modnorm_tensor(L, m, R)
                L.nth("vector_stage_done")
                L.nth("scalar_stage_done")
                if i == 0:
                    qkv_tensor(L, m, R)
                    pe.wait_ge(m.sem("vector_stage_done"), L.nth("vector_stage_done"))
                    pe.wait_ge(m.sem("scalar_stage_done"), L.nth("scalar_stage_done"))
                    for ctx_side in (False, True):
                        gqa_tensor(L, m, R, ctx_side)
                        pe.wait_ge(m.sem("vector_stage_done"), L.nth("vector_stage_done"))
                        pe.wait_ge(m.sem("scalar_stage_done"), L.nth("scalar_stage_done"))
                    project_tensor(L, m, "wo0", chunk(R.o), BOTH)
                    pe.wait_ge(m.sem("vector_stage_done"), L.nth("vector_stage_done"))
                    pe.wait_ge(m.sem("scalar_stage_done"), L.nth("scalar_stage_done"))
                else:
                    pe.wait_ge(m.sem("vector_stage_done"), L.nth("vector_stage_done"))
                    pe.wait_ge(m.sem("scalar_stage_done"), L.nth("scalar_stage_done"))
                    for name in ("rw_k", "rw_v"):
                        project_tensor(L, m, name, chunk(R.lp), BOTH, ready=1)
                        pe.wait_ge(m.sem("vector_stage_done"), L.nth("vector_stage_done"))
                        pe.wait_ge(m.sem("scalar_stage_done"), L.nth("scalar_stage_done"))
                    w = L.next_slab("lora1")
                    L.eng.wait_ge(L.landed, L.landings)
                    for part in range(2):
                        lora_tensor(L, m, R, w, part * D, BOTH)
                        pe.wait_ge(m.sem("vector_stage_done"), L.nth("vector_stage_done"))
                        pe.wait_ge(m.sem("scalar_stage_done"), L.nth("scalar_stage_done"))
                    L.eng.drain().then_inc(m.sem("slab_used"), 1)
                    w = L.next_slab("g1")
                    L.eng.wait_ge(L.landed, L.landings)
                    lora_tensor(L, m, R, w, 0, [NX])
                    L.eng.drain().then_inc(m.sem("slab_used"), 1)
                    pe.wait_ge(m.sem("vector_stage_done"), L.nth("vector_stage_done"))
                    pe.wait_ge(m.sem("scalar_stage_done"), L.nth("scalar_stage_done"))
                    project_tensor(L, m, "rw_r", chunk(R.lp), [NX], ready=1)
                    pe.wait_ge(m.sem("vector_stage_done"), L.nth("vector_stage_done"))
                    pe.wait_ge(m.sem("scalar_stage_done"), L.nth("scalar_stage_done"))
                    w2 = L.next_slab("lora2")
                    L.eng.wait_ge(L.landed, L.landings)
                    g2 = L.next_slab("g2")
                    L.eng.wait_ge(L.landed, L.landings)
                    recurrence_tensor(L, m, R, w2, g2)
                    pe.wait_ge(m.sem("vector_stage_done"), L.nth("vector_stage_done"))
                    pe.wait_ge(m.sem("scalar_stage_done"), L.nth("scalar_stage_done"))
                    L.eng.drain().then_inc(m.sem("slab_used"), 1)
                    L.eng.drain().then_inc(m.sem("slab_used"), 1)
                    project_tensor(L, m, "wo1", chunk(R.out), [NX])
                    pe.wait_ge(m.sem("vector_stage_done"), L.nth("vector_stage_done"))
                    pe.wait_ge(m.sem("scalar_stage_done"), L.nth("scalar_stage_done"))
                modnorm_tensor(L, m, R, i == 0)
                L.nth("vector_stage_done")
                L.nth("scalar_stage_done")
                swiglu_tensor(L, m, f"ffn{i}", FF // 256, R, BOTH[:2 - i])
                pe.wait_ge(m.sem("vector_stage_done"), L.nth("vector_stage_done"))
                pe.wait_ge(m.sem("scalar_stage_done"), L.nth("scalar_stage_done"))
            norm_tensor(L, m, chunk(R.h, 0, T), KC)
            pe.wait_ge(m.sem("vector_stage_done"), L.nth("vector_stage_done"))
            pe.wait_ge(m.sem("scalar_stage_done"), L.nth("scalar_stage_done"))

        @block.scalar
        def _(act):
            L = Lane(m, act, "scalar")
            act.dma_start(m.x[:, KC // 2:, :], a["x"][:, KC // 2:, :]).then_inc(m.sem("x_landed_too"), 16)
            L.eng.wait_ge(m.sem("inputs_landed"), L.nth("inputs_landed", 48))
            L.eng.wait_ge(m.sem("x_landed"), 16)
            L.eng.wait_ge(m.sem("x_landed_too"), 16)

            def copy(dst):
                return lambda g, ps: act.activation(dst(g), ps[:, :dst(g).shape[1]], ACT.Copy)

            mix_in_scalar(L, m, B)
            act.sem_inc(m.sem("scalar_stage_done"), 1)
            act.wait_ge(m.sem("vector_stage_done"), L.nth("vector_stage_done"))
            latent_scalar(L, m, B)
            act.sem_inc(m.sem("scalar_stage_done"), 1)
            act.wait_ge(m.sem("vector_stage_done"), L.nth("vector_stage_done"))
            attention_scalar(L, m, B.att)
            act.sem_inc(m.sem("scalar_stage_done"), 1)
            act.wait_ge(m.sem("vector_stage_done"), L.nth("vector_stage_done"))
            norm_scalar(L, m, chunk(B.o), chunk(B.mix), 4)
            act.sem_inc(m.sem("scalar_stage_done"), 1)
            act.wait_ge(m.sem("vector_stage_done"), L.nth("vector_stage_done"))
            conv_turn_scalar(L, m, B)
            act.sem_inc(m.sem("scalar_stage_done"), 1)
            act.wait_ge(m.sem("vector_stage_done"), L.nth("vector_stage_done"))
            filter_scalar(L, m, B)
            act.sem_inc(m.sem("scalar_stage_done"), 1)
            act.wait_ge(m.sem("vector_stage_done"), L.nth("vector_stage_done"))
            for order in range(2):
                act.sem_inc(m.sem("scalar_stage_done"), 1)
                act.wait_ge(m.sem("vector_stage_done"), L.nth("vector_stage_done"))
                filter_spectrum_scalar(L, m, B)
                act.sem_inc(m.sem("scalar_stage_done"), 1)
                act.wait_ge(m.sem("vector_stage_done"), L.nth("vector_stage_done"))
                read_banks(L, 8, never, None)
                act.sem_inc(m.sem("scalar_stage_done"), 1)
                act.wait_ge(m.sem("vector_stage_done"), L.nth("vector_stage_done"))
                if order == 0:
                    read_banks(L, 4, never, None)
                    act.sem_inc(m.sem("scalar_stage_done"), 1)
                    act.wait_ge(m.sem("vector_stage_done"), L.nth("vector_stage_done"))
                    read_banks(L, 4, always, copy(lambda g: B.z1f[:, g, :]))
                    act.sem_inc(m.sem("scalar_stage_done"), 1)
                    act.wait_ge(m.sem("vector_stage_done"), L.nth("vector_stage_done"))
            read_banks(L, 4, never, None)
            act.sem_inc(m.sem("scalar_stage_done"), 1)
            act.wait_ge(m.sem("vector_stage_done"), L.nth("vector_stage_done"))
            norm_scalar(L, m, chunk(B.z2f), lambda c: B.mix[:, 4 + c, :], 4)
            act.sem_inc(m.sem("scalar_stage_done"), 1)
            act.wait_ge(m.sem("vector_stage_done"), L.nth("vector_stage_done"))
            read_banks(L, 8, never, None)
            act.sem_inc(m.sem("scalar_stage_done"), 1)
            act.wait_ge(m.sem("vector_stage_done"), L.nth("vector_stage_done"))
            memory_scalar(L, m, B)
            act.sem_inc(m.sem("scalar_stage_done"), 1)
            act.wait_ge(m.sem("vector_stage_done"), L.nth("vector_stage_done"))
            attention_scalar(L, m, B.matt)
            act.sem_inc(m.sem("scalar_stage_done"), 1)
            act.wait_ge(m.sem("vector_stage_done"), L.nth("vector_stage_done"))
            read_banks(L, 8, never, None)
            act.sem_inc(m.sem("scalar_stage_done"), 1)
            act.wait_ge(m.sem("vector_stage_done"), L.nth("vector_stage_done"))
            swiglu_first_scalar(L, m, "moe")
            route_scalar(L, m, B)
            act.sem_inc(m.sem("scalar_stage_done"), 1)
            act.wait_ge(m.sem("vector_stage_done"), L.nth("vector_stage_done"))
            act.activation(m.cond[:, :, 0:2], m.vec("cond", 0, 16).rearrange("p (a b) -> p a b", b=2), ACT.Silu).then_inc(m.sem("cond"), 1)
            swiglu_scalar(L, m, "moe", GROUPS * EXPERTS, B.gate, [NX], B.weight)
            act.sem_inc(m.sem("scalar_stage_done"), 1)
            act.wait_ge(m.sem("vector_stage_done"), L.nth("vector_stage_done"))
            norm_scalar(L, m, chunk(m.x), chunk(B.h), KC)
            act.sem_inc(m.sem("scalar_stage_done"), 1)
            act.wait_ge(m.sem("vector_stage_done"), L.nth("vector_stage_done"))

            for i in range(2):
                modnorm_scalar(L, m, R)
                act.sem_inc(m.sem("scalar_stage_done"), 1)
                act.wait_ge(m.sem("vector_stage_done"), L.nth("vector_stage_done"))
                if i == 0:
                    qkv_scalar(L, m, R)
                    act.sem_inc(m.sem("scalar_stage_done"), 1)
                    act.wait_ge(m.sem("vector_stage_done"), L.nth("vector_stage_done"))
                    for att in (R.att, R.catt):
                        attention_scalar(L, m, att)
                        act.sem_inc(m.sem("scalar_stage_done"), 1)
                        act.wait_ge(m.sem("vector_stage_done"), L.nth("vector_stage_done"))
                    for s in range(4):
                        read_banks(L, 4, never, None)
                        if s < GUESTS["wo0"]:
                            mod_scalar(L, m, s == 0, s == GUESTS["wo0"] - 1)
                    act.sem_inc(m.sem("scalar_stage_done"), 1)
                    act.wait_ge(m.sem("vector_stage_done"), L.nth("vector_stage_done"))
                else:
                    act.sem_inc(m.sem("scalar_stage_done"), 1)
                    act.wait_ge(m.sem("vector_stage_done"), L.nth("vector_stage_done"))
                    for dst in (R.pk, R.pv):
                        read_banks(L, 16, always, copy(lambda g: chunk(dst, *BOTH[g % 2])(g // 2)))
                        act.sem_inc(m.sem("scalar_stage_done"), 1)
                        act.wait_ge(m.sem("vector_stage_done"), L.nth("vector_stage_done"))
                    for dst, f in ((R.tw, ACT.Tanh), (R.ta, ACT.Copy)):
                        read_banks(L, 2, always, lambda g, ps: act.activation(
                            dst[:, BOTH[g][0]:BOTH[g][0] + BOTH[g][1]], ps[:, :BOTH[g][1]], f))
                        act.sem_inc(m.sem("scalar_stage_done"), 1)
                        act.wait_ge(m.sem("vector_stage_done"), L.nth("vector_stage_done"))
                    read_banks(L, 1, always, lambda g, ps: act.activation(R.tg, ps, ACT.Sigmoid))
                    act.sem_inc(m.sem("scalar_stage_done"), 1)
                    act.wait_ge(m.sem("vector_stage_done"), L.nth("vector_stage_done"))
                    act.wait_ge(m.sem("spilled"), 32)
                    read_banks(L, 8, always, copy(lambda g: R.pr[:, g, :]))
                    act.sem_inc(m.sem("scalar_stage_done"), 1)
                    act.wait_ge(m.sem("vector_stage_done"), L.nth("vector_stage_done"))
                    recurrence_scalar(L, m, R)
                    act.sem_inc(m.sem("scalar_stage_done"), 1)
                    act.wait_ge(m.sem("vector_stage_done"), L.nth("vector_stage_done"))
                    read_banks(L, 8, never, None)
                    act.sem_inc(m.sem("scalar_stage_done"), 1)
                    act.wait_ge(m.sem("vector_stage_done"), L.nth("vector_stage_done"))
                swiglu_first_scalar(L, m, f"ffn{i}")
                modnorm_scalar(L, m, R, i == 0)
                act.sem_inc(m.sem("scalar_stage_done"), 1)
                act.wait_ge(m.sem("vector_stage_done"), L.nth("vector_stage_done"))
                swiglu_scalar(L, m, f"ffn{i}", FF // 256, R.gate, BOTH[:2 - i])
                act.sem_inc(m.sem("scalar_stage_done"), 1)
                act.wait_ge(m.sem("vector_stage_done"), L.nth("vector_stage_done"))
            norm_scalar(L, m, chunk(m.x), chunk(R.h, 0, T), KC)
            act.sem_inc(m.sem("scalar_stage_done"), 1)
            act.wait_ge(m.sem("vector_stage_done"), L.nth("vector_stage_done"))

        @block.vector
        def _(dve):
            L = Lane(m, dve, "vector")
            L.eng.wait_ge(m.sem("inputs_landed"), L.nth("inputs_landed", 48))
            L.eng.wait_ge(m.sem("x_landed"), 16)
            L.eng.wait_ge(m.sem("x_landed_too"), 16)
            dve.memset(m.cond[:, :, :], 0.0).then_inc(L.step, 1)
            dve.wait_ge(L.step, L.next_step())
            mix_in_vector(L, m, B)
            dve.sem_inc(m.sem("vector_stage_done"), 1)
            dve.wait_ge(m.sem("scalar_stage_done"), L.nth("scalar_stage_done"))
            latent_vector(L, m, B)
            dve.sem_inc(m.sem("vector_stage_done"), 1)
            dve.wait_ge(m.sem("scalar_stage_done"), L.nth("scalar_stage_done"))
            latent_attention_vector(L, m, B)
            dve.sem_inc(m.sem("vector_stage_done"), 1)
            dve.wait_ge(m.sem("scalar_stage_done"), L.nth("scalar_stage_done"))
            norm_vector(L, m, chunk(B.o), chunk(B.mix), 4, gains(m, "aout_g"))
            conv_vector(L, m, B)
            dve.sem_inc(m.sem("vector_stage_done"), 1)
            dve.wait_ge(m.sem("scalar_stage_done"), L.nth("scalar_stage_done"))
            read_banks(L, 8, never, None)
            dve.sem_inc(m.sem("vector_stage_done"), 1)
            dve.wait_ge(m.sem("scalar_stage_done"), L.nth("scalar_stage_done"))
            L.eng.sem_inc(m.sem("room_for_dft"), 1)
            L.nth("room_for_dft")
            filter_vector(L, m, B)
            dve.sem_inc(m.sem("vector_stage_done"), 1)
            dve.wait_ge(m.sem("scalar_stage_done"), L.nth("scalar_stage_done"))
            for order in range(2):
                parts_vector(L, m, B, order)
                dve.sem_inc(m.sem("vector_stage_done"), 1)
                dve.wait_ge(m.sem("scalar_stage_done"), L.nth("scalar_stage_done"))
                read_banks(L, 8, never, None)
                dve.sem_inc(m.sem("vector_stage_done"), 1)
                dve.wait_ge(m.sem("scalar_stage_done"), L.nth("scalar_stage_done"))
                product_vector(L, m, B)
                dve.sem_inc(m.sem("vector_stage_done"), 1)
                dve.wait_ge(m.sem("scalar_stage_done"), L.nth("scalar_stage_done"))
                if order == 0:
                    inverse0_vector(L, m, B)
                    dve.sem_inc(m.sem("vector_stage_done"), 1)
                    dve.wait_ge(m.sem("scalar_stage_done"), L.nth("scalar_stage_done"))
                    read_banks(L, 4, never, None)
                    dve.sem_inc(m.sem("vector_stage_done"), 1)
                    dve.wait_ge(m.sem("scalar_stage_done"), L.nth("scalar_stage_done"))
            inverse1_vector(L, m, B)
            dve.sem_inc(m.sem("vector_stage_done"), 1)
            dve.wait_ge(m.sem("scalar_stage_done"), L.nth("scalar_stage_done"))
            norm_vector(L, m, chunk(B.z2f), lambda c: B.mix[:, 4 + c, :], 4, gains(m, "hyout_g"))
            dve.sem_inc(m.sem("vector_stage_done"), 1)
            dve.wait_ge(m.sem("scalar_stage_done"), L.nth("scalar_stage_done"))
            read_banks(L, 8, always, add_to_x(L, m))
            dve.sem_inc(m.sem("vector_stage_done"), 1)
            dve.wait_ge(m.sem("scalar_stage_done"), L.nth("scalar_stage_done"))
            L.eng.sem_inc(m.sem("room_for_mem"), 1)
            L.nth("room_for_mem")
            memory_vector(L, m, B)
            dve.sem_inc(m.sem("vector_stage_done"), 1)
            dve.wait_ge(m.sem("scalar_stage_done"), L.nth("scalar_stage_done"))
            attention_vector(L, m, B.matt, lambda h, mt: B.mo[:, 2 * h + mt, :])
            dve.sem_inc(m.sem("vector_stage_done"), 1)
            dve.wait_ge(m.sem("scalar_stage_done"), L.nth("scalar_stage_done"))
            read_banks(L, 8, always, add_to_x(L, m))
            dve.sem_inc(m.sem("vector_stage_done"), 1)
            dve.wait_ge(m.sem("scalar_stage_done"), L.nth("scalar_stage_done"))
            route_vector(L, m, B)
            dve.sem_inc(m.sem("vector_stage_done"), 1)
            dve.wait_ge(m.sem("scalar_stage_done"), L.nth("scalar_stage_done"))
            add = add_to_x(L, m)
            split_h_vector(L, m, B, 0, T)
            swiglu_vector(L, m, "moe", GROUPS * EXPERTS, B, [NX], lambda c, g, ps: add(c, ps), B.weight)
            dve.sem_inc(m.sem("vector_stage_done"), 1)
            dve.wait_ge(m.sem("scalar_stage_done"), L.nth("scalar_stage_done"))
            norm_vector(L, m, chunk(m.x), chunk(m.x), KC, gains(m, "fin_g"))
            dve.sem_inc(m.sem("vector_stage_done"), 1)
            dve.wait_ge(m.sem("scalar_stage_done"), L.nth("scalar_stage_done"))

            for i in range(2):
                mod_gains_vector(L, m, i)
                modnorm_vector(L, m, R, i, 0)
                dve.sem_inc(m.sem("vector_stage_done"), 1)
                dve.wait_ge(m.sem("scalar_stage_done"), L.nth("scalar_stage_done"))
                if i == 0:
                    L.eng.sem_inc(m.sem("room_for_rope"), 1)
                    L.nth("room_for_rope")
                    qkv_vector(L, m, R)
                    dve.sem_inc(m.sem("vector_stage_done"), 1)
                    dve.wait_ge(m.sem("scalar_stage_done"), L.nth("scalar_stage_done"))
                    for ctx_side in (False, True):
                        gqa_vector(L, m, R, ctx_side)
                        dve.sem_inc(m.sem("vector_stage_done"), 1)
                        dve.wait_ge(m.sem("scalar_stage_done"), L.nth("scalar_stage_done"))
                    add2 = gated_add(L, m, i, 2)
                    for s in range(4):
                        read_banks(L, 4, always, lambda g, ps: add2(2 * s + g // 2, g % 2, ps))
                        if s < GUESTS["wo0"]:
                            mod_vector(L, m, s == 0, s == GUESTS["wo0"] - 1)
                    dve.sem_inc(m.sem("vector_stage_done"), 1)
                    dve.wait_ge(m.sem("scalar_stage_done"), L.nth("scalar_stage_done"))
                else:
                    shift_vector(L, m, R)
                    dve.sem_inc(m.sem("vector_stage_done"), 1)
                    dve.wait_ge(m.sem("scalar_stage_done"), L.nth("scalar_stage_done"))
                    for which, banks in ((2, 16), (3, 16), (1, 2), (4, 2), (5, 1), (0, 8)):
                        lerp_vector(L, m, R, which)
                        read_banks(L, banks, never, None)
                        dve.sem_inc(m.sem("vector_stage_done"), 1)
                        dve.wait_ge(m.sem("scalar_stage_done"), L.nth("scalar_stage_done"))
                        if which == 3:
                            L.eng.sem_inc(m.sem("kv_ready"), 1)
                            L.nth("kv_ready")
                    L.eng.sem_inc(m.sem("r_ready"), 1)
                    L.nth("r_ready")
                    L.eng.wait_ge(m.sem("wkv_tables"), L.nth("wkv_tables", 48))
                    recurrence_vector(L, m, R)
                    dve.sem_inc(m.sem("vector_stage_done"), 1)
                    dve.wait_ge(m.sem("scalar_stage_done"), L.nth("scalar_stage_done"))
                    read_banks(L, 8, always, add_to_x(L, m, mod_col(m, i, 2, 0)))
                    dve.sem_inc(m.sem("vector_stage_done"), 1)
                    dve.wait_ge(m.sem("scalar_stage_done"), L.nth("scalar_stage_done"))
                modnorm_vector(L, m, R, i, 1, i == 0)
                dve.sem_inc(m.sem("vector_stage_done"), 1)
                dve.wait_ge(m.sem("scalar_stage_done"), L.nth("scalar_stage_done"))
                swiglu_vector(L, m, f"ffn{i}", FF // 256, R, BOTH[:2 - i], gated_add(L, m, i, 5))
                dve.sem_inc(m.sem("vector_stage_done"), 1)
                dve.wait_ge(m.sem("scalar_stage_done"), L.nth("scalar_stage_done"))
            norm_vector(L, m, chunk(m.x), chunk(m.x), KC, gains(m, "fin2_g"))
            dve.sem_inc(m.sem("vector_stage_done"), 1)
            dve.wait_ge(m.sem("scalar_stage_done"), L.nth("scalar_stage_done"))
            L.eng.sem_inc(m.sem("result"), 1)
            L.nth("result")


def kernel(**inputs):
    import numpy as _np
    import concourse.bacc as _bacc
    from concourse.bass_utils import run_bass_kernel_spmd as _run

    a = {k: _np.asarray(v) for k, v in inputs.items()}
    arrays = {"wall": pack_slabs(a), "vecs": pack_vectors(a), "tabs": tables(), "x": feature_major(a["x"][0]),
              "ctx": feature_major(a["ctx_2"][0]), "mem": feature_major(a["mem"][0])}
    nc = _bacc.Bacc("TRN2", target_bir_lowering=False, num_devices=1)
    dram = {k: nc.dram_tensor(f"in_{k}", v.shape, F32, kind="ExternalInput").ap() for k, v in arrays.items()}
    dram["out"] = nc.dram_tensor("out_0", (P, KC, T), F32, kind="ExternalOutput").ap()
    dram["spill"] = nc.dram_tensor("spill", (P, KC, 2048), F32).ap()
    build(nc, dram)
    r = _run(nc, [{f"in_{k}": v for k, v in arrays.items()}], core_ids=[0])
    out = r.results[0]["out_0"]
    return _np.ascontiguousarray(out.transpose(2, 1, 0).reshape(1, T, D))
```
